# Optimizing a Trainium2 kernel written in Bass

```python
import math
import jax
import jax.numpy as jnp
from jax import lax
import numpy as np
import jax, jax.numpy as jnp

D_MODEL = 2048
BATCH = 1
SEQ = 256
DEPTH = 1

D_MIX = D_MODEL
D_POOL = D_MIX // 2
POOL_WINDOWS = (2, 4, 8, 16)
N_POOL_GROUPS = len(POOL_WINDOWS)
POOL_GROUP = D_POOL // N_POOL_GROUPS
D_ATTN = D_MIX - D_POOL
HEAD_DIM = 128
N_HEADS = D_ATTN // HEAD_DIM
IDX_HEADS = 16
IDX_DIM = 64
TOPK_MAX = 256
Q_BLOCK = 128
D_FF = 5632
CONV_WIDTH = 3
EPS = 1e-6

D_IN = D_POOL + 3 * D_ATTN + IDX_HEADS * IDX_DIM + IDX_DIM + IDX_HEADS


def rmsnorm(x, g):
    xf = x.astype(jnp.float32)
    y = xf * lax.rsqrt(jnp.mean(xf * xf, axis=-1, keepdims=True) + EPS)
    return (y * g.astype(jnp.float32)).astype(x.dtype)

def pool_mixer(u, pool_w, pool_scale):
    B, S, C = u.shape
    uf = u.astype(jnp.float32)
    csum = jnp.concatenate([jnp.zeros((B, 1, C), jnp.float32), jnp.cumsum(uf, axis=1)], axis=1)
    t = jnp.arange(S)
    outs = []
    for gi, w in enumerate(POOL_WINDOWS):
        lo = jnp.maximum(t + 1 - w, 0)
        cnt = (t + 1 - lo).astype(jnp.float32)[None, :, None]
        c_g = csum[:, :, gi * POOL_GROUP:(gi + 1) * POOL_GROUP]
        mean = (c_g[:, 1:] - c_g[:, lo]) / cnt
        outs.append(mean - uf[:, :, gi * POOL_GROUP:(gi + 1) * POOL_GROUP])
    d = jnp.stack(outs, axis=2).astype(u.dtype)
    y = jnp.einsum('bsgc,gcd->bsgd', d, pool_w).reshape(B, S, C)
    return y * pool_scale

def dsa_attention(q, k, v, q_idx, k_idx, w_idx):
    B, S, H, Dh = q.shape
    topk = min(TOPK_MAX, S // 4)
    n_blocks = S // Q_BLOCK
    key_pos = jnp.arange(S)
    scale = Dh ** -0.5
    neg = jnp.finfo(jnp.float32).min

    def one_block(blk):
        start = blk * Q_BLOCK
        qb = lax.dynamic_slice_in_dim(q, start, Q_BLOCK, axis=1)
        qib = lax.dynamic_slice_in_dim(q_idx, start, Q_BLOCK, axis=1)
        wb = lax.dynamic_slice_in_dim(w_idx, start, Q_BLOCK, axis=1)
        q_pos = start + jnp.arange(Q_BLOCK)
        rel = jax.nn.relu(jnp.einsum('bthd,bsd->bths', qib.astype(jnp.float32), k_idx.astype(jnp.float32)))
        iscore = jnp.einsum('bths,bth->bts', rel, wb.astype(jnp.float32))
        causal = key_pos[None, :] <= q_pos[:, None]
        iscore = jnp.where(causal[None], iscore, neg)
        _, sel = lax.top_k(iscore, topk)
        valid = sel <= q_pos[None, :, None]
        k_sel = jax.vmap(lambda kb, ib: kb[ib])(k, sel)
        v_sel = jax.vmap(lambda vb, ib: vb[ib])(v, sel)
        s = jnp.einsum('bthd,btjhd->bhtj', qb, k_sel).astype(jnp.float32) * scale
        s = jnp.where(valid[:, None], s, neg)
        p = jax.nn.softmax(s, axis=-1).astype(v.dtype)
        return jnp.einsum('bhtj,btjhd->bthd', p, v_sel)

    out = lax.map(one_block, jnp.arange(n_blocks, dtype=jnp.int32))
    return jnp.transpose(out, (1, 0, 2, 3, 4)).reshape(B, S, H * Dh)

def conv_ffn(h, w_up, conv_w, conv_b, w_down):
    B, S, _ = h.shape
    up = h @ w_up
    up_p = jnp.pad(up, ((0, 0), (CONV_WIDTH - 1, 0), (0, 0)))
    c = conv_b + sum(conv_w[j] * up_p[:, j:j + S] for j in range(CONV_WIDTH))
    gate, val = jnp.split(c, 2, axis=-1)
    return (jax.nn.silu(gate) * val) @ w_down

def first_inputs(seed: int = 0) -> dict:
    key = jax.random.key(seed)
    ks = jax.random.split(key, 14)
    f32 = jnp.float32
    nrm = lambda k, shape, s: jax.random.normal(k, shape, f32) * s
    return {
        "x": nrm(ks[0], (BATCH, SEQ, D_MODEL), 1.0),
        "attn_norm_g": 1.0 + nrm(ks[1], (D_MODEL,), 0.02),
        "w_in": nrm(ks[2], (D_MODEL, D_IN), D_MODEL ** -0.5),
        "pool_w": nrm(ks[3], (N_POOL_GROUPS, POOL_GROUP, POOL_GROUP), POOL_GROUP ** -0.5),
        "pool_scale": 1.0 + nrm(ks[4], (D_POOL,), 0.02),
        "q_norm_g": 1.0 + nrm(ks[5], (HEAD_DIM,), 0.02),
        "k_norm_g": 1.0 + nrm(ks[6], (HEAD_DIM,), 0.02),
        "w_out": nrm(ks[7], (D_MIX, D_MODEL), D_MIX ** -0.5),
        "ffn_norm_g": 1.0 + nrm(ks[8], (D_MODEL,), 0.02),
        "w_up": nrm(ks[9], (D_MODEL, 2 * D_FF), D_MODEL ** -0.5),
        "conv_w": nrm(ks[10], (CONV_WIDTH, 2 * D_FF), CONV_WIDTH ** -0.5),
        "conv_b": nrm(ks[11], (2 * D_FF,), 0.01),
        "w_down": nrm(ks[12], (D_FF, D_MODEL), D_FF ** -0.5),
    }

def first_block(x, attn_norm_g, w_in, pool_w, pool_scale, q_norm_g, k_norm_g, w_out,
              ffn_norm_g, w_up, conv_w, conv_b, w_down):
    B, S, _ = x.shape
    for _layer in range(DEPTH):
        h = rmsnorm(x, attn_norm_g)
        z = h @ w_in
        o = 0
        u_pool = z[..., o:o + D_POOL]; o += D_POOL
        q = z[..., o:o + D_ATTN].reshape(B, S, N_HEADS, HEAD_DIM); o += D_ATTN
        k = z[..., o:o + D_ATTN].reshape(B, S, N_HEADS, HEAD_DIM); o += D_ATTN
        v = z[..., o:o + D_ATTN].reshape(B, S, N_HEADS, HEAD_DIM); o += D_ATTN
        q_idx = z[..., o:o + IDX_HEADS * IDX_DIM].reshape(B, S, IDX_HEADS, IDX_DIM); o += IDX_HEADS * IDX_DIM
        k_idx = z[..., o:o + IDX_DIM]; o += IDX_DIM
        w_idx = z[..., o:o + IDX_HEADS] * (IDX_HEADS ** -0.5) * (IDX_DIM ** -0.5)
        q = rmsnorm(q, q_norm_g)
        k = rmsnorm(k, k_norm_g)
        y_pool = pool_mixer(u_pool, pool_w, pool_scale)
        y_attn = dsa_attention(q, k, v, q_idx, k_idx, w_idx)
        x = x + jnp.concatenate([y_pool, y_attn], axis=-1) @ w_out
        x = x + conv_ffn(rmsnorm(x, ffn_norm_g), w_up, conv_w, conv_b, w_down)
    return x


D_MIX_2 = D_MODEL
CONV_W = D_MIX_2 // 2
CONV_GROUPS = 16
GLA_HEADS = 4
GLA_DV = D_MIX_2 - CONV_W
HEAD_V = GLA_DV // GLA_HEADS
GLA_DK = GLA_DV // 2
HEAD_K = GLA_DK // GLA_HEADS
GATE_RANK = 16
GATE_TAU = 16
CHUNK = 64
CONV_K = 3
D_IN_2 = 3 * CONV_W + 2 * GLA_DK + 2 * GLA_DV + GATE_RANK


def rmsnorm_2(x, w):
    x32 = x.astype(jnp.float32)
    y = x32 * lax.rsqrt(jnp.mean(x32 * x32, axis=-1, keepdims=True) + EPS)
    return (y * w.astype(jnp.float32)).astype(x.dtype)

def causal_dwconv3(u, w):
    s = u.shape[1]
    up = jnp.pad(u, ((0, 0), (CONV_K - 1, 0), (0, 0)))
    return up[:, :s] * w[0] + up[:, 1:s + 1] * w[1] + up[:, 2:] * w[2]

def gla_chunked(q, k, v, log_a):
    bsz, s, h, dk = q.shape
    dv = v.shape[-1]
    nc = s // CHUNK

    def to_chunks(t):
        return t.reshape(bsz, nc, CHUNK, h, t.shape[-1]).transpose(1, 0, 3, 2, 4).astype(jnp.float32)

    mask = jnp.tril(jnp.ones((CHUNK, CHUNK), dtype=bool))[None, None, :, :, None]

    def step(state, inp):
        qc, kc, vc, gc = inp
        b = jnp.cumsum(gc, axis=2)
        diff = b[:, :, :, None, :] - b[:, :, None, :, :]
        decay = jnp.exp(jnp.where(mask, diff, -jnp.inf))
        scores = jnp.einsum('bhid,bhjd,bhijd->bhij', qc, kc, decay)
        o = jnp.einsum('bhij,bhje->bhie', scores, vc) + jnp.einsum('bhid,bhde->bhie', qc * jnp.exp(b), state)
        b_last = b[:, :, -1:, :]
        state = jnp.exp(b_last[:, :, 0, :])[..., None] * state + jnp.einsum(
            'bhjd,bhje->bhde', kc * jnp.exp(b_last - b), vc)
        return state, o

    state0 = jnp.zeros((bsz, h, dk, dv), jnp.float32)
    _, o = lax.scan(step, state0, (to_chunks(q), to_chunks(k), to_chunks(v), to_chunks(log_a)))
    return o.transpose(1, 0, 3, 2, 4).reshape(bsz, s, h, dv)

def hybrid_mixer(h, w_in, conv_w, gate_w2, gate_b, gla_norm_w, w_out):
    bsz, s, _ = h.shape
    proj = h @ w_in
    splits = np.cumsum([CONV_W, CONV_W, CONV_W, GLA_DK, GLA_DK, GLA_DV, GLA_DV])
    cb, cc, cx, q, k, v, r, a_lr = jnp.split(proj, splits, axis=-1)
    y_conv = cb * causal_dwconv3(cc * cx, conv_w)
    log_a = jax.nn.log_sigmoid((a_lr @ gate_w2 + gate_b).astype(jnp.float32)) / GATE_TAU
    q = q.reshape(bsz, s, GLA_HEADS, HEAD_K) * (HEAD_K ** -0.5)
    k = k.reshape(bsz, s, GLA_HEADS, HEAD_K)
    v = v.reshape(bsz, s, GLA_HEADS, HEAD_V)
    log_a = log_a.reshape(bsz, s, GLA_HEADS, HEAD_K)
    o = gla_chunked(q, k, v, log_a).astype(h.dtype)
    o = rmsnorm_2(o, gla_norm_w) * jax.nn.silu(r.reshape(bsz, s, GLA_HEADS, HEAD_V))
    y_gla = o.reshape(bsz, s, GLA_DV)
    return jnp.concatenate([y_conv, y_gla], axis=-1) @ w_out

def conv_ffn_2(h, w_up, ffn_conv_w, w_down):
    u = causal_dwconv3(h @ w_up, ffn_conv_w)
    g, val = jnp.split(u, 2, axis=-1)
    return (jax.nn.silu(g) * val) @ w_down

def second_inputs(seed: int = 0) -> dict:
    key = jax.random.key(seed)
    ks = jax.random.split(key, 20)
    n = jax.random.normal
    f = jnp.float32
    L = DEPTH
    return {
        "x": n(ks[0], (BATCH, SEQ, D_MODEL), f),
        "c": n(ks[1], (BATCH, D_MODEL), f),
        "w_mod": n(ks[2], (L, D_MODEL, 6 * D_MODEL), f) * (0.5 * D_MODEL ** -0.5),
        "b_mod": 0.01 * n(ks[3], (L, 6 * D_MODEL), f),
        "mix_pre_w": 1.0 + 0.05 * n(ks[4], (L, D_MODEL), f),
        "mix_post_w": 1.0 + 0.05 * n(ks[5], (L, D_MODEL), f),
        "w_in": n(ks[6], (L, D_MODEL, D_IN_2), f) * D_MODEL ** -0.5,
        "conv_w": n(ks[7], (L, CONV_K, CONV_W), f) * CONV_K ** -0.5,
        "gate_w2": n(ks[8], (L, GATE_RANK, GLA_DK), f) * GATE_RANK ** -0.5,
        "gate_b": 0.01 * n(ks[9], (L, GLA_DK), f),
        "gla_norm_w": 1.0 + 0.05 * n(ks[10], (L, HEAD_V), f),
        "w_out": n(ks[11], (L, D_MIX_2, D_MODEL), f) * D_MIX_2 ** -0.5,
        "ffn_pre_w": 1.0 + 0.05 * n(ks[12], (L, D_MODEL), f),
        "ffn_post_w": 1.0 + 0.05 * n(ks[13], (L, D_MODEL), f),
        "w_up": n(ks[14], (L, D_MODEL, 2 * D_FF), f) * D_MODEL ** -0.5,
        "ffn_conv_w": n(ks[15], (L, CONV_K, 2 * D_FF), f) * CONV_K ** -0.5,
        "w_down": n(ks[16], (L, D_FF, D_MODEL), f) * D_FF ** -0.5,
    }

def second_block(x, c, w_mod, b_mod, mix_pre_w, mix_post_w, w_in, conv_w, gate_w2, gate_b, gla_norm_w,
              w_out, ffn_pre_w, ffn_post_w, w_up, ffn_conv_w, w_down):
    c_act = jax.nn.silu(c)
    for l in range(DEPTH):
        mod = (c_act @ w_mod[l] + b_mod[l])[:, None, :]
        sh_m, sc_m, g_m, sh_f, sc_f, g_f = jnp.split(mod, 6, axis=-1)
        h = rmsnorm_2(x, mix_pre_w[l]) * (1 + sc_m) + sh_m
        y = hybrid_mixer(h, w_in[l], conv_w[l], gate_w2[l], gate_b[l], gla_norm_w[l], w_out[l])
        x = x + g_m * rmsnorm_2(y, mix_post_w[l])
        h = rmsnorm_2(x, ffn_pre_w[l]) * (1 + sc_f) + sh_f
        y = conv_ffn_2(h, w_up[l], ffn_conv_w[l], w_down[l])
        x = x + g_f * rmsnorm_2(y, ffn_post_w[l])
    return x


def setup_inputs(seed=0):
    out = dict(first_inputs(seed))
    for name, value in second_inputs(seed + 1).items():
        if name != "x":
            out[name + "_2"] = value
    return out


def reference(
    x, attn_norm_g, w_in, pool_w, pool_scale, q_norm_g, k_norm_g, w_out, ffn_norm_g, w_up,
    conv_w, conv_b, w_down, c_2, w_mod_2, b_mod_2, mix_pre_w_2, mix_post_w_2, w_in_2, conv_w_2,
    gate_w2_2, gate_b_2, gla_norm_w_2, w_out_2, ffn_pre_w_2, ffn_post_w_2, w_up_2, ffn_conv_w_2,
    w_down_2,
):
    x = first_block(
        x, attn_norm_g, w_in, pool_w, pool_scale, q_norm_g, k_norm_g, w_out, ffn_norm_g, w_up,
        conv_w, conv_b, w_down,
    )
    return second_block(
        x, c_2, w_mod_2, b_mod_2, mix_pre_w_2, mix_post_w_2, w_in_2, conv_w_2, gate_w2_2,
        gate_b_2, gla_norm_w_2, w_out_2, ffn_pre_w_2, ffn_post_w_2, w_up_2, ffn_conv_w_2,
        w_down_2,
    )


_drawn_inputs = setup_inputs


def setup_inputs(seed=0):
    import zlib

    import numpy as np

    out = dict(_drawn_inputs(seed))
    spreads = {}
    factors = {'pool_scale': 4.679,
     'q_norm_g': 8.0,
     'k_norm_g': 8.0,
     'ffn_norm_g': 4.056,
     'conv_b': 8.0,
     'b_mod_2': 4.57,
     'mix_pre_w_2': 13.27,
     'mix_post_w_2': 40.816,
     'gate_w2_2': 2.964,
     'gate_b_2': 200.0,
     'gla_norm_w_2': 200.0,
     'ffn_pre_w_2': 20.405,
     'ffn_post_w_2': 42.136}
    for name, (base, spread) in spreads.items():
        noise = np.random.default_rng([zlib.crc32(name.encode()), seed]).standard_normal(out[name].shape)
        drawn = base * np.exp(spread * noise) if base else spread * noise
        out[name] = jnp.asarray(drawn.astype(out[name].dtype))
    for name, factor in factors.items():
        out[name] = (out[name] * factor).astype(out[name].dtype)
    return out
```

```python
from contextlib import ExitStack

import numpy as np

import concourse.bass as bass
from concourse import mybir

F32 = mybir.dt.float32
F32R = mybir.dt.float32r
ALU = mybir.AluOpType
ACT = mybir.ActivationFunctionType
AX_X = mybir.AxisListType.X

P = 128
D = 2048
S = 256
TT = S // P
KT = D // P
F = 5632
FT = F // P
EPS = 1e-6
NEG = float(np.finfo(np.float32).min)
HEADS = 8
HD = 128
IDX_HEADS = 16
IDX_DIM = 64
TOPK = S // 4
WINDOWS = (2, 4, 8, 16)
GLA_HEADS = 4
GLA_DV = 256
CHUNK = 64
NCHUNK = S // CHUNK
GATE_RANK = 16
GATE_TAU = 16
LEVELS = (32, 16, 8, 4, 2, 1)

BLOCK = 512
KC = 4
CHUNK_EL = KC * BLOCK
HALF = CHUNK_EL // 2
RAW_SLOTS = 4
HL_SLOTS = 4
BLOCK_CHUNKS = KT // KC
UNIT_OPS = KT

IDX_REST = IDX_DIM + IDX_HEADS
IN1_TOP = 4096
IN1_REST = 5120
IN2_REST = 6144

C_ID, C_ONE, C_LVL, C_RST, C_TRI, C_INV = 0, 128, 256, 256 + 896, 256 + 896 + 256, 256 + 896 + 384
C_N = C_INV + 64

A_ATTN, A_FFN, A_PSC, A_MPRE, A_FPRE, A_MPOST, A_GB, A_QG, A_KG, A_GLA, A_CW = 0, 16, 32, 40, 56, 72, 88, 92, 93, 94, 96
A_ROWS = 120
B_MOD, B_C, B_FPOST = 0, 96, 112
CONV_ROWS = 2 * FT


def constants():
    c = np.zeros((P, C_N), np.float32)
    c[:, C_ID:C_ID + P] = np.eye(P)
    c[:, C_ONE:C_ONE + P] = 1.0
    j, i = np.arange(P)[:, None], np.arange(P)[None, :]
    for n, s in enumerate(LEVELS):
        c[:, C_LVL + n * P:C_LVL + (n + 1) * P] = (j // (2 * s) == i // (2 * s)) & (j % (2 * s) < s) & (i % (2 * s) >= s)
    c[:, C_LVL + 6 * P:C_LVL + 7 * P] = np.eye(P)
    c[:, C_RST:C_RST + S] = (np.arange(S) % CHUNK != 0)
    c[:, C_TRI:C_TRI + P] = np.where(i <= j, 0.0, NEG)
    for n, w in enumerate(WINDOWS):
        c[:, C_INV + 16 * n:C_INV + 16 * n + 16] = 1.0 / np.minimum(np.arange(16) + 1, w)
    return c


class Phase:

    def __init__(self, order, name, gemms, mods, b0):
        self.name, self.n0 = name, len(order)
        self.m0 = sum(1 for k, _ in order if k == "g")
        self.k0 = len(order) - self.m0
        self.b0, self.mod = b0, mods
        self.gemms = gemms


def plan():
    order, phases, blocks = [], {}, 0
    m = k = 0
    for name, pairs, mods, single in (
            ("rest1", 0, False, 1), ("in1", 5, True, 0), ("out1", 2, True, 0), ("up1", 11, True, 0),
            ("down1", 0, False, FT), ("rest2", 0, False, 1), ("in2", 6, True, 0), ("out2", 2, False, 0),
            ("up2", 11, False, 0), ("down2", 0, False, FT)):
        phases[name] = Phase(order, name, single, mods, blocks)
        seq = "g" * single + ("gggmgmgmgmgg" if mods else "gggggggg") * pairs
        for c in seq:
            if c == "g":
                order.append(("g", m))
                m += 1
            else:
                order.append(("m", k))
                k += 1
        blocks += 2 * pairs
    return order, phases


ORDER, PH = plan()
RAW_OF = {m: n for n, (kind, m) in enumerate(ORDER) if kind == "g"}
RAW_OF_MOD = {k: n for n, (kind, k) in enumerate(ORDER) if kind == "m"}


def raw_stride(ph):
    return 16 * (12 if ph.mod else 8) // RAW_SLOTS


def pair_items(ph, i0):
    per = 12 if ph.mod else 8
    return [(n, *ORDER[n]) for n in range(ph.n0 + per * i0, ph.n0 + per * (i0 + 1))]


def two_blocks(nc, consts, x_in, out, w):
    with ExitStack() as ctx:
        def sb(name, shape, dt=F32):
            return ctx.enter_context(nc.sbuf_tensor(name, shape, dt))

        sems = {}

        def sem(name):
            if name not in sems:
                sems[name] = ctx.enter_context(nc.semaphore(name))
            return sems[name]

        raw = sb("raw", [P, RAW_SLOTS, CHUNK_EL])
        w_hi = sb("w_hi", [P, HL_SLOTS, HALF], F32R)
        w_lo = sb("w_lo", [P, HL_SLOTS, HALF], F32R)
        x = sb("x", [P, TT, D])
        a_hi = sb("a_hi", [P, KT, S], F32R)
        a_lo = sb("a_lo", [P, KT, S], F32R)
        con = sb("con", [P, C_N])
        col = sb("col", [P, 9, P])
        modc = sb("modc", [P, 96])
        mod_acc = sb("mod_acc", [P, BLOCK])
        small = sb("small", [P, 320])
        REGION = 24576
        region = sb("region", [P, REGION])
        ps = ctx.enter_context(nc.psum_tensor("ps", [P, 4096], F32))

        def reg(at, n):
            return region[:, at:at + n]

        def main(g):
            return ps[:, 1024 * g:1024 * (g + 1)]

        SIDE = 2048

        def side(b, n=512):
            return ps[:, SIDE + 512 * b:SIDE + 512 * b + n]

        ident = con[:, C_ID:C_ID + P]
        ones = con[:, C_ONE:C_ONE + P]
        tri = con[:, C_TRI:C_TRI + P]

        def colA(r, n=1):
            return col[:, 0, r:r + n]

        def colB(r, n=1):
            return col[:, 1, r:r + n]

        def sm(at, n=1):
            return small[:, at:at + n]
        SS, MS, SD, RSTD = 0, 8, 16, 24
        C_ACT, SCALE_M, SCALE_F = 32, 48, 64
        QK_SS, QK_SD = 80, 112
        MX, NMX, RSUM, RINV = 144, 152, 160, 168
        E_LAST = 176
        O_SS, O_SD = 192, 200
        P_SS, P_SD, P_RSTD = 264, 268, 272
        GP = 216
        WIDX = 232

        hn = reg(0, 4096).rearrange("p (t d) -> p t d", t=TT)
        xt = reg(4096, 4096).rearrange("p (k s) -> p k s", k=KT)
        stage = reg(8192, 9 * P).rearrange("p (n d) -> p n d", n=9)
        z = reg(0, 12288).rearrange("p (b n) -> p b n", b=12)

        def zw(b):
            return region[:, 1024 * b:1024 * b + 2048].rearrange("p (f s) -> p f s", f=8)

        pool_w = reg(12288, 2048).rearrange("p (g c d) -> p g c d", g=4, c=2)
        kT = reg(14336, 2048).rearrange("p (h s) -> p h s", h=HEADS)
        qT = reg(16384, 2048).rearrange("p (h s) -> p h s", h=HEADS)
        kidx2 = reg(18432, 256).rearrange("p (t c d) -> p t c d", t=TT, c=2)
        kidxT = reg(18688, 256)
        relu_buf = reg(18976, 2048).rearrange("p (b h s) -> p b h s", b=2, h=4)
        sc_buf = reg(18976, 2048).rearrange("p (h s) -> p h s", h=HEADS)
        iscore = reg(21024, 512).rearrange("p (t s) -> p t s", t=TT)
        work = reg(21536, 512).rearrange("p (t s) -> p t s", t=TT)
        top8 = reg(22048, 128).rearrange("p (n e) -> p n e", e=8)
        notsel = reg(22176, 512).rearrange("p (t s) -> p t s", t=TT)
        win = [reg(22688 + 512 * n, 512).rearrange("p (f s) -> p f s", f=2) for n in range(2)]
        pT = reg(0, 2048)
        dT = zw(4)
        yT_attn = zw(6)
        yT_pool = zw(8)
        A1, A2, A3, A4, A5, A6 = (12288 + 1024 * n for n in range(6))

        def head_tok(at):
            return reg(at, 1024).rearrange("p (h s) -> p h s", h=GLA_HEADS)
        q_ex = reg(18432, 1536).rearrange("p (h c s) -> p h c s", h=GLA_HEADS, c=3)
        states = reg(19968, 3072).rearrange("p (c h e) -> p c h e", c=3, h=GLA_HEADS)
        a_lr = reg(19968, 32).rearrange("p (t r) -> p t r", t=TT)
        a_lrT = region[0:GATE_RANK, 20224:20224 + S]
        gate_w2 = region[0:GATE_RANK, 23040:23040 + 512]
        o_gla = reg(A2, 2048).rearrange("p (t h e) -> p t h e", t=TT, h=GLA_HEADS)
        yT_gla = zw(0)
        yT_conv = zw(6)
        g = reg(0, FT * S).rearrange("p (f s) -> p f s", f=FT)
        c_gate = reg(11264, 1024).rearrange("p (f s) -> p f s", f=4)
        c_val = reg(12288, 1024).rearrange("p (f s) -> p f s", f=4)
        y = reg(12288, 4096).rearrange("p (t d) -> p t d", t=TT)
        diag = reg(16384, 2048).rearrange("p (k f) -> p k f", k=KT)
        g_row = reg(22528, 2048)

        raw_full = [sem(f"raw_full{s}") for s in range(RAW_SLOTS)]
        hi_ready = sem("hi_ready")
        lo_ready = sem("lo_ready")
        w_used = sem("w_used")
        mod_step = sem("mod_step")
        mod_red = sem("mod_red")
        epi_done = sem("epi_done")
        act_hi = sem("act_hi")
        act_ready = sem("act_ready")

        RUNS = {
            "in1": [(0, 1, "W"), (1, 4, "T"), (4, 5, "W")],
            "out1": [(0, 1, "T"), (1, 2, "T")],
            "up1": [(0, 1, "W"), (1, 11, "W")],
            "in2": [(0, 1, "W"), (1, 3, "T"), (3, 6, "W")],
            "out2": [(0, 1, "T"), (1, 2, "T")],
            "up2": [(0, 1, "W"), (1, 11, "W")],
        }
        FILL = {"in1": 0, "out1": 1, "up1": 2, "in2": 3, "out2": 4, "up2": 5}

        def run_pairs(eng, name, body):
            for a, b, layout in RUNS[name]:
                if b - a == 1:
                    body(a, a, 0, layout)
                else:
                    with eng.Fori(a, b) as i:
                        body(a, i, i - a, layout)

        def block_end(ph, i0, blk):
            return 2 * (ph.m0 + 8 * i0 + 4 * (blk + 1))

        def phase_end(name):
            return block_end(PH[name], RUNS[name][-1][1] - 1, 1)

        def down_end(name):
            return 2 * (PH[name].m0 + FT)

        block = ctx.enter_context(nc.Block())

        @block.sync
        def _(sp):
            def slot_free(n, r=0, stride=16):
                if n < RAW_SLOTS:
                    return
                kind, at = ORDER[n - RAW_SLOTS]
                if kind == "g":
                    sp.wait_ge(lo_ready, 2 * (at + 1) + r * stride)
                else:
                    sp.wait_ge(mod_step, 4 * (at + 1) + r * stride)

            def settled(value):
                return value if type(value) is int else sp.snap(value)

            def rest(name, wt, c0, cols):
                n = PH[name].n0
                slot_free(n)
                with nc.allow_non_contiguous_dma(reason="the last few columns of w_in"):
                    sp.dma_start(raw[:, n % RAW_SLOTS, 0:KT * cols].rearrange("p (k n) -> p k n", k=KT),
                                 wt[:, c0:c0 + cols].rearrange("(k p) n -> p k n", p=P)).then_inc(raw_full[n % RAW_SLOTS], 16)

            def pairs(name, wt, column, step):
                ph = PH[name]

                def body(i0, i, r, layout):
                    for n, kind, at in pair_items(ph, i0):
                        if kind == "g":
                            blk, c = divmod((at - ph.m0) % 8, 4)
                            src = wt[c * KC * P:(c + 1) * KC * P, bass.ds(settled(column(i0, blk) + step * r), BLOCK)]
                        else:
                            c = at % 4
                            src = w["w_mod_2"][c * KC * P:(c + 1) * KC * P, bass.ds(settled(at // 4 * BLOCK + r * BLOCK), BLOCK)]
                        slot_free(n, r)
                        sp.dma_start(raw[:, n % RAW_SLOTS, :].rearrange("p (k n) -> p k n", k=KC),
                                     src.rearrange("(k p) n -> p k n", p=P)).then_inc(raw_full[n % RAW_SLOTS], 16)

                run_pairs(sp, name, body)

            def down(name, wt):
                ph = PH[name]

                def load(j, kt, r):
                    n = ph.n0 + j
                    src = wt[bass.ds(settled(kt * P), P), :]
                    slot_free(n, r, 8)
                    sp.dma_start(raw[:, n % RAW_SLOTS, :], src).then_inc(raw_full[n % RAW_SLOTS], 16)

                for j in range(4):
                    load(j, j, 0)
                with sp.Fori(1, FT // 4) as i:
                    for j in range(4):
                        load(4 + j, i * 4 + j, i - 1)

            sp.dma_start(x[:], x_in.rearrange("(t p) d -> p t d", p=P)).then_inc(sem("x_loaded"), 16)
            rest("rest1", w["w_in"], IN1_REST, IDX_REST)
            pairs("in1", w["w_in"], lambda i, blk: IN1_TOP - 1024 * i + BLOCK * blk, -1024)
            pairs("out1", w["w_out"], lambda i, blk: 1024 * i + BLOCK * blk, 1024)
            pairs("up1", w["w_up"], lambda i, blk: BLOCK * i + F * blk, BLOCK)
            down("down1", w["w_down"])
            rest("rest2", w["w_in_2"], IN2_REST, GATE_RANK)

            starts = {0: 3072, 1: 4096, 2: 5120, 3: 0, 4: 1024, 5: 2048}
            pairs("in2", w["w_in_2"], lambda i, blk: starts[i] + BLOCK * blk, 1024)
            pairs("out2", w["w_out_2"], lambda i, blk: 1024 * i + BLOCK * blk, 1024)
            pairs("up2", w["w_up_2"], lambda i, blk: BLOCK * i + F * blk, BLOCK)
            down("down2", w["w_down_2"])
            for t in range(TT):
                sp.wait_ge(sem("x_new"), 5 + t)
                sp.dma_start(out[t * P:(t + 1) * P, :], x[:, t, :]).then_inc(sem("stored"), 16)
            sp.wait_ge(sem("stored"), 16 * TT)

        @block.scalar
        def _(act):
            seq = [0]

            def link(ins):
                seq[0] += 1
                ins.then_inc(sem("act_step"), 1)
                act.wait_ge(sem("act_step"), seq[0])

            def round_half(m, half, r=0, stride=16, raw_add=0, n_el=HALF):
                n, hh = RAW_OF[m], 2 * m + half
                if half == 0:
                    act.wait_ge(raw_full[n % RAW_SLOTS], 16 * (n // RAW_SLOTS + 1) + r * raw_add)
                if hh >= HL_SLOTS:
                    act.wait_ge(w_used, hh - HL_SLOTS + 1 + r * stride)
                nc.scalar.activation(w_hi[:, hh % HL_SLOTS, 0:n_el], raw[:, n % RAW_SLOTS, half * n_el:(half + 1) * n_el],
                                     ACT.Copy).then_inc(hi_ready, 1)

            def rest_rounds(name, cols):
                for half in range(2):
                    round_half(PH[name].m0, half, n_el=KT * cols // 2)

            def lead(name, chunks):
                for c in range(chunks):
                    for half in range(2):
                        round_half(PH[name].m0 + c, half)

            def pairs(name, epi, before=None, done=2):
                ph = PH[name]

                def body(i0, i, r, layout):
                    for c in range(8):
                        if i0 > 0 or c >= done:
                            for half in range(2):
                                round_half(ph.m0 + 8 * i0 + c, half, r, 16, raw_stride(ph))
                        if c == 1:
                            if i0 > 0:
                                epi(ph, 1, i0 - 1, i - 1, r)
                            elif before:
                                before()
                        if c == 5:
                            epi(ph, 0, i0, i, r)

                run_pairs(act, name, body)

            def last_epi(name, epi):
                i = RUNS[name][-1][1] - 1
                epi(PH[name], 1, i, i, 0)

            def norm(p, f):
                if p == 0:
                    act.wait_ge(sem("x_loaded"), 16)
                elif p == 1:
                    act.wait_ge(epi_done, PH["out1"].b0 + 4)
                else:
                    act.wait_ge(sem("x_new"), 2 * (p - 1))
                for t in range(TT):
                    nc.scalar.activation(xt.rearrange("p k s -> p (k s)")[:, t * D:(t + 1) * D], x[:, t, :], ACT.Square,
                                         accum_out=sm(SS + 2 * p + t)).then_inc(sem("sq_done"), 1)
                act.wait_ge(sem("ms_ready"), p + 1)
                nc.scalar.activation(sm(SD + 2 * p, 2), sm(MS + 2 * p, 2), ACT.Sqrt).then_inc(sem("sd_ready"), 1)
                act.wait_ge(sem("rstd_ready"), p + 1)
                nc.scalar.activation(hn[:, 1, :], x[:, 1, :], ACT.Copy, scale=sm(RSTD + 2 * p + 1)).then_inc(sem("hn_act"), 1)
                for k in range(KT // 2):
                    act.wait_ge(sem("xt_ready"), KT * p + 2 * k + 2)
                    nc.scalar.activation(a_hi[:, 2 * k:2 * k + 2, :], xt[:, 2 * k:2 * k + 2, :], ACT.Copy).then_inc(act_hi, 1)

            def split_mixed(first, second, waits):
                for k, src in [(k, first[:, 2 * k:2 * k + 2, :]) for k in range(4)] + [(k + 4, second[:, 2 * k:2 * k + 2, :]) for k in range(4)]:
                    if k in waits:
                        act.wait_ge(*waits[k])
                    nc.scalar.activation(a_hi[:, 2 * k:2 * k + 2, :], src, ACT.Copy).then_inc(act_hi, 1)

            def epi_z(ph, blk, i0, i, r):
                act.wait_ge(w_used, block_end(ph, i0, blk) + 16 * r)
                nc.scalar.activation(z[:, bass.ds(2 * i + blk, 1), :].rearrange("p b n -> p (b n)"), main(blk), ACT.Copy).then_inc(epi_done, 1)

            def epi_none(ph, blk, i0, i, r):
                pass

            def epi_conv(layer, q):
                def epi(ph, blk, i0, i, r):
                    dst = (c_gate, c_val)[blk]
                    act.wait_ge(w_used, block_end(ph, i0, blk) + 16 * r)
                    if q + i0 > 0 or i0 > 0:
                        act.wait_ge(sem("g_done"), q * 11 + i0 + r)
                    last = 2 if layer == 1 else 6
                    for f in range(4):
                        tap = col[:, last, bass.ds(4 * i + f + FT * blk, 1)]
                        bias = col[:, 3, bass.ds(4 * i + f + FT * blk, 1)] if layer == 1 else 0.0
                        nc.scalar.activation(dst[:, f, :], main(blk)[:, S * f:S * (f + 1)], ACT.Identity, bias=bias,
                                             scale=tap).then_inc(sem("conv_first"), 1)
                    if blk == 0:
                        act.wait_ge(epi_done, ph.b0 + 2 * i0 + 1 + 2 * r)
                        nc.scalar.activation(c_gate, c_gate, ACT.Silu).then_inc(sem("silu_done"), 1)
                return epi

            def down(name, q, epi_prev):
                ph = PH[name]

                def split_g(j, kt, r):
                    nc.scalar.activation(a_hi[:, j % 4, :], g[:, bass.ds(kt, 1), :].rearrange("p f s -> p (f s)"),
                                         ACT.Copy).then_inc(sem("g_hi"), 1)

                epi_prev()
                act.wait_ge(sem("g_done"), 11 * (q + 1))
                for j in range(4):
                    split_g(j, j, 0)
                    if j >= 2:
                        for half in range(2):
                            round_half(ph.m0 + j, half)
                with act.Fori(1, FT // 4) as i:
                    for j in range(4):
                        act.wait_ge(w_used, 2 * (ph.m0 + j + 1) + 8 * (i - 1))
                        split_g(j, i * 4 + j, i - 1)
                        for half in range(2):
                            round_half(ph.m0 + 4 + j, half, i - 1, 8, 16)

            loads = [(con[:], consts)]
            for name, r in (("attn_norm_g", A_ATTN), ("ffn_norm_g", A_FFN), ("pool_scale", A_PSC), ("mix_pre_w_2", A_MPRE),
                            ("ffn_pre_w_2", A_FPRE), ("mix_post_w_2", A_MPOST), ("gate_b_2", A_GB), ("q_norm_g", A_QG),
                            ("k_norm_g", A_KG), ("gla_norm_w_2", A_GLA)):
                v = w[name].rearrange("(r p) -> r p", p=P)
                loads.append((stage[r:r + v.shape[0], 0, :], v))
            loads.append((stage[A_CW:A_CW + 24, 0, :], w["conv_w_2"].rearrange("j (r p) -> (j r) p", p=P)))
            for name, r in (("b_mod_2", B_MOD), ("c_2", B_C), ("ffn_post_w_2", B_FPOST)):
                v = w[name].rearrange("(r p) -> r p", p=P)
                loads.append((stage[r:r + v.shape[0], 1, :], v))
            for j in range(3):
                loads.append((stage[0:CONV_ROWS, (4, 5, 2)[j], :],
                              w["conv_w"][j].rearrange("(r p) -> r p", p=P)))
            loads.append((stage[0:CONV_ROWS, 3, :], w["conv_b"].rearrange("(r p) -> r p", p=P)))
            for j in range(3):
                loads.append((stage[0:CONV_ROWS, (7, 8, 6)[j], :], w["ffn_conv_w_2"][j].rearrange("(r p) -> r p", p=P)))
            loads.append((pool_w, w["pool_w"].rearrange("g (c p) d -> p g c d", p=P)))
            for dst, src in loads:
                act.dma_start(dst, src).then_inc(sem("params_loaded"), 16)

            act.wait_ge(sem("cols_turned"), 1)
            nc.scalar.activation(col[:, 0, 0:A_ROWS], ps[:, SIDE:SIDE + A_ROWS], ACT.Copy).then_inc(sem("cols_ready"), 1)
            nc.scalar.activation(col[:, 1, :], ps[:, SIDE + P:SIDE + 2 * P], ACT.Copy).then_inc(sem("cols_ready"), 1)
            nc.scalar.activation(col[:, 2:9, 0:CONV_ROWS],
                                 ps[:, SIDE + 2 * P:SIDE + 9 * P].rearrange("p (n r) -> p n r", n=7)[:, :, 0:CONV_ROWS],
                                 ACT.Copy).then_inc(sem("cols_ready"), 1)
            act.wait_ge(sem("cols_ready"), 3)
            nc.scalar.activation(sm(C_ACT, KT), colB(B_C, KT), ACT.Silu).then_inc(sem("c_act"), 1)

            rest_rounds("rest1", IDX_REST)
            lead("in1", 1)
            norm(0, 0)

            def rest1_out():
                act.wait_ge(w_used, 2)
                for t in range(TT):
                    nc.scalar.activation(kidx2[:, t, :, :], side(t, IDX_DIM).unsqueeze(1).to_broadcast([P, 2, IDX_DIM]),
                                         ACT.Copy).then_inc(sem("kidx_out"), 1)
                    nc.scalar.activation(sm(WIDX + IDX_HEADS * t, IDX_HEADS), side(t, IDX_REST)[:, IDX_DIM:IDX_REST], ACT.Copy,
                                         scale=IDX_HEADS ** -0.5 * IDX_DIM ** -0.5).then_inc(sem("kidx_out"), 1)

            pairs("in1", epi_z, before=rest1_out, done=1)
            lead("out1", 2)
            last_epi("in1", epi_z)

            act.wait_ge(epi_done, 10)
            nc.scalar.activation(kT.rearrange("p h s -> p (h s)"), reg(4096, 2048), ACT.Square).then_inc(sem("qk_sq"), 1)
            nc.scalar.activation(qT.rearrange("p h s -> p (h s)"), reg(6144, 2048), ACT.Square).then_inc(sem("qk_sq"), 1)
            act.wait_ge(sem("kidx_turned"), 1)
            nc.scalar.activation(kidxT, side(2, 256), ACT.Copy).then_inc(sem("kidxT_ready"), 1)
            act.wait_ge(sem("qk_ms"), 1)
            nc.scalar.activation(sm(QK_SD, 32), sm(QK_SS, 32), ACT.Sqrt).then_inc(sem("qk_sd"), 1)
            for t in range(TT):
                K = P * (t + 1)
                for b in range(4):
                    n = 4 * t + b
                    act.wait_ge(sem("is_done"), n + 1)
                    if n >= 2:
                        act.wait_ge(sem("relu_used"), n - 1)
                    got = side(2 * (n % 2), 1024).rearrange("p (b j s) -> p b j s", b=2, j=2)[:, :, :, 0:K]
                    nc.scalar.activation(relu_buf[:, n % 2, :, 0:K].rearrange("p (j b) s -> p b j s", b=2), got,
                                         ACT.Relu).then_inc(sem("relu_ready"), 1)
            for n in range(8):
                dst, wcol = ((kT, colA(A_KG)), (qT, colA(A_QG)))[n // 4]
                b, t = divmod(n % 4, 2)
                act.wait_ge(sem("qk_turned"), n + 1)
                nc.scalar.activation(dst[:, 4 * b:4 * b + 4, t * P:(t + 1) * P], side(n % 4).rearrange("p (h s) -> p h s", h=4),
                                     ACT.Copy, scale=wcol).then_inc(sem("qkT_ready"), 1)
            for t in range(TT):
                K = P * (t + 1)
                act.wait_ge(sem("sm_ready"), t + 1)
                nc.scalar.activation(sc_buf[:, :, 0:K], sc_buf[:, :, 0:K], ACT.Exp, scale=HD ** -0.5).then_inc(sem("p_exp"), 1)
                act.wait_ge(sem("p_turned"), t + 1)
                nc.scalar.activation(pT[:, 0:1024 * (t + 1)], ps[:, SIDE:SIDE + 1024 * (t + 1)], ACT.Copy).then_inc(sem("pT_ready"), 1)
                act.wait_ge(sem("pv_done"), t + 1)
                nc.scalar.activation(yT_attn[:, :, t * P:(t + 1) * P], ps[:, SIDE:SIDE + 1024].rearrange("p (h s) -> p h s", h=HEADS),
                                     ACT.Copy).then_inc(sem("yT_attn_ready"), 1)
            act.wait_ge(sem("pool_mixed"), 1)
            for f in range(8):
                nc.scalar.activation(yT_pool[:, f, :], ps[:, SIDE + S * f:SIDE + S * (f + 1)], ACT.Copy,
                                     scale=colA(A_PSC + f)).then_inc(sem("yT_pool_ready"), 1)
            split_mixed(yT_pool, yT_attn, {0: (sem("yT_pool_ready"), 8), 4: (sem("yT_attn_ready"), 2)})

            pairs("out1", epi_none)
            lead("up1", 2)
            norm(1, 2)
            pairs("up1", epi_conv(1, 0))
            lead("down1", 2)
            down("down1", 0, lambda: last_epi("up1", epi_conv(1, 0)))

            rest_rounds("rest2", GATE_RANK)
            lead("in2", 1)
            act.dma_start(gate_w2, w["gate_w2_2"]).then_inc(sem("gate_loaded"), 16)
            norm(2, 3)

            def rest2_out():
                act.wait_ge(w_used, 2 * (PH["rest2"].m0 + 1))
                for t in range(TT):
                    nc.scalar.activation(a_lr[:, t, :], side(t, GATE_RANK), ACT.Copy).then_inc(sem("alr_out"), 1)

            pairs("in2", epi_z, before=rest2_out, done=1)
            lead("out2", 2)
            last_epi("in2", epi_z)

            act.wait_ge(sem("alr_turned"), 1)
            nc.scalar.activation(a_lrT, ps[0:GATE_RANK, SIDE + 1024:SIDE + 1024 + S], ACT.Copy).then_inc(sem("alrT_ready"), 1)
            act.wait_ge(sem("gate_mm"), 1)
            xg, ta = head_tok(A1), head_tok(A2)
            for h in range(GLA_HEADS):
                nc.scalar.activation(xg[:, h, :], ps[:, SIDE + S * h:SIDE + S * (h + 1)], ACT.Identity,
                                     bias=colA(A_GB + h)).then_inc(sem("xg_ready"), 1)
            act.wait_ge(sem("xg_ready"), 4)
            link(nc.scalar.activation(ta, xg, ACT.Abs))
            link(nc.scalar.activation(ta, ta, ACT.Exp, scale=-1.0))
            nc.scalar.activation(ta, ta, ACT.Ln, bias=ones[:, 0:1]).then_inc(sem("ln_ready"), 1)
            act.wait_ge(sem("b_ready"), 1)
            nc.scalar.activation(head_tok(A1), head_tok(A4), ACT.Exp).then_inc(sem("eb_ready"), 1)
            nc.scalar.activation(sm(E_LAST, 16), reg(A4, 1024).rearrange("p (c s) -> p c s", s=CHUNK)[:, :, CHUNK - 1],
                                 ACT.Exp).then_inc(sem("e_last"), 1)
            act.wait_ge(sem("kd_diff"), 1)
            nc.scalar.activation(reg(A3, 1024), reg(A3, 1024), ACT.Exp, scale=-1.0).then_inc(sem("kd_exp"), 1)
            act.wait_ge(sem("kd_turned"), 1)
            nc.scalar.activation(reg(A6, 1024), ps[:, SIDE:SIDE + 1024], ACT.Copy).then_inc(sem("kdT_ready"), 1)
            for n in range(len(LEVELS)):
                act.wait_ge(sem("lvl_diff"), n + 1)
                link(nc.scalar.activation(reg(A1, 1024), reg(A1, 1024), ACT.Abs))
                nc.scalar.activation(reg(A1, 1024), reg(A1, 1024), ACT.Exp, scale=-1.0).then_inc(sem("lvl_exp"), 1)
            r_gate = reg(4096, 2048)
            nc.scalar.activation(r_gate, r_gate, ACT.Silu).then_inc(sem("r_silu"), 1)
            act.wait_ge(sem("o_done"), 1)
            nc.scalar.activation(o_gla.rearrange("p t h e -> p (t h e)"), ps[:, SIDE:SIDE + 2048], ACT.Copy).then_inc(sem("o_out"), 1)
            act.wait_ge(sem("o_out"), 1)
            nc.scalar.activation(reg(A4, 2048), o_gla.rearrange("p t h e -> p (t h e)"), ACT.Square).then_inc(sem("o_sq"), 1)
            act.wait_ge(sem("o_ms"), 1)
            nc.scalar.activation(sm(O_SD, 8), sm(O_SS, 8), ACT.Sqrt).then_inc(sem("o_sd"), 1)
            act.wait_ge(sem("o_turned"), 1)
            for f in range(8):
                nc.scalar.activation(yT_gla[:, f, :], ps[:, SIDE + S * f:SIDE + S * (f + 1)], ACT.Copy,
                                     scale=colA(A_GLA + f % 2)).then_inc(sem("yT_gla_ready"), 1)
            split_mixed(yT_conv, yT_gla, {0: (sem("yT_conv_ready"), 1), 4: (sem("yT_gla_ready"), 8)})

            def gate_row(q):
                act.wait_ge(sem("row_mm"), q + 1)
                nc.scalar.activation(g_row, ps[:, SIDE:SIDE + 2048], ACT.Copy).then_inc(sem("row_ready"), 1)

            def post_norm(q, rows):
                for t in range(TT):
                    nc.scalar.activation(xt.rearrange("p k s -> p (k s)")[:, t * D:(t + 1) * D], rows(t), ACT.Square,
                                         accum_out=sm(P_SS + 2 * q + t)).then_inc(sem("post_sq"), 1)
                act.wait_ge(sem("post_ms"), q + 1)
                nc.scalar.activation(sm(P_SD + 2 * q, 2),
                                     sm(P_SS + 2 * q, 2), ACT.Sqrt).then_inc(sem("post_sd"), 1)

            def epi_y(ph, blk, i0, i, r):
                act.wait_ge(w_used, block_end(ph, i0, blk))
                j = 2 * i0 + blk
                nc.scalar.activation(y[:, :, BLOCK * j:BLOCK * (j + 1)], main(blk).rearrange("p (t n) -> p t n", t=TT),
                                     ACT.Copy).then_inc(epi_done, 1)

            gate_row(0)
            pairs("out2", epi_y)
            lead("up2", 2)
            last_epi("out2", epi_y)
            act.wait_ge(epi_done, PH["out2"].b0 + 4)
            post_norm(0, lambda t: y[:, t, :])
            norm(3, 5)
            gate_row(1)
            pairs("up2", epi_conv(2, 1))
            lead("down2", 2)
            down("down2", 1, lambda: last_epi("up2", epi_conv(2, 1)))
            act.wait_ge(w_used, down_end("down2"))
            post_norm(1, lambda t: ps[:, D * t:D * (t + 1)])

        @block.vector
        def _(dve):
            v = nc.vector
            seq = [0]

            def link(ins):
                seq[0] += 1
                ins.then_inc(sem("dve_step"), 1)
                dve.wait_ge(sem("dve_step"), seq[0])

            def low_half(m, half, r=0, stride=16, n_el=HALF):
                n, hh = RAW_OF[m], 2 * m + half
                dve.wait_ge(hi_ready, hh + 1 + r * stride)
                v.tensor_tensor(w_lo[:, hh % HL_SLOTS, 0:n_el], raw[:, n % RAW_SLOTS, half * n_el:(half + 1) * n_el],
                                w_hi[:, hh % HL_SLOTS, 0:n_el].bitcast(F32), ALU.subtract).then_inc(lo_ready, 1)

            def rest_lows(name, cols):
                for half in range(2):
                    low_half(PH[name].m0, half, n_el=KT * cols // 2)

            def lead(name, chunks):
                for c in range(chunks):
                    for half in range(2):
                        low_half(PH[name].m0 + c, half)

            def mod_chunk(ph, k, r):
                n, c = RAW_OF_MOD[k], k % 4
                dve.wait_ge(raw_full[n % RAW_SLOTS], 16 * (n // RAW_SLOTS + 1) + r * raw_stride(ph))
                part = raw[:, n % RAW_SLOTS, :].rearrange("p (k n) -> p k n", k=KC)
                for kk in range(KC):
                    kt = KC * c + kk
                    step = UNIT_OPS * (k // 4) + kt
                    if kt == 0:
                        v.tensor_scalar(mod_acc[:], part[:, 0, :], sm(C_ACT), None, ALU.mult).then_inc(mod_step, 1)
                    else:
                        dve.wait_ge(mod_step, step + r * UNIT_OPS)
                        v.scalar_tensor_tensor(out=mod_acc[:], in0=part[:, kk, :], scalar=sm(C_ACT + kt), in1=mod_acc[:],
                                               op0=ALU.mult, op1=ALU.add).then_inc(mod_step, 1)

            def mod_columns(unit, u):
                dve.wait_ge(mod_red, u + 1)
                v.tensor_tensor(modc[:, bass.ds(u * 4, 4)], side(3)[:, 508:512], col[:, 1, bass.ds(u * 4 + B_MOD, 4)],
                                ALU.add).then_inc(sem("modc_ready"), 1)

            def pairs(name, epi, before=None, done=2):
                ph = PH[name]

                def body(i0, i, r, layout):
                    for n, kind, at in pair_items(ph, i0):
                        if kind == "m":
                            if at % 4 == 0 and i0 > 0:
                                mod_columns(at // 4 - 1, at // 4 - 1 + r)
                            mod_chunk(ph, at, r)
                            continue
                        c = (at - ph.m0) % 8
                        if i0 > 0 or c >= done:
                            for half in range(2):
                                low_half(at, half, r)
                        if c == 1:
                            if i0 > 0:
                                epi(ph, 1, i0 - 1, i - 1, r)
                            elif before:
                                before()
                        if c == 5:
                            epi(ph, 0, i0, i, r)

                run_pairs(dve, name, body)

            def last_epi(name, epi):
                i = RUNS[name][-1][1] - 1
                epi(PH[name], 1, i, i, 0)

            def last_unit(name):
                u = PH[name].k0 // 4 + RUNS[name][-1][1] - 1
                mod_columns(u, u)

            def norm(p, f, scale, shift=None):
                dve.wait_ge(sem("sq_done"), 2 * p + 2)
                v.tensor_scalar(sm(MS + 2 * p, 2), sm(SS + 2 * p, 2), 1.0 / D, EPS, ALU.mult, ALU.add).then_inc(sem("ms_ready"), 1)
                dve.wait_ge(sem("sd_ready"), p + 1)
                v.reciprocal(sm(RSTD + 2 * p, 2), sm(SD + 2 * p, 2)).then_inc(sem("rstd_ready"), 1)
                dve.wait_ge(sem("rstd_ready"), p + 1)
                v.tensor_scalar(hn[:, 0, :], x[:, 0, :], sm(RSTD + 2 * p), None, ALU.mult).then_inc(sem("hn_dve"), 1)

                def lows(k):
                    dve.wait_ge(act_hi, 8 * f + k + 1)
                    v.tensor_tensor(a_lo[:, 2 * k:2 * k + 2, :], xt[:, 2 * k:2 * k + 2, :],
                                    a_hi[:, 2 * k:2 * k + 2, :].bitcast(F32), ALU.subtract).then_inc(act_ready, 1)

                for k in range(KT // 2):
                    dve.wait_ge(sem("turned"), 8 * p + k + 1)
                    for kk in range(2):
                        kt = 2 * k + kk
                        add = (None, ALU.bypass) if shift is None else (shift[:, kt:kt + 1], ALU.add)
                        v.tensor_scalar(xt[:, kt, :], side(k % 4)[:, S * kk:S * (kk + 1)], scale[:, kt:kt + 1], add[0],
                                        ALU.mult, add[1]).then_inc(sem("xt_ready"), 1)
                    if k:
                        lows(k - 1)
                lows(KT // 2 - 1)

            def split_mixed(f, first, second):
                for k, src in [(k, first[:, 2 * k:2 * k + 2, :]) for k in range(4)] + [(k + 4, second[:, 2 * k:2 * k + 2, :]) for k in range(4)]:
                    dve.wait_ge(act_hi, 8 * f + k + 1)
                    v.tensor_tensor(a_lo[:, 2 * k:2 * k + 2, :], src, a_hi[:, 2 * k:2 * k + 2, :].bitcast(F32),
                                    ALU.subtract).then_inc(act_ready, 1)

            def epi_none(ph, blk, i0, i, r):
                pass

            def epi_residual(ph, blk, i0, i, r):
                dve.wait_ge(w_used, block_end(ph, i0, blk))
                j = 2 * i0 + blk
                xs = x[:, :, BLOCK * j:BLOCK * (j + 1)]
                v.tensor_tensor(xs, main(blk).rearrange("p (t n) -> p t n", t=TT), xs, ALU.add).then_inc(epi_done, 1)

            def epi_conv(layer, q):
                rows = (4, 5) if layer == 1 else (7, 8)

                def epi(ph, blk, i0, i, r):
                    dst = (c_gate, c_val)[blk]
                    n = q * 22 + 2 * i0 + blk
                    dve.wait_ge(sem("conv_first"), 4 * n + 4 + 8 * r)
                    for j, shift in ((1, 1), (0, 2)):
                        if j == 0:
                            dve.wait_ge(sem("conv_second"), 4 * n + 4 + 8 * r)
                        for f in range(4):
                            tap = col[:, rows[j], bass.ds(4 * i + f + FT * blk, 1)]
                            ins = v.scalar_tensor_tensor(
                                out=dst[:, f, shift:], in0=main(blk)[:, S * f:S * (f + 1) - shift], scalar=tap, in1=dst[:, f, shift:],
                                op0=ALU.mult, op1=ALU.add)
                            if j == 1:
                                ins.then_inc(sem("conv_second"), 1)
                            elif f == 3:
                                ins.then_inc(epi_done, 1)
                    if blk == 1:
                        dve.wait_ge(sem("silu_done"), q * 11 + i0 + 1 + r)
                        dve.wait_ge(epi_done, ph.b0 + 2 * i0 + 2 + 2 * r)
                        v.tensor_tensor(g[:, bass.ds(4 * i, 4), :], c_gate, c_val, ALU.mult).then_inc(sem("g_done"), 1)
                return epi

            def down(name, q):
                ph = PH[name]

                def split_g(j, kt, r):
                    dve.wait_ge(sem("g_hi"), FT * q + j + 1 + 4 * r)
                    v.tensor_tensor(a_lo[:, j % 4, :], g[:, bass.ds(kt, 1), :].rearrange("p f s -> p (f s)"),
                                    a_hi[:, j % 4, :].bitcast(F32), ALU.subtract).then_inc(sem("g_split"), 1)

                for j in range(4):
                    split_g(j, j, 0)
                    if j >= 2:
                        for half in range(2):
                            low_half(ph.m0 + j, half)
                with dve.Fori(1, FT // 4) as i:
                    for j in range(4):
                        split_g(4 + j, i * 4 + j, i - 1)
                        for half in range(2):
                            low_half(ph.m0 + 4 + j, half, i - 1, 8)

            rest_lows("rest1", IDX_REST)
            lead("in1", 1)
            dve.wait_ge(sem("cols_ready"), 3)
            norm(0, 0, colA(A_ATTN, KT))
            dve.wait_ge(sem("c_act"), 1)
            pairs("in1", epi_none, done=1)
            lead("out1", 2)
            last_unit("in1")

            for n in range(2):
                dve.wait_ge(sem("qk_sq"), n + 1)
                src = (kT, qT)[n].rearrange("p h s -> p (h s)").rearrange("p (n d) -> p n d", d=HD)
                link(v.tensor_reduce(sm(QK_SS + 16 * n, 16), src, AX_X, ALU.add))
            v.tensor_scalar(sm(QK_SS, 32), sm(QK_SS, 32), 1.0 / HD, EPS, ALU.mult, ALU.add).then_inc(sem("qk_ms"), 1)
            dve.wait_ge(sem("qk_sd"), 1)
            link(v.reciprocal(sm(QK_SS, 32), sm(QK_SD, 32)))
            for n in range(2):
                zz = reg(4096 + 2048 * n, 2048).rearrange("p (n d) -> p n d", d=HD)
                v.tensor_tensor(zz, zz, sm(QK_SS + 16 * n, 16).unsqueeze(2).to_broadcast([P, 16, HD]), ALU.mult).then_inc(sem("qk_normed"), 1)
            for t in range(TT):
                K = P * (t + 1)
                for b in range(4):
                    n = 4 * t + b
                    dve.wait_ge(sem("relu_ready"), n + 1)
                    for hq in range(4):
                        wcol = sm(WIDX + IDX_HEADS * t + 4 * b + hq)
                        rel = relu_buf[:, n % 2, hq, 0:K]
                        if b + hq == 0:
                            link(v.tensor_scalar(iscore[:, t, 0:K], rel, wcol, None, ALU.mult))
                            continue
                        ins = v.scalar_tensor_tensor(out=iscore[:, t, 0:K], in0=rel, scalar=wcol, in1=iscore[:, t, 0:K],
                                                     op0=ALU.mult, op1=ALU.add)
                        if hq == 3:
                            ins.then_inc(sem("relu_used"), 1)
                            dve.wait_ge(sem("relu_used"), n + 1)
                        else:
                            link(ins)
                last = iscore[:, t, t * P:(t + 1) * P]
                link(v.tensor_tensor(last, last, tri, ALU.add))
                link(v.tensor_copy(work[:, t, 0:K], iscore[:, t, 0:K]))
                for k in range(TOPK // 8):
                    link(v.max(top8[:, 8 * t + k, :], work[:, t, 0:K]))
                    link(v.match_replace(work[:, t, 0:K], top8[:, 8 * t + k, :], work[:, t, 0:K], NEG))
                link(v.tensor_tensor(notsel[:, t, 0:K], iscore[:, t, 0:K], work[:, t, 0:K], ALU.is_equal))
            for t in range(TT):
                K = P * (t + 1)
                s = sc_buf[:, :, 0:K]
                dve.wait_ge(sem("sc_done"), t + 1)
                if t:
                    dve.wait_ge(sem("p_turned"), t)
                link(v.scalar_tensor_tensor(out=s, in0=notsel[:, t, 0:K].unsqueeze(1).to_broadcast([P, HEADS, K]), scalar=NEG,
                                            in1=ps[:, SIDE:SIDE + HEADS * S].rearrange("p (h s) -> p h s", h=HEADS)[:, :, 0:K],
                                            op0=ALU.mult, op1=ALU.add))
                link(v.tensor_reduce(sm(MX, HEADS), s, AX_X, ALU.max))
                v.tensor_tensor(s, s, sm(MX, HEADS).unsqueeze(2).to_broadcast([P, HEADS, K]), ALU.subtract).then_inc(sem("sm_ready"), 1)
                dve.wait_ge(sem("p_exp"), t + 1)
                link(v.tensor_reduce(sm(RSUM, HEADS), s, AX_X, ALU.add))
                link(v.reciprocal(sm(RINV, HEADS), sm(RSUM, HEADS)))
                v.tensor_tensor(s, s, sm(RINV, HEADS).unsqueeze(2).to_broadcast([P, HEADS, K]), ALU.mult).then_inc(sem("p_ready"), 1)
            split_mixed(1, yT_pool, yT_attn)

            pairs("out1", epi_residual)
            lead("up1", 2)
            last_epi("out1", epi_residual)
            last_unit("out1")
            norm(1, 2, colA(A_FFN, KT))
            pairs("up1", epi_conv(1, 0))
            lead("down1", 2)
            last_epi("up1", epi_conv(1, 0))
            last_unit("up1")
            down("down1", 0)
            rest_lows("rest2", GATE_RANK)
            lead("in2", 1)
            dve.wait_ge(w_used, down_end("down1"))
            for t in range(TT):
                v.tensor_tensor(x[:, t, :], ps[:, D * t:D * (t + 1)], x[:, t, :], ALU.add).then_inc(sem("x_new"), 1)

            def scales(at, wcols, first):
                dve.wait_ge(sem("modc_ready"), first // 4 + 4)
                link(v.scalar_tensor_tensor(out=sm(at, KT), in0=modc[:, first:first + KT], scalar=1.0, in1=wcols, op0=ALU.add, op1=ALU.mult))

            scales(SCALE_M, colA(A_MPRE, KT), 16)
            norm(2, 3, sm(SCALE_M, KT), modc[:, 0:KT])
            pairs("in2", epi_none, done=1)
            lead("out2", 2)
            last_unit("in2")

            xg, ta, bb = head_tok(A1), head_tok(A2), head_tok(A4)
            dve.wait_ge(sem("ln_ready"), 1)
            link(v.scalar_tensor_tensor(out=ta, in0=xg, scalar=0.0, in1=ta, op0=ALU.min, op1=ALU.subtract))
            link(v.tensor_scalar(ta, ta, 1.0 / GATE_TAU, None, ALU.mult))
            for h in range(GLA_HEADS):
                ins = v.tensor_tensor_scan(bb[:, h, :], con[:, C_RST:C_RST + S], ta[:, h, :], 0.0, ALU.mult, ALU.add)
                if h < GLA_HEADS - 1:
                    link(ins)
            ins.then_inc(sem("b_ready"), 1)
            dve.wait_ge(sem("b_ready"), 1)
            q, k = head_tok(0), head_tok(1024)
            GS = HD ** -0.5
            bc = reg(A4, 1024).rearrange("p (c s) -> p c s", s=CHUNK)
            v.tensor_tensor(reg(A3, 1024).rearrange("p (c s) -> p c s", s=CHUNK), bc,
                            bc[:, :, CHUNK - 1:CHUNK].to_broadcast([P, 16, CHUNK]), ALU.subtract).then_inc(sem("kd_diff"), 1)
            dve.wait_ge(sem("eb_ready"), 1)
            dve.wait_ge(sem("q_ex_zero"), 1)
            for c in range(1, NCHUNK):
                at = CHUNK * (c % 2)
                ins = v.scalar_tensor_tensor(out=q_ex[:, :, c - 1, at:at + CHUNK], in0=q[:, :, CHUNK * c:CHUNK * (c + 1)], scalar=GS,
                                             in1=head_tok(A1)[:, :, CHUNK * c:CHUNK * (c + 1)], op0=ALU.mult, op1=ALU.mult)
            ins.then_inc(sem("q_ex_ready"), 1)
            dve.wait_ge(sem("kd_exp"), 1)
            v.tensor_tensor(reg(A3, 1024), reg(A3, 1024), reg(1024, 1024), ALU.mult).then_inc(sem("kd_ready"), 1)
            dve.wait_ge(sem("e_last"), 1)
            dve.wait_ge(sem("u_done"), 1)
            link(v.tensor_copy(states[:, 0, :, :], side(0, 1024).rearrange("p (h e) -> p h e", h=GLA_HEADS)))
            dve.wait_ge(sem("u_done"), 2)
            for c in (1, 2):
                if c == 2:
                    dve.wait_ge(sem("u_done"), 3)
                for h in range(GLA_HEADS):
                    ins = v.scalar_tensor_tensor(out=states[:, c, h, :], in0=states[:, c - 1, h, :], scalar=sm(E_LAST + NCHUNK * h + c),
                                                 in1=side((0, 2, 0)[c], 1024)[:, GLA_DV * h:GLA_DV * (h + 1)], op0=ALU.mult, op1=ALU.add)
                    if h < GLA_HEADS - 1 or c == 2:
                        link(ins) if h < GLA_HEADS - 1 else ins.then_inc(sem("states_ready"), 1)
                    else:
                        ins.then_inc(sem("u_used"), 1)
                        dve.wait_ge(sem("u_used"), 1)
            for n in range(len(LEVELS) + 1):
                if n < len(LEVELS):
                    s = LEVELS[n]
                    b4 = reg(A4, 1024).rearrange("p (c s) -> p c s", s=2 * s)
                    if n:
                        dve.wait_ge(sem("k_lvl"), n)
                    v.tensor_tensor(reg(A1, 1024).rearrange("p (c s) -> p c s", s=2 * s), b4,
                                    b4[:, :, s - 1:s].to_broadcast([P, 512 // s, 2 * s]), ALU.subtract).then_inc(sem("lvl_diff"), 1)
                    dve.wait_ge(sem("lvl_exp"), n + 1)
                    if n:
                        dve.wait_ge(sem("lvl_mm"), n)
                    v.scalar_tensor_tensor(out=head_tok(A2), in0=q, scalar=GS, in1=head_tok(A1), op0=ALU.mult,
                                           op1=ALU.mult).then_inc(sem("q_lvl"), 1)
                else:
                    dve.wait_ge(sem("lvl_mm"), n)
                    v.tensor_scalar(head_tok(A2), q, GS, None, ALU.mult).then_inc(sem("q_lvl"), 1)
                dve.wait_ge(sem("lvl_mm"), n + 1)
                mask = con[:, C_LVL + P * n:C_LVL + P * (n + 1)].unsqueeze(1).to_broadcast([P, 8, P])
                got = side(2 * (n % 2), 1024).rearrange("p (n i) -> p n i", n=8)
                acc = reg(A5, 1024).rearrange("p (n i) -> p n i", n=8)
                tmp = reg(A6, 1024).rearrange("p (n i) -> p n i", n=8)
                if n == 0:
                    link(v.tensor_tensor(acc, got, mask, ALU.mult))
                else:
                    link(v.tensor_tensor(tmp, got, mask, ALU.mult))
                    ins = v.tensor_tensor(acc, acc, tmp, ALU.add)
                    if n < len(LEVELS):
                        link(ins)
                    else:
                        ins.then_inc(sem("scores_ready"), 1)
            dve.wait_ge(sem("o_sq"), 1)
            link(v.tensor_reduce(sm(O_SS, 8), reg(A4, 2048).rearrange("p (n e) -> p n e", e=GLA_DV), AX_X, ALU.add))
            v.tensor_scalar(sm(O_SS, 8), sm(O_SS, 8), 1.0 / GLA_DV, EPS, ALU.mult, ALU.add).then_inc(sem("o_ms"), 1)
            dve.wait_ge(sem("o_sd"), 1)
            link(v.reciprocal(sm(O_SS, 8), sm(O_SD, 8)))
            o8 = reg(A2, 2048).rearrange("p (n e) -> p n e", e=GLA_DV)
            link(v.tensor_tensor(o8, o8, sm(O_SS, 8).unsqueeze(2).to_broadcast([P, 8, GLA_DV]), ALU.mult))
            dve.wait_ge(sem("r_silu"), 1)
            for b in range(2):
                oo = reg(A2, 2048).rearrange("p (t n) -> p t n", t=TT)[:, :, 512 * b:512 * (b + 1)]
                v.tensor_tensor(oo, oo, z[:, 4 + b, :].rearrange("p (t n) -> p t n", t=TT), ALU.mult).then_inc(sem("o_gated"), 1)
            cb, cc, cx = zw(6), zw(8), zw(10)
            dve.wait_ge(sem("ccx_ready"), 1)
            for f in range(8):
                link(v.tensor_scalar(cx[:, f, :], cc[:, f, :], colA(A_CW + 16 + f), None, ALU.mult))
            for j, shift in ((1, 1), (0, 2)):
                for f in range(8):
                    link(v.scalar_tensor_tensor(out=cx[:, f, shift:], in0=cc[:, f, 0:S - shift], scalar=colA(A_CW + 8 * j + f),
                                                in1=cx[:, f, shift:], op0=ALU.mult, op1=ALU.add))
            v.tensor_tensor(cb, cb, cx, ALU.mult).then_inc(sem("yT_conv_ready"), 1)
            split_mixed(4, yT_conv, yT_gla)

            def gate_diag(qq, wcols, first):
                dve.wait_ge(sem("modc_ready"), first // 4 + 4)
                link(v.tensor_tensor(sm(GP + 0, KT), modc[:, first:first + KT], wcols, ALU.mult))
                v.tensor_tensor(diag, ident.unsqueeze(1).to_broadcast([P, KT, P]), sm(GP, KT).unsqueeze(2).to_broadcast([P, KT, P]),
                                ALU.mult).then_inc(sem("diag_ready"), 1)

            def post_norm(qq, rows):
                dve.wait_ge(sem("post_sq"), 2 * qq + 2)
                v.tensor_scalar(sm(P_SS + 2 * qq, 2), sm(P_SS + 2 * qq, 2), 1.0 / D, EPS, ALU.mult, ALU.add).then_inc(sem("post_ms"), 1)
                dve.wait_ge(sem("post_sd"), qq + 1)
                link(v.reciprocal(sm(P_RSTD + 2 * qq, 2), sm(P_SD + 2 * qq, 2)))
                dve.wait_ge(sem("row_ready"), qq + 1)
                for t in range(TT):
                    link(v.scalar_tensor_tensor(out=y[:, t, :], in0=rows(t), scalar=sm(P_RSTD + 2 * qq + t), in1=g_row, op0=ALU.mult, op1=ALU.mult))
                    v.tensor_tensor(x[:, t, :], x[:, t, :], y[:, t, :], ALU.add).then_inc(sem("x_new"), 1)

            gate_diag(0, colA(A_MPOST, KT), 32)
            pairs("out2", epi_none)
            lead("up2", 2)
            post_norm(0, lambda t: y[:, t, :])
            scales(SCALE_F, colA(A_FPRE, KT), 64)
            norm(3, 5, sm(SCALE_F, KT), modc[:, 48:64])
            gate_diag(1, colB(B_FPOST, KT), 80)
            pairs("up2", epi_conv(2, 1))
            lead("down2", 2)
            last_epi("up2", epi_conv(2, 1))
            down("down2", 1)
            dve.wait_ge(w_used, down_end("down2"))
            post_norm(1, lambda t: ps[:, D * t:D * (t + 1)])

        @block.gpsimd
        def _(pool):
            gp = nc.gpsimd
            seq = [0]

            def link(ins):
                seq[0] += 1
                ins.then_inc(sem("pool_step"), 1)
                pool.wait_ge(sem("pool_step"), seq[0])

            pool.wait_ge(epi_done, 10)
            pool.wait_ge(sem("qkT_ready"), 4)
            for n, win_size in enumerate(WINDOWS):
                u = yT_pool[:, 2 * n:2 * n + 2, :]
                cur, sh, b = u, 1, 0
                while sh < win_size:
                    nxt = win[b]
                    link(gp.tensor_tensor(nxt[:, :, sh:], cur[:, :, sh:], cur[:, :, 0:S - sh], ALU.add))
                    link(gp.tensor_copy(nxt[:, :, 0:sh], cur[:, :, 0:sh]))
                    cur, b, sh = nxt, 1 - b, 2 * sh
                mean = win[b]
                link(gp.tensor_scalar(mean[:, :, 16:], cur[:, :, 16:], 1.0 / win_size, None, ALU.mult))
                link(gp.tensor_tensor(mean[:, :, 0:16], cur[:, :, 0:16],
                                      con[:, C_INV + 16 * n:C_INV + 16 * n + 16].unsqueeze(1).to_broadcast([P, 2, 16]), ALU.mult))
                ins = gp.tensor_tensor(dT[:, 2 * n:2 * n + 2, :], mean, u, ALU.subtract)
                if n < len(WINDOWS) - 1:
                    link(ins)
                else:
                    ins.then_inc(sem("d_ready"), 1)

            pool.wait_ge(epi_done, PH["in2"].b0 + 1)
            gp.memset(q_ex, 0.0).then_inc(sem("q_ex_zero"), 1)
            pool.wait_ge(epi_done, PH["in2"].b0 + 12)
            gp.tensor_tensor(zw(8), zw(8), zw(10), ALU.mult).then_inc(sem("ccx_ready"), 1)
            k = reg(1024, 1024)
            for n in range(len(LEVELS)):
                pool.wait_ge(sem("lvl_exp"), n + 1)
                if n:
                    pool.wait_ge(sem("lvl_mm"), n)
                gp.tensor_tensor(reg(A3, 1024), k, reg(A1, 1024), ALU.mult).then_inc(sem("k_lvl"), 1)

        @block.tensor
        def _(pe):
            mmul = nc.tensor.matmul

            def three(dst, lhs_hi, lhs_lo, rhs_hi, rhs_lo, start, stop):
                mmul(dst, lhs_hi, rhs_hi, start=start, stop=False, skip_group_check=True)
                mmul(dst, lhs_hi, rhs_lo, start=False, stop=False, skip_group_check=True)
                return mmul(dst, lhs_lo, rhs_hi, start=False, stop=stop, skip_group_check=True)

            def rest(name, cols, f, p):
                pe.wait_ge(sem("xt_ready"), KT * (p + 1))
                m = PH[name].m0
                for half in range(2):
                    hh = 2 * m + half
                    pe.wait_ge(lo_ready, hh + 1)
                    for kk in range(KT // 2):
                        kt = KT // 2 * half + kk
                        if kt % 2 == 0:
                            pe.wait_ge(act_ready, 8 * f + kt // 2 + 1)
                        for t in range(TT):
                            tok = slice(t * P, (t + 1) * P)
                            wc = slice(kk * cols, (kk + 1) * cols)
                            mm = three(side(t, cols), a_hi[:, kt, tok], a_lo[:, kt, tok], w_hi[:, hh % HL_SLOTS, wc],
                                       w_lo[:, hh % HL_SLOTS, wc], kt == 0, kt == KT - 1)
                    mm.then_inc(w_used, 1)

            def half_T(dst, hh, kts, first, last):
                for kk, kt in enumerate(kts):
                    for t in range(TT):
                        tok = slice(t * P, (t + 1) * P)
                        wc = slice(kk * BLOCK, (kk + 1) * BLOCK)
                        mm = three(dst[:, t * BLOCK:(t + 1) * BLOCK], a_hi[:, kt, tok], a_lo[:, kt, tok],
                                   w_hi[:, hh % HL_SLOTS, wc], w_lo[:, hh % HL_SLOTS, wc],
                                   first and kk == 0, last and kk == len(kts) - 1)
                return mm

            def half_W(dst, hh, kts, first, last):
                for kk, kt in enumerate(kts):
                    for ft in range(4):
                        wc = slice(kk * BLOCK + ft * P, kk * BLOCK + (ft + 1) * P)
                        mm = three(dst[:, ft * S:(ft + 1) * S], w_hi[:, hh % HL_SLOTS, wc], w_lo[:, hh % HL_SLOTS, wc],
                                   a_hi[:, kt, :], a_lo[:, kt, :], first and kk == 0 and ft % 2 == 0, last and kk == len(kts) - 1)
                return mm

            def pairs(name, fresh):
                ph = PH[name]
                f = FILL[name]

                def body(i0, i, r, layout):
                    for blk in range(2):
                        b = ph.b0 + 2 * i0 + blk
                        if b >= 2:
                            pe.wait_ge(epi_done, b - 1 + 2 * r)
                        for c in range(BLOCK_CHUNKS):
                            for half in range(2):
                                hh = 2 * (ph.m0 + 8 * i0 + 4 * blk + c) + half
                                pe.wait_ge(lo_ready, hh + 1 + 16 * r)
                                if fresh and i0 == 0 and blk == 0:
                                    pe.wait_ge(act_ready, 8 * f + 2 * c + half + 1)
                                kts = [KC * c + 2 * half, KC * c + 2 * half + 1]
                                (half_T if layout == "T" else half_W)(
                                    main(blk), hh, kts, c + half == 0, c == BLOCK_CHUNKS - 1 and half == 1).then_inc(w_used, 1)
                    if ph.mod:
                        u = ph.k0 // 4 + i0
                        pe.wait_ge(mod_step, UNIT_OPS * (u + 1) + UNIT_OPS * r)
                        for j in range(4):
                            mm = mmul(side(3)[:, 508 + j:509 + j], mod_acc[:, j * P:(j + 1) * P], ones[:, 0:1], start=True, stop=True)
                        mm.then_inc(mod_red, 1)

                run_pairs(pe, name, body)

            def down(name, q):
                ph = PH[name]

                def chunk(j, r):
                    pe.wait_ge(sem("g_split"), FT * q + j + 1 + 4 * r)
                    for half in range(2):
                        hh = 2 * (ph.m0 + j) + half
                        pe.wait_ge(lo_ready, hh + 1 + 8 * r)
                        for t in range(TT):
                            for n in range(2):
                                at = t * D + half * HALF + n * BLOCK
                                tok = slice(t * P, (t + 1) * P)
                                wc = slice(n * BLOCK, (n + 1) * BLOCK)
                                mm = three(ps[:, at:at + BLOCK], a_hi[:, j % 4, tok], a_lo[:, j % 4, tok], w_hi[:, hh % HL_SLOTS, wc],
                                           w_lo[:, hh % HL_SLOTS, wc], j == 0, False)
                        mm.then_inc(w_used, 1)

                for j in range(4):
                    chunk(j, 0)
                with pe.Fori(1, FT // 4) as i:
                    for j in range(4):
                        chunk(4 + j, i - 1)

            def norm(p):
                pe.wait_ge(sem("hn_dve"), p + 1)
                pe.wait_ge(sem("hn_act"), p + 1)
                for k in range(KT // 2):
                    if k >= 4:
                        pe.wait_ge(sem("xt_ready"), KT * p + 2 * (k - 4) + 2)
                    for kk in range(2):
                        for t in range(TT):
                            at = S * kk + P * t
                            mm = nc.tensor.transpose(side(k % 4)[:, at:at + P], hn[:, t, (2 * k + kk) * P:(2 * k + kk + 1) * P], ident)
                    mm.then_inc(sem("turned"), 1)

            pe.wait_ge(sem("params_loaded"), 16 * 23)
            rows = [A_ROWS, P] + [CONV_ROWS] * 7
            for n in range(9):
                mm = nc.tensor.transpose(ps[:, SIDE + P * n:SIDE + P * n + rows[n]], stage[0:rows[n], n, :], ident[0:rows[n], 0:rows[n]])
            mm.then_inc(sem("cols_turned"), 1)
            pe.wait_ge(sem("cols_ready"), 3)

            norm(0)
            rest("rest1", IDX_REST, 0, 0)
            pairs("in1", False)

            pe.wait_ge(sem("kidx_out"), 4)
            for t in range(TT):
                mm = nc.tensor.transpose(side(2)[:, t * P:(t + 1) * P], kidx2[:, t, :, :].rearrange("p c d -> p (c d)"), ident)
            mm.then_inc(sem("kidx_turned"), 1)
            pe.wait_ge(sem("kidxT_ready"), 1)
            pe.wait_ge(sem("modc_ready"), 5)
            for t in range(TT):
                K = P * (t + 1)
                for b in range(4):
                    n = 4 * t + b
                    if n >= 2:
                        pe.wait_ge(sem("relu_ready"), n - 1)
                    for hq in range(4):
                        h = 4 * b + hq
                        half = slice(IDX_DIM * (h % 2), IDX_DIM * (h % 2 + 1))
                        at = S * (hq // 2)
                        mm = mmul(side(2 * (n % 2) + hq % 2)[:, at:at + K], zw(0)[half, h // 2, t * P:(t + 1) * P],
                                  kidxT[half, 0:K], start=True, stop=True, skip_group_check=True)
                    mm.then_inc(sem("is_done"), 1)
            for n in range(8):
                b, t = divmod(n % 4, 2)
                if n % 4 == 0:
                    pe.wait_ge(sem("qk_normed"), n // 4 + 1)
                pe.wait_ge(sem("relu_ready"), 8)
                if n >= 4:
                    pe.wait_ge(sem("qkT_ready"), n - 3)
                for h in range(4):
                    at = t * 512 + h * HD
                    mm = nc.tensor.transpose(side(n % 4)[:, h * P:(h + 1) * P], z[:, 4 + 2 * (n // 4) + b, at:at + HD], ident)
                mm.then_inc(sem("qk_turned"), 1)
            pe.wait_ge(sem("qkT_ready"), 8)
            for t in range(TT):
                K = P * (t + 1)
                if t:
                    pe.wait_ge(sem("yT_attn_ready"), t)
                for h in range(HEADS):
                    mm = mmul(ps[:, SIDE + S * h:SIDE + S * h + K], qT[:, h, t * P:(t + 1) * P], kT[:, h, 0:K], start=True, stop=True,
                              skip_group_check=True)
                mm.then_inc(sem("sc_done"), 1)
                pe.wait_ge(sem("p_ready"), t + 1)
                for st in range(t + 1):
                    for h in range(HEADS):
                        at = SIDE + P * (HEADS * st + h)
                        mm = nc.tensor.transpose(ps[:, at:at + P], sc_buf[:, h, st * P:(st + 1) * P], ident)
                mm.then_inc(sem("p_turned"), 1)
                pe.wait_ge(sem("pT_ready"), t + 1)
                for h in range(HEADS):
                    for st in range(t + 1):
                        at = st * 512 + (h % 4) * HD
                        mm = mmul(ps[:, SIDE + P * h:SIDE + P * (h + 1)], z[:, 2 + h // 4, at:at + HD],
                                  pT[:, P * (HEADS * st + h):P * (HEADS * st + h + 1)], start=(st == 0), stop=(st == t), skip_group_check=True)
                mm.then_inc(sem("pv_done"), 1)
            pe.wait_ge(sem("yT_attn_ready"), 2)
            pe.wait_ge(sem("d_ready"), 1)
            for f in range(8):
                for c in range(2):
                    mm = mmul(ps[:, SIDE + S * f:SIDE + S * (f + 1)], pool_w[:, f // 2, c, P * (f % 2):P * (f % 2 + 1)],
                              dT[:, 2 * (f // 2) + c, :], start=(c == 0), stop=(c == 1), skip_group_check=True)
            mm.then_inc(sem("pool_mixed"), 1)

            pairs("out1", True)
            norm(1)
            pairs("up1", True)
            down("down1", 0)

            norm(2)
            rest("rest2", GATE_RANK, 3, 2)
            pairs("in2", False)
            pe.wait_ge(sem("alr_out"), 2)
            for t in range(TT):
                mm = nc.tensor.transpose(ps[0:GATE_RANK, SIDE + 1024 + t * P:SIDE + 1024 + (t + 1) * P], a_lr[:, t, :], ident)
            mm.then_inc(sem("alr_turned"), 1)
            pe.wait_ge(sem("alrT_ready"), 1)
            pe.wait_ge(sem("gate_loaded"), 16)
            for h in range(GLA_HEADS):
                mm = mmul(ps[:, SIDE + S * h:SIDE + S * (h + 1)], gate_w2[:, h * HD:(h + 1) * HD], a_lrT, start=True, stop=True,
                          skip_group_check=True)
            mm.then_inc(sem("gate_mm"), 1)
            pe.wait_ge(sem("kd_ready"), 1)
            for h in range(GLA_HEADS):
                for t in range(TT):
                    at = SIDE + P * (TT * h + t)
                    mm = nc.tensor.transpose(ps[:, at:at + P], head_tok(A3)[:, h, t * P:(t + 1) * P], ident)
            mm.then_inc(sem("kd_turned"), 1)
            pe.wait_ge(sem("kdT_ready"), 1)
            kdT = reg(A6, 1024).rearrange("p (h t d) -> p h t d", h=GLA_HEADS, t=TT)

            def vv(t, h):
                return z[:, 2 + h // 2, 512 * t + GLA_DV * (h % 2):512 * t + GLA_DV * (h % 2 + 1)]

            pe.wait_ge(sem("modc_ready"), 24)
            for c in range(NCHUNK - 1):
                if c == 2:
                    pe.wait_ge(sem("u_used"), 1)
                rows_c = slice(CHUNK * (c % 2), CHUNK * (c % 2 + 1))
                for h in range(GLA_HEADS):
                    mm = mmul(side((0, 2, 0)[c], 1024)[:, GLA_DV * h:GLA_DV * (h + 1)], kdT[rows_c, h, c // 2, :], vv(c // 2, h)[rows_c, :],
                              start=True, stop=True, skip_group_check=True)
                mm.then_inc(sem("u_done"), 1)
            pe.wait_ge(sem("states_ready"), 1)
            for n in range(len(LEVELS) + 1):
                pe.wait_ge(sem("q_lvl"), n + 1)
                if n < len(LEVELS):
                    pe.wait_ge(sem("k_lvl"), n + 1)
                kk = head_tok(A3) if n < len(LEVELS) else head_tok(1024)
                for h in range(GLA_HEADS):
                    for t in range(TT):
                        tok = slice(t * P, (t + 1) * P)
                        at = P * (TT * h + t)
                        mm = mmul(side(2 * (n % 2), 1024)[:, at:at + P], kk[:, h, tok], head_tok(A2)[:, h, tok], start=True, stop=True,
                                  skip_group_check=True)
                mm.then_inc(sem("lvl_mm"), 1)
            pe.wait_ge(sem("scores_ready"), 1)
            pe.wait_ge(sem("q_ex_ready"), 1)
            sc = reg(A5, 1024).rearrange("p (h t i) -> p h t i", h=GLA_HEADS, t=TT)
            for t in range(TT):
                for h in range(GLA_HEADS):
                    dst = side(2 * t, 1024)[:, GLA_DV * h:GLA_DV * (h + 1)]
                    mmul(dst, sc[:, h, t, :], vv(t, h), start=True, stop=False, skip_group_check=True)
                    chunks = [c for c in (2 * t, 2 * t + 1) if c > 0]
                    for c in chunks:
                        mm = mmul(dst, q_ex[:, h, c - 1, :], states[:, c - 1, h, :], start=False, stop=(c == chunks[-1]),
                                  skip_group_check=True)
            mm.then_inc(sem("o_done"), 1)
            pe.wait_ge(sem("o_gated"), 2)
            for f in range(8):
                for t in range(TT):
                    mm = nc.tensor.transpose(ps[:, SIDE + S * f + P * t:SIDE + S * f + P * (t + 1)],
                                             reg(A2, 2048).rearrange("p (t n) -> p t n", t=TT)[:, t, f * P:(f + 1) * P], ident)
            mm.then_inc(sem("o_turned"), 1)

            def gate_row(q):
                pe.wait_ge(sem("diag_ready"), q + 1)
                for n in range(4):
                    mm = mmul(side(n), ones, diag[:, 4 * n:4 * n + 4, :].rearrange("p k f -> p (k f)"), start=True, stop=True)
                mm.then_inc(sem("row_mm"), 1)

            pe.wait_ge(sem("yT_gla_ready"), 8)
            gate_row(0)
            pairs("out2", True)
            norm(3)
            gate_row(1)
            pairs("up2", True)
            pe.wait_ge(sem("row_ready"), 2)
            down("down2", 1)


VECTORS = ["attn_norm_g", "w_in", "pool_w", "pool_scale", "q_norm_g", "k_norm_g", "w_out", "ffn_norm_g", "w_up", "conv_w", "conv_b",
           "w_down", "c_2", "w_mod_2", "b_mod_2", "mix_pre_w_2", "mix_post_w_2", "w_in_2", "conv_w_2", "gate_w2_2", "gate_b_2",
           "gla_norm_w_2", "w_out_2", "ffn_pre_w_2", "ffn_post_w_2", "w_up_2", "ffn_conv_w_2", "w_down_2"]


def kernel(**inputs):
    import concourse.bacc as bacc
    from concourse.bass_utils import run_bass_kernel_spmd

    nc = bacc.Bacc("TRN2", target_bir_lowering=False, num_devices=1, dynamic_dma_scratch_size=1024)
    arrays = {}

    def dram(name, a):
        arrays[name] = a
        return nc.dram_tensor(name, a.shape, F32, kind="ExternalInput").ap()

    x = np.ascontiguousarray(inputs["x"])
    x_in = dram("in_x", x.reshape(S, D))
    w = {}
    for name in VECTORS:
        a = np.ascontiguousarray(inputs[name])
        if name.endswith("_2") and a.shape[0] == 1:
            a = a.reshape(a.shape[1:])
        w[name] = dram("in_" + name, a)
    consts = dram("in_constants", constants())
    out = nc.dram_tensor("out_x", (S, D), F32, kind="ExternalOutput").ap()
    two_blocks(nc, consts, x_in, out, w)
    r = run_bass_kernel_spmd(nc, [arrays], core_ids=[0])
    return r.results[0]["out_x"].reshape(x.shape)
```

```python
from contextlib import ExitStack

import numpy as np

import concourse.bass as bass
from concourse import mybir

F32 = mybir.dt.float32
F32R = mybir.dt.float32r
ALU = mybir.AluOpType
ACT = mybir.ActivationFunctionType
AX_X = mybir.AxisListType.X

P = 128
D = 2048
S = 256
TT = S // P
KT = D // P
F = 5632
FT = F // P
EPS = 1e-6
NEG = float(np.finfo(np.float32).min)
HEADS = 8
HD = 128
IDX_HEADS = 16
IDX_DIM = 64
TOPK = S // 4
WINDOWS = (2, 4, 8, 16)
GLA_HEADS = 4
GLA_DV = 256
CHUNK = 64
NCHUNK = S // CHUNK
GATE_RANK = 16
GATE_TAU = 16
LEVELS = (32, 16, 8, 4, 2, 1)

BLOCK = 512
KC = 4
CHUNK_EL = KC * BLOCK
HALF = CHUNK_EL // 2
RAW_SLOTS = 4
HL_SLOTS = 4
BLOCK_CHUNKS = KT // KC
UNIT_OPS = KT

IDX_REST = IDX_DIM + IDX_HEADS
IN1_STARTS = (4096, 2048, 1024, 0, 3072)
IN2_STARTS = (3072, 4096, 5120, 1024, 2048, 0)
IN1_REST = 5120
IN2_REST = 6144

C_ID, C_ONE, C_LVL, C_RST, C_TRI, C_INV = 0, 128, 256, 256 + 896, 256 + 896 + 256, 256 + 896 + 384
C_N = C_INV + 64

A_ATTN, A_FFN, A_PSC, A_MPRE, A_FPRE, A_MPOST, A_GB, A_QG, A_KG, A_GLA, A_CW = 0, 16, 32, 40, 56, 72, 88, 92, 93, 94, 96
A_ROWS = 120
B_MOD, B_C, B_FPOST = 0, 96, 112
CONV_ROWS = 2 * FT
N_FIRST, N_SECOND = 12, 10


def constants():
    c = np.zeros((P, C_N), np.float32)
    c[:, C_ID:C_ID + P] = np.eye(P)
    c[:, C_ONE:C_ONE + P] = 1.0
    j, i = np.arange(P)[:, None], np.arange(P)[None, :]
    for n, s in enumerate(LEVELS):
        c[:, C_LVL + n * P:C_LVL + (n + 1) * P] = (j // (2 * s) == i // (2 * s)) & (j % (2 * s) < s) & (i % (2 * s) >= s)
    c[:, C_LVL + 6 * P:C_LVL + 7 * P] = np.eye(P)
    c[:, C_RST:C_RST + S] = (np.arange(S) % CHUNK != 0)
    c[:, C_TRI:C_TRI + P] = np.where(i <= j, 0.0, NEG)
    for n, w in enumerate(WINDOWS):
        c[:, C_INV + 16 * n:C_INV + 16 * n + 16] = 1.0 / np.minimum(np.arange(16) + 1, w)
    return c


class Pair:

    def __init__(self, order, units, block, mod):
        self.m0 = sum(1 for kind, _ in order if kind == "g")
        self.n0, self.b0 = len(order), block
        self.unit = units if mod else None


class Phase:
    def __init__(self):
        self.pairs, self.rest, self.m0, self.n0 = [], None, None, None


STREAM = (
    ("in1", (1, 1, 1, 1, 0), True, 0),
    ("out1", (1, 1), False, 0),
    ("up1", (1,) * 11, False, 0),
    ("down1", (), False, FT),
    ("in2", (1, 0, 0, 0, 0, 0), True, 0),
    ("out2", (1, 1), False, 0),
    ("up2", (1,) * 4 + (0,) * 7, False, 0),
    ("down2", (), False, FT),
)


def plan():
    order, phases, blocks, units = [], {}, 0, 0
    count = {"g": 0, "m": 0}

    def add(kinds):
        for kind in kinds:
            order.append((kind, count[kind]))
            count[kind] += 1

    for name, mods, rest, single in STREAM:
        ph = phases[name] = Phase()
        ph.m0, ph.n0 = count["g"], len(order)
        for i, mod in enumerate(mods):
            ph.pairs.append(Pair(order, units, blocks, mod))
            units += mod
            blocks += 2
            add("gggmgmgmgmgg" if mod else "g" * 8)
            if rest and i == 0:
                ph.rest = count["g"]
                add("g")
        add("g" * single)
    return order, phases


ORDER, PH = plan()
RAW_OF = {m: n for n, (kind, m) in enumerate(ORDER) if kind == "g"}
RAW_OF_MOD = {k: n for n, (kind, k) in enumerate(ORDER) if kind == "m"}


def raw_stride(pair):
    return 16 * (8 if pair.unit is None else 12) // RAW_SLOTS


def pair_items(pair):
    return [(n, *ORDER[n]) for n in range(pair.n0, pair.n0 + (8 if pair.unit is None else 12))]


def two_blocks(nc, consts, x_in, out, w):
    with ExitStack() as ctx:
        def sb(name, shape, dt=F32):
            return ctx.enter_context(nc.sbuf_tensor(name, shape, dt))

        sems = {}

        def sem(name):
            if name not in sems:
                sems[name] = ctx.enter_context(nc.semaphore(name))
            return sems[name]

        raw = sb("raw", [P, RAW_SLOTS, CHUNK_EL])
        w_hi = sb("w_hi", [P, HL_SLOTS, HALF], F32R)
        w_lo = sb("w_lo", [P, HL_SLOTS, HALF], F32R)
        x = sb("x", [P, TT, D])
        a_hi = sb("a_hi", [P, KT, S], F32R)
        a_lo = sb("a_lo", [P, KT, S], F32R)
        con = sb("con", [P, C_N])
        col = sb("col", [P, 9, P])
        modc = sb("modc", [P, 96])
        mod_acc = sb("mod_acc", [P, BLOCK])
        small = sb("small", [P, 288])
        REGION = 24576
        region = sb("region", [P, REGION])
        ps = ctx.enter_context(nc.psum_tensor("ps", [P, 4096], F32))

        def reg(at, n):
            return region[:, at:at + n]

        def main(g):
            return ps[:, 1024 * g:1024 * (g + 1)]

        SIDE = 2048

        def side(b, n=512):
            return ps[:, SIDE + 512 * b:SIDE + 512 * b + n]

        ident = con[:, C_ID:C_ID + P]
        ones = con[:, C_ONE:C_ONE + P]
        tri = con[:, C_TRI:C_TRI + P]

        def colA(r, n=1):
            return col[:, 0, r:r + n]

        def colB(r, n=1):
            return col[:, 1, r:r + n]

        def sm(at, n=1):
            return small[:, at:at + n]
        SS, MS, SD, RSTD = 0, 8, 16, 24
        C_ACT, SCALE_M, SCALE_F = 32, 48, 64
        QK_SS, QK_SD = 80, 112
        MX, NMX, RSUM, RINV = 144, 152, 160, 168
        E_LAST = 176
        O_SS, O_SD = 192, 200
        P_SS, P_SD, P_RSTD = 264, 272, 276
        GP = 216
        WIDX = 232

        hn = reg(0, 4096).rearrange("p (t d) -> p t d", t=TT)
        xt = reg(4096, 4096).rearrange("p (k s) -> p k s", k=KT)
        stage = reg(8192, 9 * P).rearrange("p (n d) -> p n d", n=9)
        z = reg(0, 12288).rearrange("p (b n) -> p b n", b=12)

        def zw(b):
            return region[:, 1024 * b:1024 * b + 2048].rearrange("p (f s) -> p f s", f=8)

        pool_w = reg(12288, 2048).rearrange("p (g c d) -> p g c d", g=4, c=2)
        kT = reg(14336, 2048).rearrange("p (h s) -> p h s", h=HEADS)
        qT = reg(16384, 2048).rearrange("p (h s) -> p h s", h=HEADS)
        kidx2 = reg(18432, 256).rearrange("p (t c d) -> p t c d", t=TT, c=2)
        kidxT = reg(18688, 256)
        relu_buf = reg(18944, 1024).rearrange("p (b j s) -> p b j s", b=2, j=2)
        sc_buf = reg(18944, 2048).rearrange("p (b n) -> p b n", b=2)
        iscore = reg(21024, 512).rearrange("p (t s) -> p t s", t=TT)
        work = reg(21536, 512).rearrange("p (t s) -> p t s", t=TT)
        top8 = reg(22048, 128).rearrange("p (n e) -> p n e", e=8)
        notsel = reg(22176, 512).rearrange("p (t s) -> p t s", t=TT)
        win = [reg(22688 + 512 * n, 512).rearrange("p (f s) -> p f s", f=2) for n in range(2)]
        pT = [reg(0, 512), reg(512, 512), reg(1024, 1024), reg(21024, 1024)]
        dT = zw(2)
        yT_attn = zw(4)
        yT_pool = zw(6)
        A1, A2, A3, A4, A5, A6 = (12288 + 1024 * n for n in range(6))
        A7 = 23552

        def head_tok(at):
            return reg(at, 1024).rearrange("p (h s) -> p h s", h=GLA_HEADS)
        q_ex = reg(18432, 1536).rearrange("p (h c s) -> p h c s", h=GLA_HEADS, c=3)
        states = reg(19968, 3072).rearrange("p (c h e) -> p c h e", c=3, h=GLA_HEADS)
        a_lr = reg(19968, 32).rearrange("p (t r) -> p t r", t=TT)
        a_lrT = region[0:GATE_RANK, 20224:20224 + S]
        gate_w2 = region[0:GATE_RANK, 23040:23040 + 512]
        o_gla = reg(A2, 2048).rearrange("p (t h e) -> p t h e", t=TT, h=GLA_HEADS)
        yT_gla = zw(0)
        cc, cx, cb = zw(6), zw(8), zw(10)
        yT_conv = cb
        q_lvl_at = (A2, A7)
        g = reg(0, FT * S).rearrange("p (f s) -> p f s", f=FT)
        c_gate = reg(11264, 1024).rearrange("p (f s) -> p f s", f=4)
        c_val = reg(12288, 1024).rearrange("p (f s) -> p f s", f=4)
        y = reg(12288, 4096).rearrange("p (t d) -> p t d", t=TT)
        diag = reg(16384, 2048).rearrange("p (k f) -> p k f", k=KT)
        g_row = reg(22528, 2048)

        raw_full = [sem(f"raw_full{s}") for s in range(RAW_SLOTS)]
        hi_ready = sem("hi_ready")
        lo_ready = sem("lo_ready")
        w_used = sem("w_used")
        mod_step = sem("mod_step")
        mod_red = sem("mod_red")
        epi_done = sem("epi_done")
        act_hi = sem("act_hi")
        act_ready = sem("act_ready")

        RUNS = {
            "in1": [(0, 1, "W"), (1, 2, "T"), (2, 3, "T"), (3, 4, "W"), (4, 5, "T")],
            "out1": [(0, 1, "T"), (1, 2, "T")],
            "up1": [(0, 1, "W"), (1, 11, "W")],
            "in2": [(0, 1, "W"), (1, 2, "T"), (2, 3, "T"), (3, 4, "W"), (4, 5, "W"), (5, 6, "W")],
            "out2": [(0, 1, "T"), (1, 2, "T")],
            "up2": [(0, 1, "W"), (1, 4, "W"), (4, 5, "W"), (5, 11, "W")],
        }
        FILL = {"in1": 0, "out1": 1, "up1": 2, "in2": 3, "out2": 4, "up2": 5}

        def run_pairs(eng, name, body):
            for a, b, layout in RUNS[name]:
                if b - a == 1:
                    body(a, a, 0, layout)
                else:
                    with eng.Fori(a, b) as i:
                        body(a, i, i - a, layout)

        def block_end(ph, i0, blk):
            return 2 * (ph.pairs[i0].m0 + 4 * (blk + 1))

        def blocks_before(name):
            return PH[name].pairs[0].b0

        def down_end(name):
            return 2 * (PH[name].m0 + FT)

        block = ctx.enter_context(nc.Block())

        @block.sync
        def _(sp):
            def slot_free(n, r=0, stride=16):
                if n < RAW_SLOTS:
                    return
                kind, at = ORDER[n - RAW_SLOTS]
                if kind == "g":
                    sp.wait_ge(lo_ready, 2 * (at + 1) + r * stride)
                else:
                    sp.wait_ge(mod_step, 4 * (at + 1) + r * stride)

            def settled(value):
                return value if type(value) is int else sp.snap(value)

            def rest(name, wt, c0, cols):
                n = RAW_OF[PH[name].rest]
                slot_free(n)
                with nc.allow_non_contiguous_dma(reason="the last few columns of w_in"):
                    sp.dma_start(raw[:, n % RAW_SLOTS, 0:KT * cols].rearrange("p (k n) -> p k n", k=KT),
                                 wt[:, c0:c0 + cols].rearrange("(k p) n -> p k n", p=P)).then_inc(raw_full[n % RAW_SLOTS], 16)

            def pairs(name, wt, column, step=0, narrow=None):
                ph = PH[name]

                def body(i0, i, r, layout):
                    pair = ph.pairs[i0]
                    for n, kind, at in pair_items(pair):
                        if kind == "g":
                            blk, c = divmod(at - pair.m0, 4)
                            src = wt[c * KC * P:(c + 1) * KC * P, bass.ds(settled(column(i0, blk) + step * r), BLOCK)]
                        else:
                            c = at % 4
                            src = w["w_mod_2"][c * KC * P:(c + 1) * KC * P, bass.ds(settled(pair.unit * BLOCK + r * BLOCK), BLOCK)]
                        slot_free(n, r)
                        sp.dma_start(raw[:, n % RAW_SLOTS, :].rearrange("p (k n) -> p k n", k=KC),
                                     src.rearrange("(k p) n -> p k n", p=P)).then_inc(raw_full[n % RAW_SLOTS], 16)
                    if narrow and i0 == 0:
                        rest(name, wt, *narrow)

                run_pairs(sp, name, body)

            def down(name, wt):
                ph = PH[name]

                def load(j, kt, r):
                    n = ph.n0 + j
                    src = wt[bass.ds(settled(kt * P), P), :]
                    slot_free(n, r, 8)
                    sp.dma_start(raw[:, n % RAW_SLOTS, :], src).then_inc(raw_full[n % RAW_SLOTS], 16)

                for j in range(4):
                    load(j, j, 0)
                with sp.Fori(1, FT // 4) as i:
                    for j in range(4):
                        load(4 + j, i * 4 + j, i - 1)

            for t in range(TT):
                sp.dma_start(x[:, t, :], x_in[t * P:(t + 1) * P, :]).then_inc(sem(f"x_loaded{t}"), 16)
            pairs("in1", w["w_in"], lambda i, blk: IN1_STARTS[i] + BLOCK * blk, narrow=(IN1_REST, IDX_REST))
            pairs("out1", w["w_out"], lambda i, blk: 1024 * i + BLOCK * blk)
            pairs("up1", w["w_up"], lambda i, blk: BLOCK * i + F * blk, BLOCK)
            down("down1", w["w_down"])
            pairs("in2", w["w_in_2"], lambda i, blk: IN2_STARTS[i] + BLOCK * blk, narrow=(IN2_REST, GATE_RANK))
            pairs("out2", w["w_out_2"], lambda i, blk: 1024 * i + BLOCK * blk)
            pairs("up2", w["w_up_2"], lambda i, blk: BLOCK * i + F * blk, BLOCK)
            down("down2", w["w_down_2"])
            for t in range(TT):
                sp.wait_ge(sem("x_new"), 5 + t)
                sp.dma_start(out[t * P:(t + 1) * P, :], x[:, t, :]).then_inc(sem("stored"), 16)
            sp.wait_ge(sem("stored"), 16 * TT)

        @block.scalar
        def _(act):
            seq = [0]

            def link(ins):
                seq[0] += 1
                ins.then_inc(sem("act_step"), 1)
                act.wait_ge(sem("act_step"), seq[0])

            def round_half(m, half, r=0, stride=16, raw_add=0, n_el=HALF):
                n, hh = RAW_OF[m], 2 * m + half
                if half == 0:
                    act.wait_ge(raw_full[n % RAW_SLOTS], 16 * (n // RAW_SLOTS + 1) + r * raw_add)
                if hh >= HL_SLOTS:
                    act.wait_ge(w_used, hh - HL_SLOTS + 1 + r * stride)
                nc.scalar.activation(w_hi[:, hh % HL_SLOTS, 0:n_el], raw[:, n % RAW_SLOTS, half * n_el:(half + 1) * n_el],
                                     ACT.Copy).then_inc(hi_ready, 1)

            def rest_rounds(name, cols):
                for half in range(2):
                    round_half(PH[name].rest, half, n_el=KT * cols // 2)

            def lead(name):
                for c in range(2):
                    for half in range(2):
                        round_half(PH[name].m0 + c, half)

            def pairs(name, epi, narrow=0, between=None, late=None):
                ph = PH[name]

                def body(i0, i, r, layout):
                    pair = ph.pairs[i0]
                    for c in range(8):
                        if i0 > 0 or c >= 2:
                            for half in range(2):
                                round_half(pair.m0 + c, half, r, 16, raw_stride(pair))
                        if c == 1 and i0 > 0:
                            epi(ph, 1, i0 - 1, i - 1, r)
                        if c == 5:
                            epi(ph, 0, i0, i, r)
                        if between:
                            between(8 * i0 + c)
                    if late:
                        late(ph, i0, r)
                    if narrow and i0 == 0:
                        rest_rounds(name, narrow)

                run_pairs(act, name, body)

            def last_epi(name, epi):
                i = RUNS[name][-1][1] - 1
                epi(PH[name], 1, i, i, 0)

            def norm_sums(p):
                if p == 0:
                    act.wait_ge(sem("x_loaded0"), 16)
                elif p == 1:
                    act.wait_ge(epi_done, blocks_before("up1"))
                else:
                    act.wait_ge(sem("x_new"), 2 * (p - 2) + 1)
                nc.scalar.activation(xt.rearrange("p k s -> p (k s)")[:, 0:D], x[:, 0, :], ACT.Square,
                                     accum_out=sm(SS + 2 * p)).then_inc(sem("sq_done"), 1)

            def norm(p):
                act.wait_ge(sem("ms_ready"), p + 1)
                nc.scalar.activation(sm(SD + 2 * p, 2), sm(MS + 2 * p, 2), ACT.Sqrt).then_inc(sem("sd_ready"), 1)
                act.wait_ge(sem("rstd_ready"), p + 1)
                nc.scalar.activation(hn[:, 1, :], x[:, 1, :], ACT.Copy, scale=sm(RSTD + 2 * p + 1)).then_inc(sem("hn_act"), 1)
                for k in range(KT // 2):
                    act.wait_ge(sem("xt_ready"), KT * p + 2 * k + 2)
                    nc.scalar.activation(a_hi[:, 2 * k:2 * k + 2, :], xt[:, 2 * k:2 * k + 2, :], ACT.Copy).then_inc(act_hi, 1)

            def split_mixed(first, second, waits):
                for k, src in [(k, first[:, 2 * k:2 * k + 2, :]) for k in range(4)] + [(k + 4, second[:, 2 * k:2 * k + 2, :]) for k in range(4)]:
                    if k in waits:
                        act.wait_ge(*waits[k])
                    nc.scalar.activation(a_hi[:, 2 * k:2 * k + 2, :], src, ACT.Copy).then_inc(act_hi, 1)

            def epi_z(ph, blk, i0, i, r):
                act.wait_ge(w_used, block_end(ph, i0, blk) + 16 * r)
                nc.scalar.activation(z[:, bass.ds(2 * i + blk, 1), :].rearrange("p b n -> p (b n)"), main(blk), ACT.Copy).then_inc(epi_done, 1)

            def epi_none(ph, blk, i0, i, r):
                pass

            def epi_conv(layer, q):
                def epi(ph, blk, i0, i, r):
                    dst = (c_gate, c_val)[blk]
                    act.wait_ge(w_used, block_end(ph, i0, blk) + 16 * r)
                    if q + i0 > 0 or i0 > 0:
                        act.wait_ge(sem("g_done"), q * 11 + i0 + r)
                    last = 2 if layer == 1 else 6
                    for f in range(4):
                        tap = col[:, last, bass.ds(4 * i + f + FT * blk, 1)]
                        bias = col[:, 3, bass.ds(4 * i + f + FT * blk, 1)] if layer == 1 else 0.0
                        nc.scalar.activation(dst[:, f, :], main(blk)[:, S * f:S * (f + 1)], ACT.Identity, bias=bias,
                                             scale=tap).then_inc(sem("conv_first"), 1)
                return epi

            def gate_silu(ph, i0, r):
                act.wait_ge(epi_done, ph.pairs[i0].b0 + 1 + 2 * r)
                nc.scalar.activation(c_gate, c_gate, ACT.Silu).then_inc(sem("silu_done"), 1)

            def down(name, q, epi_prev):
                ph = PH[name]

                def split_g(j, kt, r):
                    nc.scalar.activation(a_hi[:, j % 4, :], g[:, bass.ds(kt, 1), :].rearrange("p f s -> p (f s)"),
                                         ACT.Copy).then_inc(sem("g_hi"), 1)

                epi_prev()
                act.wait_ge(sem("g_done"), 11 * (q + 1))
                for j in range(4):
                    split_g(j, j, 0)
                    if j >= 2:
                        for half in range(2):
                            round_half(ph.m0 + j, half)
                with act.Fori(1, FT // 4) as i:
                    for j in range(4):
                        act.wait_ge(w_used, 2 * (ph.m0 + j + 1) + 8 * (i - 1))
                        split_g(j, i * 4 + j, i - 1)
                        for half in range(2):
                            round_half(ph.m0 + 4 + j, half, i - 1, 8, 16)

            loads = [(con[:], consts)]
            for name, r in (("attn_norm_g", A_ATTN), ("ffn_norm_g", A_FFN), ("pool_scale", A_PSC), ("mix_pre_w_2", A_MPRE),
                            ("ffn_pre_w_2", A_FPRE), ("mix_post_w_2", A_MPOST), ("gate_b_2", A_GB), ("q_norm_g", A_QG),
                            ("k_norm_g", A_KG), ("gla_norm_w_2", A_GLA)):
                v = w[name].rearrange("(r p) -> r p", p=P)
                loads.append((stage[r:r + v.shape[0], 0, :], v))
            loads.append((stage[A_CW:A_CW + 24, 0, :], w["conv_w_2"].rearrange("j (r p) -> (j r) p", p=P)))
            assert len(loads) == N_FIRST
            for dst, src in loads:
                act.dma_start(dst, src).then_inc(sem("first_params"), 16)
            loads = []
            for name, r in (("b_mod_2", B_MOD), ("c_2", B_C), ("ffn_post_w_2", B_FPOST)):
                v = w[name].rearrange("(r p) -> r p", p=P)
                loads.append((stage[r:r + v.shape[0], 1, :], v))
            for j in range(3):
                loads.append((stage[0:CONV_ROWS, (4, 5, 2)[j], :], w["conv_w"][j].rearrange("(r p) -> r p", p=P)))
            loads.append((stage[0:CONV_ROWS, 3, :], w["conv_b"].rearrange("(r p) -> r p", p=P)))
            for j in range(3):
                loads.append((stage[0:CONV_ROWS, (7, 8, 6)[j], :], w["ffn_conv_w_2"][j].rearrange("(r p) -> r p", p=P)))
            assert len(loads) == N_SECOND
            for dst, src in loads:
                act.dma_start(dst, src).then_inc(sem("second_params"), 16)

            norm_sums(0)
            act.wait_ge(sem("cols_turned"), 1)
            nc.scalar.activation(col[:, 0, 0:A_ROWS], ps[:, SIDE:SIDE + A_ROWS], ACT.Copy).then_inc(sem("cols_ready"), 1)
            norm(0)
            lead("in1")
            act.dma_start(pool_w, w["pool_w"].rearrange("g (c p) d -> p g c d", p=P)).then_inc(sem("pool_w_loaded"), 16)
            act.wait_ge(sem("cols_turned"), 2)
            nc.scalar.activation(col[:, 1, :], side(0, P), ACT.Copy).then_inc(sem("cols_ready"), 1)
            nc.scalar.activation(col[:, 2:9, 0:CONV_ROWS],
                                 ps[:, SIDE + P:SIDE + 8 * P].rearrange("p (n r) -> p n r", n=7)[:, :, 0:CONV_ROWS],
                                 ACT.Copy).then_inc(sem("cols_ready"), 1)
            act.wait_ge(sem("cols_ready"), 3)
            nc.scalar.activation(sm(C_ACT, KT), colB(B_C, KT), ACT.Silu).then_inc(sem("c_act"), 1)

            def rest1_out():
                act.wait_ge(w_used, 2 * (PH["in1"].rest + 1))
                for t in range(TT):
                    nc.scalar.activation(kidx2[:, t, :, :], side(t, IDX_DIM).unsqueeze(1).to_broadcast([P, 2, IDX_DIM]),
                                         ACT.Copy).then_inc(sem("kidx_out"), 1)
                    nc.scalar.activation(sm(WIDX + IDX_HEADS * t, IDX_HEADS), side(t, IDX_REST)[:, IDX_DIM:IDX_REST], ACT.Copy,
                                         scale=IDX_HEADS ** -0.5 * IDX_DIM ** -0.5).then_inc(sem("kidx_out"), 1)

            def rectify(n):
                K = P * (n // 8 + 1)
                act.wait_ge(sem("is_done"), n + 1)
                if n >= 2:
                    act.wait_ge(sem("relu_used"), n - 1)
                nc.scalar.activation(relu_buf[:, n % 2, :, 0:K], side(n % 3).rearrange("p (j s) -> p j s", j=2)[:, :, 0:K],
                                     ACT.Relu).then_inc(sem("relu_ready"), 1)

            def qk_out(n):
                dst, wcol = ((kT, colA(A_KG)), (qT, colA(A_QG)))[n // 4]
                b, t = divmod(n % 4, 2)
                act.wait_ge(sem("qk_turned"), n + 1)
                nc.scalar.activation(dst[:, 4 * b:4 * b + 4, t * P:(t + 1) * P], side(n % 3).rearrange("p (h s) -> p h s", h=4),
                                     ACT.Copy, scale=wcol).then_inc(sem("qkT_ready"), 1)

            def soft_exp(u):
                K = P * (u // 2 + 1)
                s = sc_buf[:, u % 2, 0:4 * K]
                act.wait_ge(sem("sm_ready"), u + 1)
                nc.scalar.activation(s, s, ACT.Exp, scale=HD ** -0.5).then_inc(sem("p_exp"), 1)

            def probs_out(u):
                act.wait_ge(sem("p_turned"), u + 1)
                at = SIDE + 512 * (u % 2 if u < 2 else 0)
                nc.scalar.activation(pT[u], ps[:, at:at + 512 * (u // 2 + 1)], ACT.Copy).then_inc(sem("pT_ready"), 1)

            def attn_out(u):
                t, hg = divmod(u, 2)
                act.wait_ge(sem("pv_done"), u + 1)
                nc.scalar.activation(yT_attn[:, 4 * hg:4 * hg + 4, t * P:(t + 1) * P], side(2).rearrange("p (h s) -> p h s", h=4),
                                     ACT.Copy).then_inc(sem("yT_attn_ready"), 1)

            def pool_out(e):
                act.wait_ge(sem("pool_mixed"), e + 1)
                for f in (2 * e, 2 * e + 1):
                    nc.scalar.activation(yT_pool[:, f, :], side(3)[:, S * (f % 2):S * (f % 2 + 1)], ACT.Copy,
                                         scale=colA(A_PSC + f)).then_inc(sem("yT_pool_ready"), 1)

            def mixer1(at):
                if at == 10:
                    rest1_out()
                if at == 12:
                    act.wait_ge(sem("kidx_turned"), 1)
                    nc.scalar.activation(kidxT, side(2, 256), ACT.Copy).then_inc(sem("kidxT_ready"), 1)
                if 13 <= at < 21:
                    rectify(2 * (at - 13))
                    rectify(2 * (at - 13) + 1)
                if at in (22, 26):
                    n = (at - 22) // 4
                    act.wait_ge(epi_done, 4 + 2 * n)
                    nc.scalar.activation((kT, qT)[n].rearrange("p h s -> p (h s)"), reg(2048 + 2048 * n, 2048),
                                         ACT.Square).then_inc(sem("qk_sq"), 1)
                if at == 29:
                    act.wait_ge(sem("qk_ms"), 1)
                    nc.scalar.activation(sm(QK_SD, 32), sm(QK_SS, 32), ACT.Sqrt).then_inc(sem("qk_sd"), 1)
                if 34 <= at < 38:
                    qk_out(2 * (at - 34))
                    qk_out(2 * (at - 34) + 1)
                if at == 39:
                    soft_exp(0)

            pairs("in1", epi_z, IDX_REST, mixer1)
            lead("out1")
            last_epi("in1", epi_z)
            soft_exp(1)
            probs_out(0)
            probs_out(1)
            pool_out(0)
            soft_exp(2)
            attn_out(0)
            pool_out(1)
            attn_out(1)
            probs_out(2)
            pool_out(2)
            soft_exp(3)
            attn_out(2)
            pool_out(3)
            probs_out(3)
            attn_out(3)
            split_mixed(yT_pool, yT_attn, {0: (sem("yT_pool_ready"), 8), 4: (sem("yT_attn_ready"), 4)})

            pairs("out1", epi_none)
            lead("up1")
            norm_sums(1)
            norm(1)
            pairs("up1", epi_conv(1, 0), late=gate_silu)
            lead("down1")
            down("down1", 0, lambda: last_epi("up1", epi_conv(1, 0)))

            lead("in2")
            act.dma_start(gate_w2, w["gate_w2_2"]).then_inc(sem("gate_loaded"), 16)
            norm_sums(2)
            norm(2)
            xg, ta = head_tok(A1), head_tok(A2)
            r_gate = reg(4096, 2048)

            def mixer2(at):
                if at == 10:
                    act.wait_ge(w_used, 2 * (PH["in2"].rest + 1))
                    for t in range(TT):
                        nc.scalar.activation(a_lr[:, t, :], side(t, GATE_RANK), ACT.Copy).then_inc(sem("alr_out"), 1)
                if at == 12:
                    act.wait_ge(sem("alr_turned"), 1)
                    nc.scalar.activation(a_lrT, ps[0:GATE_RANK, SIDE + 1024:SIDE + 1024 + S], ACT.Copy).then_inc(sem("alrT_ready"), 1)
                if at == 14:
                    act.wait_ge(sem("gate_mm"), 1)
                    for h in range(GLA_HEADS):
                        nc.scalar.activation(xg[:, h, :], ps[:, SIDE + S * h:SIDE + S * (h + 1)], ACT.Identity,
                                             bias=colA(A_GB + h)).then_inc(sem("xg_ready"), 1)
                if at == 15:
                    act.wait_ge(sem("xg_ready"), 4)
                    link(nc.scalar.activation(ta, xg, ACT.Abs))
                    link(nc.scalar.activation(ta, ta, ACT.Exp, scale=-1.0))
                    nc.scalar.activation(ta, ta, ACT.Ln, bias=ones[:, 0:1]).then_inc(sem("ln_ready"), 1)
                if at == 18:
                    act.wait_ge(sem("b_ready"), 1)
                    nc.scalar.activation(head_tok(A1), head_tok(A4), ACT.Exp).then_inc(sem("eb_ready"), 1)
                    nc.scalar.activation(sm(E_LAST, 16), reg(A4, 1024).rearrange("p (c s) -> p c s", s=CHUNK)[:, :, CHUNK - 1],
                                         ACT.Exp).then_inc(sem("e_last"), 1)
                if at == 19:
                    act.wait_ge(sem("kd_diff"), 1)
                    nc.scalar.activation(reg(A3, 1024), reg(A3, 1024), ACT.Exp, scale=-1.0).then_inc(sem("kd_exp"), 1)
                if at == 22:
                    act.wait_ge(sem("kd_turned"), 1)
                    nc.scalar.activation(reg(A6, 1024), ps[:, SIDE:SIDE + 1024], ACT.Copy).then_inc(sem("kdT_ready"), 1)
                if at >= 24 and at % 2 == 0 and (at - 24) // 2 < len(LEVELS):
                    act.wait_ge(sem("lvl_diff"), (at - 24) // 2 + 1)
                    link(nc.scalar.activation(reg(A1, 1024), reg(A1, 1024), ACT.Abs))
                    nc.scalar.activation(reg(A1, 1024), reg(A1, 1024), ACT.Exp, scale=-1.0).then_inc(sem("lvl_exp"), 1)
                if at == 37:
                    act.wait_ge(epi_done, blocks_before("in2") + 6)
                    nc.scalar.activation(r_gate, r_gate, ACT.Silu).then_inc(sem("r_silu"), 1)
                if at in (39, 43):
                    b = (at - 39) // 4
                    act.wait_ge(sem("ccx_ready"), b + 1)
                    for f in range(4 * b, 4 * b + 4):
                        nc.scalar.activation(cx[:, f, :], cc[:, f, :], ACT.Copy, scale=colA(A_CW + 16 + f)).then_inc(sem("mix_tap"), 1)
                if at == 41:
                    act.wait_ge(sem("o_done"), 1)
                    nc.scalar.activation(o_gla.rearrange("p t h e -> p (t h e)"), ps[:, SIDE:SIDE + 2048], ACT.Copy).then_inc(sem("o_out"), 1)
                    act.wait_ge(sem("o_out"), 1)
                    nc.scalar.activation(reg(A4, 2048), o_gla.rearrange("p t h e -> p (t h e)"), ACT.Square).then_inc(sem("o_sq"), 1)
                if at == 44:
                    act.wait_ge(sem("o_ms"), 1)
                    nc.scalar.activation(sm(O_SD, 8), sm(O_SS, 8), ACT.Sqrt).then_inc(sem("o_sd"), 1)
                if at == 47:
                    act.wait_ge(sem("o_turned"), 1)
                    for f in range(8):
                        nc.scalar.activation(yT_gla[:, f, :], ps[:, SIDE + S * f:SIDE + S * (f + 1)], ACT.Copy,
                                             scale=colA(A_GLA + f % 2)).then_inc(sem("yT_gla_ready"), 1)

            pairs("in2", epi_z, GATE_RANK, mixer2)
            lead("out2")
            last_epi("in2", epi_z)
            split_mixed(yT_conv, yT_gla, {0: (sem("yT_conv_ready"), 1), 2: (sem("yT_conv_ready"), 2), 4: (sem("yT_gla_ready"), 8)})

            def gate_row(q):
                act.wait_ge(sem("row_mm"), q + 1)
                nc.scalar.activation(g_row, ps[:, SIDE:SIDE + 2048], ACT.Copy).then_inc(sem("row_ready"), 1)

            def post_sd(q):
                act.wait_ge(sem("post_ms"), q + 1)
                nc.scalar.activation(sm(P_SD + 2 * q, 2), sm(P_SS, 2), ACT.Sqrt).then_inc(sem("post_sd"), 1)

            def epi_sums(ph, blk, i0, i, r):
                act.wait_ge(w_used, block_end(ph, i0, blk))
                j = 2 * i0 + blk
                for t in range(TT):
                    nc.scalar.activation(xt.rearrange("p k s -> p (k s)")[:, BLOCK * (2 * j + t):BLOCK * (2 * j + t + 1)],
                                         main(blk)[:, BLOCK * t:BLOCK * (t + 1)], ACT.Square,
                                         accum_out=sm(P_SS + 4 * t + j)).then_inc(sem("post_sq"), 1)

            gate_row(0)
            pairs("out2", epi_sums)
            lead("up2")
            last_epi("out2", epi_sums)
            post_sd(0)
            norm_sums(3)
            norm(3)

            def last_row(at):
                if at == 39:
                    gate_row(1)

            pairs("up2", epi_conv(2, 1), between=last_row, late=gate_silu)
            lead("down2")
            down("down2", 1, lambda: last_epi("up2", epi_conv(2, 1)))
            act.wait_ge(w_used, down_end("down2"))
            for t in range(TT):
                if t:
                    act.wait_ge(sem("yg_ready"), 1)
                nc.scalar.activation(xt.rearrange("p k s -> p (k s)")[:, t * D:(t + 1) * D], ps[:, D * t:D * (t + 1)], ACT.Square,
                                     accum_out=sm(P_SS + 4 * t)).then_inc(sem("post_sq"), 1)
            post_sd(1)

        @block.vector
        def _(dve):
            v = nc.vector
            seq = [0]

            def link(ins):
                seq[0] += 1
                ins.then_inc(sem("dve_step"), 1)
                dve.wait_ge(sem("dve_step"), seq[0])

            def low_half(m, half, r=0, stride=16, n_el=HALF):
                n, hh = RAW_OF[m], 2 * m + half
                dve.wait_ge(hi_ready, hh + 1 + r * stride)
                v.tensor_tensor(w_lo[:, hh % HL_SLOTS, 0:n_el], raw[:, n % RAW_SLOTS, half * n_el:(half + 1) * n_el],
                                w_hi[:, hh % HL_SLOTS, 0:n_el].bitcast(F32), ALU.subtract).then_inc(lo_ready, 1)

            def rest_lows(name, cols):
                for half in range(2):
                    low_half(PH[name].rest, half, n_el=KT * cols // 2)

            def lead(name):
                for c in range(2):
                    for half in range(2):
                        low_half(PH[name].m0 + c, half)

            def mod_chunk(pair, k, r):
                n, c = RAW_OF_MOD[k], k % 4
                dve.wait_ge(raw_full[n % RAW_SLOTS], 16 * (n // RAW_SLOTS + 1) + r * raw_stride(pair))
                part = raw[:, n % RAW_SLOTS, :].rearrange("p (k n) -> p k n", k=KC)
                for kk in range(KC):
                    kt = KC * c + kk
                    step = UNIT_OPS * (k // 4) + kt
                    if kt == 0:
                        v.tensor_scalar(mod_acc[:], part[:, 0, :], sm(C_ACT), None, ALU.mult).then_inc(mod_step, 1)
                    else:
                        dve.wait_ge(mod_step, step + r * UNIT_OPS)
                        v.scalar_tensor_tensor(out=mod_acc[:], in0=part[:, kk, :], scalar=sm(C_ACT + kt), in1=mod_acc[:],
                                               op0=ALU.mult, op1=ALU.add).then_inc(mod_step, 1)

            def mod_columns(u):
                dve.wait_ge(mod_red, u + 1)
                v.tensor_tensor(modc[:, bass.ds(u * 4, 4)], side(3)[:, 508:512], col[:, 1, bass.ds(u * 4 + B_MOD, 4)],
                                ALU.add).then_inc(sem("modc_ready"), 1)

            def pairs(name, epi, narrow=0, between=None):
                ph = PH[name]

                def body(i0, i, r, layout):
                    pair = ph.pairs[i0]
                    for n, kind, at in pair_items(pair):
                        if kind == "m":
                            mod_chunk(pair, at, r)
                            continue
                        c = at - pair.m0
                        if i0 > 0 or c >= 2:
                            for half in range(2):
                                low_half(at, half, r)
                        if c == 2 and i0 > 0:
                            if ph.pairs[i0 - 1].unit is not None:
                                mod_columns(ph.pairs[i0 - 1].unit + r)
                            epi(ph, 1, i0 - 1, i - 1, r)
                        if c == 6:
                            epi(ph, 0, i0, i, r)
                        if between:
                            between(8 * i0 + c)
                    if narrow and i0 == 0:
                        rest_lows(name, narrow)

                run_pairs(dve, name, body)

            def last_epi(name, epi):
                i = RUNS[name][-1][1] - 1
                epi(PH[name], 1, i, i, 0)

            def last_unit(name):
                mod_columns(PH[name].pairs[-1].unit)

            def norm_sums(p):
                if p == 0:
                    dve.wait_ge(sem("x_loaded1"), 16)
                elif p == 1:
                    dve.wait_ge(epi_done, blocks_before("up1"))
                else:
                    dve.wait_ge(sem("x_new"), 2 * (p - 1))
                v.scalar_tensor_tensor(out=xt.rearrange("p k s -> p (k s)")[:, D:2 * D], in0=x[:, 1, :], scalar=1.0, in1=x[:, 1, :],
                                       op0=ALU.mult, op1=ALU.mult, accum_out=sm(SS + 2 * p + 1)).then_inc(sem("sq_done"), 1)
                dve.wait_ge(sem("sq_done"), 2 * p + 2)
                v.tensor_scalar(sm(MS + 2 * p, 2), sm(SS + 2 * p, 2), 1.0 / D, EPS, ALU.mult, ALU.add).then_inc(sem("ms_ready"), 1)

            def norm(p, f, scale, shift=None):
                dve.wait_ge(sem("sd_ready"), p + 1)
                v.reciprocal(sm(RSTD + 2 * p, 2), sm(SD + 2 * p, 2)).then_inc(sem("rstd_ready"), 1)
                dve.wait_ge(sem("rstd_ready"), p + 1)
                v.tensor_scalar(hn[:, 0, :], x[:, 0, :], sm(RSTD + 2 * p), None, ALU.mult).then_inc(sem("hn_dve"), 1)

                def lows(k):
                    dve.wait_ge(act_hi, 8 * f + k + 1)
                    v.tensor_tensor(a_lo[:, 2 * k:2 * k + 2, :], xt[:, 2 * k:2 * k + 2, :],
                                    a_hi[:, 2 * k:2 * k + 2, :].bitcast(F32), ALU.subtract).then_inc(act_ready, 1)

                for k in range(KT // 2):
                    dve.wait_ge(sem("turned"), 8 * p + k + 1)
                    for kk in range(2):
                        kt = 2 * k + kk
                        add = (None, ALU.bypass) if shift is None else (shift[:, kt:kt + 1], ALU.add)
                        v.tensor_scalar(xt[:, kt, :], side(k % 4)[:, S * kk:S * (kk + 1)], scale[:, kt:kt + 1], add[0],
                                        ALU.mult, add[1]).then_inc(sem("xt_ready"), 1)
                    if k:
                        lows(k - 1)
                lows(KT // 2 - 1)

            def split_mixed(f, first, second):
                for k, src in [(k, first[:, 2 * k:2 * k + 2, :]) for k in range(4)] + [(k + 4, second[:, 2 * k:2 * k + 2, :]) for k in range(4)]:
                    dve.wait_ge(act_hi, 8 * f + k + 1)
                    v.tensor_tensor(a_lo[:, 2 * k:2 * k + 2, :], src, a_hi[:, 2 * k:2 * k + 2, :].bitcast(F32),
                                    ALU.subtract).then_inc(act_ready, 1)

            def epi_none(ph, blk, i0, i, r):
                pass

            def epi_residual(ph, blk, i0, i, r):
                dve.wait_ge(w_used, block_end(ph, i0, blk))
                j = 2 * i0 + blk
                xs = x[:, :, BLOCK * j:BLOCK * (j + 1)]
                v.tensor_tensor(xs, main(blk).rearrange("p (t n) -> p t n", t=TT), xs, ALU.add).then_inc(epi_done, 1)

            def epi_conv(layer, q):
                rows = (4, 5) if layer == 1 else (7, 8)

                def epi(ph, blk, i0, i, r):
                    dst = (c_gate, c_val)[blk]
                    n = q * 22 + 2 * i0 + blk
                    dve.wait_ge(sem("conv_first"), 4 * n + 4 + 8 * r)
                    for j, shift in ((1, 1), (0, 2)):
                        if j == 0:
                            dve.wait_ge(sem("conv_second"), 4 * n + 4 + 8 * r)
                        for f in range(4):
                            tap = col[:, rows[j], bass.ds(4 * i + f + FT * blk, 1)]
                            ins = v.scalar_tensor_tensor(
                                out=dst[:, f, shift:], in0=main(blk)[:, S * f:S * (f + 1) - shift], scalar=tap, in1=dst[:, f, shift:],
                                op0=ALU.mult, op1=ALU.add)
                            if j == 1:
                                ins.then_inc(sem("conv_second"), 1)
                            elif f == 3:
                                ins.then_inc(epi_done, 1)
                    if blk == 1:
                        dve.wait_ge(sem("silu_done"), q * 11 + i0 + 1 + r)
                        dve.wait_ge(epi_done, ph.pairs[i0].b0 + 2 + 2 * r)
                        v.tensor_tensor(g[:, bass.ds(4 * i, 4), :], c_gate, c_val, ALU.mult).then_inc(sem("g_done"), 1)
                return epi

            def down(name, q):
                ph = PH[name]

                def split_g(j, kt, r):
                    dve.wait_ge(sem("g_hi"), FT * q + j + 1 + 4 * r)
                    v.tensor_tensor(a_lo[:, j % 4, :], g[:, bass.ds(kt, 1), :].rearrange("p f s -> p (f s)"),
                                    a_hi[:, j % 4, :].bitcast(F32), ALU.subtract).then_inc(sem("g_split"), 1)

                for j in range(4):
                    split_g(j, j, 0)
                    if j >= 2:
                        for half in range(2):
                            low_half(ph.m0 + j, half)
                with dve.Fori(1, FT // 4) as i:
                    for j in range(4):
                        split_g(4 + j, i * 4 + j, i - 1)
                        for half in range(2):
                            low_half(ph.m0 + 4 + j, half, i - 1, 8)

            norm_sums(0)
            dve.wait_ge(sem("cols_ready"), 1)
            norm(0, 0, colA(A_ATTN, KT))
            lead("in1")
            dve.wait_ge(sem("c_act"), 1)

            def index_sum(n):
                t, b = divmod(n, 8)
                K = P * (t + 1)
                dve.wait_ge(sem("relu_ready"), n + 1)
                for j in range(2):
                    h = 4 * (b // 2) + b % 2 + 2 * j
                    wcol = sm(WIDX + IDX_HEADS * t + h)
                    rel = relu_buf[:, n % 2, j, 0:K]
                    if b + j == 0:
                        link(v.tensor_scalar(iscore[:, t, 0:K], rel, wcol, None, ALU.mult))
                        continue
                    ins = v.scalar_tensor_tensor(out=iscore[:, t, 0:K], in0=rel, scalar=wcol, in1=iscore[:, t, 0:K],
                                                 op0=ALU.mult, op1=ALU.add)
                    if j == 0:
                        link(ins)
                    else:
                        ins.then_inc(sem("relu_used"), 1)
                        dve.wait_ge(sem("relu_used"), n + 1)

            def reach(t):
                K = P * (t + 1)
                last = iscore[:, t, t * P:(t + 1) * P]
                link(v.tensor_tensor(last, last, tri, ALU.add))
                link(v.tensor_copy(work[:, t, 0:K], iscore[:, t, 0:K]))

            def best(t, rounds):
                K = P * (t + 1)
                for k in rounds:
                    link(v.max(top8[:, 8 * t + k, :], work[:, t, 0:K]))
                    link(v.match_replace(work[:, t, 0:K], top8[:, 8 * t + k, :], work[:, t, 0:K], NEG))

            def left(t):
                K = P * (t + 1)
                link(v.tensor_tensor(notsel[:, t, 0:K], iscore[:, t, 0:K], work[:, t, 0:K], ALU.is_equal))

            def soft_shift(u):
                t = u // 2
                K = P * (t + 1)
                s = sc_buf[:, u % 2, 0:4 * K].rearrange("p (h s) -> p h s", h=4)
                at = SIDE + 512 * (u % 2 if u < 2 else 0)
                dve.wait_ge(sem("sc_done"), u + 1)
                if u >= 2:
                    dve.wait_ge(sem("p_turned"), u - 1)
                link(v.scalar_tensor_tensor(out=s, in0=notsel[:, t, 0:K].unsqueeze(1).to_broadcast([P, 4, K]), scalar=NEG,
                                            in1=ps[:, at:at + 4 * K].rearrange("p (h s) -> p h s", h=4), op0=ALU.mult, op1=ALU.add))
                link(v.tensor_reduce(sm(MX, 4), s, AX_X, ALU.max))
                v.tensor_tensor(s, s, sm(MX, 4).unsqueeze(2).to_broadcast([P, 4, K]), ALU.subtract).then_inc(sem("sm_ready"), 1)

            def soft_norm(u):
                K = P * (u // 2 + 1)
                s = sc_buf[:, u % 2, 0:4 * K].rearrange("p (h s) -> p h s", h=4)
                dve.wait_ge(sem("p_exp"), u + 1)
                link(v.tensor_reduce(sm(RSUM, 4), s, AX_X, ALU.add))
                link(v.reciprocal(sm(RINV, 4), sm(RSUM, 4)))
                v.tensor_tensor(s, s, sm(RINV, 4).unsqueeze(2).to_broadcast([P, 4, K]), ALU.mult).then_inc(sem("p_ready"), 1)

            def mixer1(at):
                if 14 <= at < 22:
                    index_sum(2 * (at - 14))
                    index_sum(2 * (at - 14) + 1)
                if at == 22:
                    reach(0)
                    best(0, range(3))
                if at == 23:
                    best(0, range(3, 8))
                    left(0)
                if at == 24:
                    reach(1)
                    best(1, range(1))
                if at in (25, 26, 27):
                    best(1, range(1 + 2 * (at - 25), 3 + 2 * (at - 25)))
                if at in (27, 28):
                    n = at - 27
                    dve.wait_ge(sem("qk_sq"), n + 1)
                    src = (kT, qT)[n].rearrange("p h s -> p (h s)").rearrange("p (n d) -> p n d", d=HD)
                    link(v.tensor_reduce(sm(QK_SS + 16 * n, 16), src, AX_X, ALU.add))
                if at == 28:
                    v.tensor_scalar(sm(QK_SS, 32), sm(QK_SS, 32), 1.0 / HD, EPS, ALU.mult, ALU.add).then_inc(sem("qk_ms"), 1)
                if at == 30:
                    dve.wait_ge(sem("qk_sd"), 1)
                    v.reciprocal(sm(QK_SS, 32), sm(QK_SD, 32)).then_inc(sem("qk_rstd"), 1)
                if at == 31:
                    best(1, range(7, 8))
                    left(1)
                if at == 38:
                    soft_shift(0)
                if at == 39:
                    soft_shift(1)

            pairs("in1", epi_none, IDX_REST, mixer1)
            lead("out1")
            soft_norm(0)
            soft_norm(1)
            soft_shift(2)
            soft_norm(2)
            soft_shift(3)
            soft_norm(3)
            split_mixed(1, yT_pool, yT_attn)

            pairs("out1", epi_residual)
            lead("up1")
            last_epi("out1", epi_residual)
            norm_sums(1)
            last_unit("out1")
            norm(1, 2, colA(A_FFN, KT))
            pairs("up1", epi_conv(1, 0))
            lead("down1")
            last_epi("up1", epi_conv(1, 0))
            last_unit("up1")
            down("down1", 0)

            def scales(at, wcols, first):
                dve.wait_ge(sem("modc_ready"), first // 4 + 4)
                link(v.scalar_tensor_tensor(out=sm(at, KT), in0=modc[:, first:first + KT], scalar=1.0, in1=wcols, op0=ALU.add, op1=ALU.mult))

            lead("in2")
            scales(SCALE_M, colA(A_MPRE, KT), 16)
            dve.wait_ge(w_used, down_end("down1"))
            for t in range(TT):
                v.tensor_tensor(x[:, t, :], ps[:, D * t:D * (t + 1)], x[:, t, :], ALU.add).then_inc(sem("x_new"), 1)
            norm_sums(2)
            norm(2, 3, sm(SCALE_M, KT), modc[:, 0:KT])

            xg, ta, bb = head_tok(A1), head_tok(A2), head_tok(A4)
            q, k = head_tok(0), head_tok(1024)
            GS = HD ** -0.5
            bc = reg(A4, 1024).rearrange("p (c s) -> p c s", s=CHUNK)

            def log_decay():
                dve.wait_ge(sem("ln_ready"), 1)
                link(v.scalar_tensor_tensor(out=ta, in0=xg, scalar=0.0, in1=ta, op0=ALU.min, op1=ALU.subtract))
                link(v.tensor_scalar(ta, ta, 1.0 / GATE_TAU, None, ALU.mult))

            def decay_sums():
                for h in range(GLA_HEADS):
                    ins = v.tensor_tensor_scan(bb[:, h, :], con[:, C_RST:C_RST + S], ta[:, h, :], 0.0, ALU.mult, ALU.add)
                    if h < GLA_HEADS - 1:
                        link(ins)
                ins.then_inc(sem("b_ready"), 1)
                dve.wait_ge(sem("b_ready"), 1)
                v.tensor_tensor(reg(A3, 1024).rearrange("p (c s) -> p c s", s=CHUNK), bc,
                                bc[:, :, CHUNK - 1:CHUNK].to_broadcast([P, 16, CHUNK]), ALU.subtract).then_inc(sem("kd_diff"), 1)

            def from_start():
                dve.wait_ge(sem("eb_ready"), 1)
                dve.wait_ge(sem("q_ex_zero"), 1)
                for c in range(1, NCHUNK):
                    at = CHUNK * (c % 2)
                    ins = v.scalar_tensor_tensor(out=q_ex[:, :, c - 1, at:at + CHUNK], in0=q[:, :, CHUNK * c:CHUNK * (c + 1)], scalar=GS,
                                                 in1=head_tok(A1)[:, :, CHUNK * c:CHUNK * (c + 1)], op0=ALU.mult, op1=ALU.mult)
                ins.then_inc(sem("q_ex_ready"), 1)

            def to_end():
                dve.wait_ge(sem("kd_exp"), 1)
                v.tensor_tensor(reg(A3, 1024), reg(A3, 1024), reg(1024, 1024), ALU.mult).then_inc(sem("kd_ready"), 1)

            def first_states():
                dve.wait_ge(sem("e_last"), 1)
                dve.wait_ge(sem("u_done"), 1)
                link(v.tensor_copy(states[:, 0, :, :], side(0, 1024).rearrange("p (h e) -> p h e", h=GLA_HEADS)))
                dve.wait_ge(sem("u_done"), 2)
                for h in range(GLA_HEADS):
                    ins = v.scalar_tensor_tensor(out=states[:, 1, h, :], in0=states[:, 0, h, :], scalar=sm(E_LAST + NCHUNK * h + 1),
                                                 in1=side(2, 1024)[:, GLA_DV * h:GLA_DV * (h + 1)], op0=ALU.mult, op1=ALU.add)
                ins.then_inc(sem("u_used"), 1)

            def last_state():
                dve.wait_ge(sem("u_done"), 3)
                dve.wait_ge(sem("u_used"), 1)
                for h in range(GLA_HEADS):
                    ins = v.scalar_tensor_tensor(out=states[:, 2, h, :], in0=states[:, 1, h, :], scalar=sm(E_LAST + NCHUNK * h + 2),
                                                 in1=side(0, 1024)[:, GLA_DV * h:GLA_DV * (h + 1)], op0=ALU.mult, op1=ALU.add)
                ins.then_inc(sem("states_ready"), 1)

            def level_diff(n):
                s = LEVELS[n]
                b4 = reg(A4, 1024).rearrange("p (c s) -> p c s", s=2 * s)
                if n:
                    dve.wait_ge(sem("k_lvl"), n)
                    dve.wait_ge(sem("q_lvl"), n)
                else:
                    dve.wait_ge(sem("q_ex_ready"), 1)
                v.tensor_tensor(reg(A1, 1024).rearrange("p (c s) -> p c s", s=2 * s), b4,
                                b4[:, :, s - 1:s].to_broadcast([P, 512 // s, 2 * s]), ALU.subtract).then_inc(sem("lvl_diff"), 1)

            def level_q(n):
                if n >= 2:
                    dve.wait_ge(sem("lvl_mm"), n - 1)
                qt = head_tok(q_lvl_at[n % 2])
                if n < len(LEVELS):
                    dve.wait_ge(sem("lvl_exp"), n + 1)
                    v.scalar_tensor_tensor(out=qt, in0=q, scalar=GS, in1=head_tok(A1), op0=ALU.mult, op1=ALU.mult).then_inc(sem("q_lvl"), 1)
                else:
                    v.tensor_scalar(qt, q, GS, None, ALU.mult).then_inc(sem("q_lvl"), 1)

            def level_sum(n):
                dve.wait_ge(sem("lvl_mm"), n + 1)
                mask = con[:, C_LVL + P * n:C_LVL + P * (n + 1)].unsqueeze(1).to_broadcast([P, 8, P])
                got = side(2 * (n % 2), 1024).rearrange("p (n i) -> p n i", n=8)
                acc = reg(A5, 1024).rearrange("p (n i) -> p n i", n=8)
                tmp = reg(A6, 1024).rearrange("p (n i) -> p n i", n=8)
                if n == 0:
                    v.tensor_tensor(acc, got, mask, ALU.mult).then_inc(sem("lvl_sum"), 1)
                else:
                    dve.wait_ge(sem("lvl_sum"), n)
                    link(v.tensor_tensor(tmp, got, mask, ALU.mult))
                    v.tensor_tensor(acc, acc, tmp, ALU.add).then_inc(sem("lvl_sum"), 1)

            def o_means():
                dve.wait_ge(sem("o_sq"), 1)
                link(v.tensor_reduce(sm(O_SS, 8), reg(A4, 2048).rearrange("p (n e) -> p n e", e=GLA_DV), AX_X, ALU.add))
                v.tensor_scalar(sm(O_SS, 8), sm(O_SS, 8), 1.0 / GLA_DV, EPS, ALU.mult, ALU.add).then_inc(sem("o_ms"), 1)

            def o_norm():
                dve.wait_ge(sem("o_sd"), 1)
                link(v.reciprocal(sm(O_SS, 8), sm(O_SD, 8)))
                o8 = reg(A2, 2048).rearrange("p (n e) -> p n e", e=GLA_DV)
                link(v.tensor_tensor(o8, o8, sm(O_SS, 8).unsqueeze(2).to_broadcast([P, 8, GLA_DV]), ALU.mult))

            def o_gate():
                dve.wait_ge(sem("r_silu"), 1)
                for b in range(2):
                    oo = reg(A2, 2048).rearrange("p (t n) -> p t n", t=TT)[:, :, 512 * b:512 * (b + 1)]
                    v.tensor_tensor(oo, oo, z[:, 4 + b, :].rearrange("p (t n) -> p t n", t=TT), ALU.mult).then_inc(sem("o_gated"), 1)

            def mix_taps(b, j, shift):
                if j == 1:
                    dve.wait_ge(sem("mix_tap"), 12 * b + 4)
                else:
                    dve.wait_ge(sem("mix_tap"), 12 * b + 8)
                for f in range(4 * b, 4 * b + 4):
                    v.scalar_tensor_tensor(out=cx[:, f, shift:], in0=cc[:, f, 0:S - shift], scalar=colA(A_CW + 8 * j + f),
                                           in1=cx[:, f, shift:], op0=ALU.mult, op1=ALU.add).then_inc(sem("mix_tap"), 1)

            def conv_out(b):
                dve.wait_ge(sem("mix_tap"), 12 * b + 12)
                dve.wait_ge(epi_done, blocks_before("in2") + 11 + b)
                v.tensor_tensor(cb[:, 4 * b:4 * b + 4, :], cb[:, 4 * b:4 * b + 4, :], cx[:, 4 * b:4 * b + 4, :],
                                ALU.mult).then_inc(sem("yT_conv_ready"), 1)

            def gate_diag(wcols, first):
                dve.wait_ge(sem("modc_ready"), first // 4 + 4)
                link(v.tensor_tensor(sm(GP, KT), modc[:, first:first + KT], wcols, ALU.mult))
                v.tensor_tensor(diag, ident.unsqueeze(1).to_broadcast([P, KT, P]), sm(GP, KT).unsqueeze(2).to_broadcast([P, KT, P]),
                                ALU.mult).then_inc(sem("diag_ready"), 1)

            def mixer2(at):
                if at == 16:
                    log_decay()
                if at == 17:
                    decay_sums()
                if at == 19:
                    from_start()
                if at == 20:
                    to_end()
                if at == 24:
                    first_states()
                if at == 26:
                    last_state()
                if at >= 24 and at % 2 == 0 and (at - 24) // 2 < len(LEVELS):
                    level_diff((at - 24) // 2)
                if at >= 25 and at % 2 == 1 and (at - 25) // 2 <= len(LEVELS):
                    level_q((at - 25) // 2)
                if at >= 28 and at % 2 == 0 and (at - 28) // 2 <= len(LEVELS):
                    level_sum((at - 28) // 2)
                if at in (40, 41):
                    mix_taps(0, 41 - at, at - 39)
                if at == 43:
                    o_means()
                if at in (44, 45):
                    mix_taps(1, 45 - at, at - 43)
                if at == 45:
                    o_norm()
                if at == 46:
                    o_gate()
                if at == 47:
                    conv_out(0)

            pairs("in2", epi_none, GATE_RANK, mixer2)
            lead("out2")
            conv_out(1)
            gate_diag(colA(A_MPOST, KT), 32)
            split_mixed(4, yT_conv, yT_gla)

            def epi_gated(ph, blk, i0, i, r):
                j = 2 * i0 + blk
                dve.wait_ge(sem("post_sq"), 2 * j + 2)
                dve.wait_ge(sem("row_ready"), 1)
                v.tensor_tensor(y[:, :, BLOCK * j:BLOCK * (j + 1)], main(blk).rearrange("p (t n) -> p t n", t=TT),
                                g_row[:, BLOCK * j:BLOCK * (j + 1)].unsqueeze(1).to_broadcast([P, TT, BLOCK]),
                                ALU.mult).then_inc(epi_done, 1)

            def post_add(qq):
                dve.wait_ge(sem("post_sd"), qq + 1)
                link(v.reciprocal(sm(P_RSTD + 2 * qq, 2), sm(P_SD + 2 * qq, 2)))
                for t in range(TT):
                    v.scalar_tensor_tensor(out=x[:, t, :], in0=y[:, t, :], scalar=sm(P_RSTD + 2 * qq + t), in1=x[:, t, :],
                                           op0=ALU.mult, op1=ALU.add).then_inc(sem("x_new"), 1)

            pairs("out2", epi_gated)
            lead("up2")
            dve.wait_ge(sem("post_sq"), 8)
            link(v.tensor_reduce(sm(P_RSTD, 2), sm(P_SS, 8).rearrange("p (t j) -> p t j", t=TT), AX_X, ALU.add))
            v.tensor_scalar(sm(P_SS, 2), sm(P_RSTD, 2), 1.0 / D, EPS, ALU.mult, ALU.add).then_inc(sem("post_ms"), 1)
            last_epi("out2", epi_gated)
            dve.wait_ge(epi_done, blocks_before("up2"))
            post_add(0)
            norm_sums(3)
            last_unit("out2")
            scales(SCALE_F, colA(A_FPRE, KT), 64)
            norm(3, 5, sm(SCALE_F, KT), modc[:, 48:64])

            def last_row(at):
                if at == 36:
                    gate_diag(colB(B_FPOST, KT), 80)

            pairs("up2", epi_conv(2, 1), between=last_row)
            lead("down2")
            last_epi("up2", epi_conv(2, 1))
            down("down2", 1)
            dve.wait_ge(w_used, down_end("down2"))
            dve.wait_ge(sem("row_ready"), 2)
            for t in (1, 0):
                if t == 0:
                    dve.wait_ge(sem("post_sq"), 9)
                v.tensor_tensor(y[:, t, :], ps[:, D * t:D * (t + 1)], g_row, ALU.mult).then_inc(sem("yg_ready"), 1)
            dve.wait_ge(sem("post_sq"), 10)
            v.tensor_scalar(sm(P_SS, 2), sm(P_SS, 8).rearrange("p (t j) -> p t j", t=TT)[:, :, 0], 1.0 / D, EPS, ALU.mult,
                            ALU.add).then_inc(sem("post_ms"), 1)
            dve.wait_ge(sem("yg_ready"), 2)
            post_add(1)

        @block.gpsimd
        def _(pool):
            gp = nc.gpsimd
            seq = [0]

            def link(ins):
                seq[0] += 1
                ins.then_inc(sem("pool_step"), 1)
                pool.wait_ge(sem("pool_step"), seq[0])

            pool.wait_ge(sem("qk_rstd"), 1)
            for n in range(2):
                zz = reg(2048 + 2048 * n, 2048).rearrange("p (n d) -> p n d", d=HD)
                gp.tensor_tensor(zz, zz, sm(QK_SS + 16 * n, 16).unsqueeze(2).to_broadcast([P, 16, HD]), ALU.mult).then_inc(sem("qk_normed"), 1)
            pool.wait_ge(epi_done, 8)
            pool.wait_ge(sem("qkT_ready"), 4)
            for n, win_size in enumerate(WINDOWS):
                u = yT_pool[:, 2 * n:2 * n + 2, :]
                cur, sh, b = u, 1, 0
                while sh < win_size:
                    nxt = win[b]
                    link(gp.tensor_tensor(nxt[:, :, sh:], cur[:, :, sh:], cur[:, :, 0:S - sh], ALU.add))
                    link(gp.tensor_copy(nxt[:, :, 0:sh], cur[:, :, 0:sh]))
                    cur, b, sh = nxt, 1 - b, 2 * sh
                mean = win[b]
                link(gp.tensor_scalar(mean[:, :, 16:], cur[:, :, 16:], 1.0 / win_size, None, ALU.mult))
                link(gp.tensor_tensor(mean[:, :, 0:16], cur[:, :, 0:16],
                                      con[:, C_INV + 16 * n:C_INV + 16 * n + 16].unsqueeze(1).to_broadcast([P, 2, 16]), ALU.mult))
                ins = gp.tensor_tensor(dT[:, 2 * n:2 * n + 2, :], mean, u, ALU.subtract)
                if n < len(WINDOWS) - 1:
                    link(ins)
                else:
                    ins.then_inc(sem("d_ready"), 1)

            pool.wait_ge(epi_done, blocks_before("in2") + 1)
            gp.memset(q_ex, 0.0).then_inc(sem("q_ex_zero"), 1)
            for n in range(len(LEVELS)):
                pool.wait_ge(sem("lvl_exp"), n + 1)
                if n:
                    pool.wait_ge(sem("lvl_mm"), n)
                else:
                    pool.wait_ge(sem("kd_turned"), 1)
                gp.tensor_tensor(reg(A3, 1024), reg(1024, 1024), reg(A1, 1024), ALU.mult).then_inc(sem("k_lvl"), 1)
            for b in range(2):
                pool.wait_ge(epi_done, blocks_before("in2") + 9 + b)
                gp.tensor_tensor(cc[:, 4 * b:4 * b + 4, :], cc[:, 4 * b:4 * b + 4, :], cx[:, 4 * b:4 * b + 4, :],
                                 ALU.mult).then_inc(sem("ccx_ready"), 1)

        @block.tensor
        def _(pe):
            mmul = nc.tensor.matmul

            def three(dst, lhs_hi, lhs_lo, rhs_hi, rhs_lo, start, stop):
                mmul(dst, lhs_hi, rhs_hi, start=start, stop=False, skip_group_check=True)
                mmul(dst, lhs_hi, rhs_lo, start=False, stop=False, skip_group_check=True)
                return mmul(dst, lhs_lo, rhs_hi, start=False, stop=stop, skip_group_check=True)

            def rest(name, cols):
                m = PH[name].rest
                for half in range(2):
                    hh = 2 * m + half
                    pe.wait_ge(lo_ready, hh + 1)
                    for kk in range(KT // 2):
                        kt = KT // 2 * half + kk
                        for t in range(TT):
                            tok = slice(t * P, (t + 1) * P)
                            wc = slice(kk * cols, (kk + 1) * cols)
                            mm = three(side(t, cols), a_hi[:, kt, tok], a_lo[:, kt, tok], w_hi[:, hh % HL_SLOTS, wc],
                                       w_lo[:, hh % HL_SLOTS, wc], kt == 0, kt == KT - 1)
                    mm.then_inc(w_used, 1)

            def half_T(dst, hh, kts, first, last):
                for kk, kt in enumerate(kts):
                    for t in range(TT):
                        tok = slice(t * P, (t + 1) * P)
                        wc = slice(kk * BLOCK, (kk + 1) * BLOCK)
                        mm = three(dst[:, t * BLOCK:(t + 1) * BLOCK], a_hi[:, kt, tok], a_lo[:, kt, tok],
                                   w_hi[:, hh % HL_SLOTS, wc], w_lo[:, hh % HL_SLOTS, wc],
                                   first and kk == 0, last and kk == len(kts) - 1)
                return mm

            def half_W(dst, hh, kts, first, last):
                for kk, kt in enumerate(kts):
                    for ft in range(4):
                        wc = slice(kk * BLOCK + ft * P, kk * BLOCK + (ft + 1) * P)
                        mm = three(dst[:, ft * S:(ft + 1) * S], w_hi[:, hh % HL_SLOTS, wc], w_lo[:, hh % HL_SLOTS, wc],
                                   a_hi[:, kt, :], a_lo[:, kt, :], first and kk == 0 and ft % 2 == 0, last and kk == len(kts) - 1)
                return mm

            def pairs(name, narrow=0, between=None):
                ph = PH[name]
                f = FILL[name]

                def body(i0, i, r, layout):
                    pair = ph.pairs[i0]
                    for blk in range(2):
                        b = pair.b0 + blk
                        if b >= 2:
                            pe.wait_ge(epi_done, b - 1 + 2 * r)
                        for c in range(BLOCK_CHUNKS):
                            for half in range(2):
                                hh = 2 * (pair.m0 + 4 * blk + c) + half
                                pe.wait_ge(lo_ready, hh + 1 + 16 * r)
                                if i0 == 0 and blk == 0:
                                    pe.wait_ge(act_ready, 8 * f + 2 * c + half + 1)
                                kts = [KC * c + 2 * half, KC * c + 2 * half + 1]
                                (half_T if layout == "T" else half_W)(
                                    main(blk), hh, kts, c + half == 0, c == BLOCK_CHUNKS - 1 and half == 1).then_inc(w_used, 1)
                            if between:
                                between(8 * i0 + 4 * blk + c)
                    if pair.unit is not None:
                        pe.wait_ge(mod_step, UNIT_OPS * (pair.unit + 1) + UNIT_OPS * r)
                        for j in range(4):
                            mm = mmul(side(3)[:, 508 + j:509 + j], mod_acc[:, j * P:(j + 1) * P], ones[:, 0:1], start=True, stop=True)
                        mm.then_inc(mod_red, 1)
                    if narrow and i0 == 0:
                        rest(name, narrow)

                run_pairs(pe, name, body)

            def down(name, q):
                ph = PH[name]

                def chunk(j, r):
                    pe.wait_ge(sem("g_split"), FT * q + j + 1 + 4 * r)
                    for half in range(2):
                        hh = 2 * (ph.m0 + j) + half
                        pe.wait_ge(lo_ready, hh + 1 + 8 * r)
                        for t in range(TT):
                            for n in range(2):
                                at = t * D + half * HALF + n * BLOCK
                                tok = slice(t * P, (t + 1) * P)
                                wc = slice(n * BLOCK, (n + 1) * BLOCK)
                                mm = three(ps[:, at:at + BLOCK], a_hi[:, j % 4, tok], a_lo[:, j % 4, tok], w_hi[:, hh % HL_SLOTS, wc],
                                           w_lo[:, hh % HL_SLOTS, wc], j == 0, False)
                        mm.then_inc(w_used, 1)

                for j in range(4):
                    chunk(j, 0)
                with pe.Fori(1, FT // 4) as i:
                    for j in range(4):
                        chunk(4 + j, i - 1)

            def norm(p):
                pe.wait_ge(sem("hn_dve"), p + 1)
                pe.wait_ge(sem("hn_act"), p + 1)
                for k in range(KT // 2):
                    if k >= 4:
                        pe.wait_ge(sem("xt_ready"), KT * p + 2 * (k - 4) + 2)
                    for kk in range(2):
                        for t in range(TT):
                            at = S * kk + P * t
                            mm = nc.tensor.transpose(side(k % 4)[:, at:at + P], hn[:, t, (2 * k + kk) * P:(2 * k + kk + 1) * P], ident)
                    mm.then_inc(sem("turned"), 1)

            rows = [A_ROWS, P] + [CONV_ROWS] * 7
            pe.wait_ge(sem("first_params"), 16 * N_FIRST)
            nc.tensor.transpose(side(0, A_ROWS), stage[0:A_ROWS, 0, :], ident[0:A_ROWS, 0:A_ROWS]).then_inc(sem("cols_turned"), 1)
            pe.wait_ge(sem("cols_ready"), 1)
            norm(0)
            pe.wait_ge(sem("second_params"), 16 * N_SECOND)
            pe.wait_ge(sem("xt_ready"), KT)
            for n in range(1, 9):
                at = SIDE + P * (n - 1)
                mm = nc.tensor.transpose(ps[:, at:at + rows[n]], stage[0:rows[n], n, :], ident[0:rows[n], 0:rows[n]])
            mm.then_inc(sem("cols_turned"), 1)

            def index_scores(n):
                t, b = divmod(n, 8)
                K = P * (t + 1)
                if n >= 3:
                    pe.wait_ge(sem("relu_ready"), n - 2)
                for j in range(2):
                    h = 4 * (b // 2) + b % 2 + 2 * j
                    half = slice(IDX_DIM * (h % 2), IDX_DIM * (h % 2 + 1))
                    mm = mmul(side(n % 3)[:, S * j:S * j + K], zw(0)[half, h // 2, t * P:(t + 1) * P], kidxT[half, 0:K],
                              start=True, stop=True, skip_group_check=True)
                mm.then_inc(sem("is_done"), 1)

            def qk_turn(n):
                b, t = divmod(n % 4, 2)
                pe.wait_ge(sem("qk_normed"), n // 4 + 1)
                pe.wait_ge(sem("relu_ready"), 16)
                if n >= 3:
                    pe.wait_ge(sem("qkT_ready"), n - 2)
                for h in range(4):
                    at = t * 512 + h * HD
                    mm = nc.tensor.transpose(side(n % 3)[:, h * P:(h + 1) * P], z[:, 2 + 2 * (n // 4) + b, at:at + HD], ident)
                mm.then_inc(sem("qk_turned"), 1)

            def scores(u):
                t, hg = divmod(u, 2)
                K = P * (t + 1)
                at = SIDE + 512 * (u % 2 if u < 2 else 0)
                pe.wait_ge(sem("qkT_ready"), 8)
                if u >= 2:
                    pe.wait_ge(sem("pT_ready"), u)
                for j in range(4):
                    mm = mmul(ps[:, at + K * j:at + K * (j + 1)], qT[:, 4 * hg + j, t * P:(t + 1) * P], kT[:, 4 * hg + j, 0:K],
                              start=True, stop=True, skip_group_check=True)
                mm.then_inc(sem("sc_done"), 1)

            def probs_turn(u):
                t = u // 2
                K = P * (t + 1)
                at = SIDE + 512 * (u % 2 if u < 2 else 0)
                pe.wait_ge(sem("p_ready"), u + 1)
                for st in range(t + 1):
                    for j in range(4):
                        o = at + P * (4 * st + j)
                        mm = nc.tensor.transpose(ps[:, o:o + P], sc_buf[:, u % 2, K * j + st * P:K * j + (st + 1) * P], ident)
                mm.then_inc(sem("p_turned"), 1)

            def attend(u):
                t, hg = divmod(u, 2)
                pe.wait_ge(sem("pT_ready"), u + 1)
                pe.wait_ge(epi_done, 10)
                if u:
                    pe.wait_ge(sem("yT_attn_ready"), u)
                for j in range(4):
                    for st in range(t + 1):
                        at = st * 512 + j * HD
                        mm = mmul(side(2)[:, P * j:P * (j + 1)], z[:, 8 + hg, at:at + HD], pT[u][:, P * (4 * st + j):P * (4 * st + j + 1)],
                                  start=(st == 0), stop=(st == t), skip_group_check=True)
                mm.then_inc(sem("pv_done"), 1)

            def pool_mix(e):
                pe.wait_ge(sem("d_ready"), 1)
                pe.wait_ge(sem("pool_w_loaded"), 16)
                if e:
                    pe.wait_ge(sem("yT_pool_ready"), 2 * e)
                else:
                    pe.wait_ge(sem("modc_ready"), 4)
                for f in range(2):
                    for c in range(2):
                        mm = mmul(side(3)[:, S * f:S * (f + 1)], pool_w[:, e, c, P * f:P * (f + 1)], dT[:, 2 * e + c, :],
                                  start=(c == 0), stop=(c == 1), skip_group_check=True)
                mm.then_inc(sem("pool_mixed"), 1)

            def mixer1(at):
                if at == 9:
                    pe.wait_ge(sem("kidx_out"), 4)
                    for t in range(TT):
                        mm = nc.tensor.transpose(side(2)[:, t * P:(t + 1) * P], kidx2[:, t, :, :].rearrange("p c d -> p (c d)"), ident)
                    mm.then_inc(sem("kidx_turned"), 1)
                if at == 11:
                    pe.wait_ge(sem("kidxT_ready"), 1)
                if 11 <= at < 19:
                    index_scores(2 * (at - 11))
                    index_scores(2 * (at - 11) + 1)
                if 31 <= at < 35:
                    qk_turn(2 * (at - 31))
                    qk_turn(2 * (at - 31) + 1)
                if at == 36:
                    scores(0)
                    scores(1)

            pe.wait_ge(sem("cols_ready"), 3)
            pairs("in1", IDX_REST, mixer1)
            probs_turn(0)
            probs_turn(1)
            pool_mix(0)
            scores(2)
            attend(0)
            pool_mix(1)
            attend(1)
            probs_turn(2)
            pool_mix(2)
            scores(3)
            attend(2)
            pool_mix(3)
            probs_turn(3)
            attend(3)

            pairs("out1")
            norm(1)
            pairs("up1")
            down("down1", 0)

            norm(2)
            kdT = reg(A6, 1024).rearrange("p (h t d) -> p h t d", h=GLA_HEADS, t=TT)

            def vv(t, h):
                return z[:, 2 + h // 2, 512 * t + GLA_DV * (h % 2):512 * t + GLA_DV * (h % 2 + 1)]

            def state_add(c):
                rows_c = slice(CHUNK * (c % 2), CHUNK * (c % 2 + 1))
                for h in range(GLA_HEADS):
                    mm = mmul(side((0, 2, 0)[c], 1024)[:, GLA_DV * h:GLA_DV * (h + 1)], kdT[rows_c, h, c // 2, :], vv(c // 2, h)[rows_c, :],
                              start=True, stop=True, skip_group_check=True)
                mm.then_inc(sem("u_done"), 1)

            def level_scores(n):
                pe.wait_ge(sem("q_lvl"), n + 1)
                if n < len(LEVELS):
                    pe.wait_ge(sem("k_lvl"), n + 1)
                if n >= 2:
                    pe.wait_ge(sem("lvl_sum"), n - 1)
                else:
                    pe.wait_ge(sem("states_ready"), 1)
                kk = head_tok(A3) if n < len(LEVELS) else head_tok(1024)
                for h in range(GLA_HEADS):
                    for t in range(TT):
                        tok = slice(t * P, (t + 1) * P)
                        at = P * (TT * h + t)
                        mm = mmul(side(2 * (n % 2), 1024)[:, at:at + P], kk[:, h, tok], head_tok(q_lvl_at[n % 2])[:, h, tok], start=True,
                                  stop=True, skip_group_check=True)
                mm.then_inc(sem("lvl_mm"), 1)

            def mixer2(at):
                if at == 9:
                    pe.wait_ge(sem("alr_out"), 2)
                    for t in range(TT):
                        mm = nc.tensor.transpose(ps[0:GATE_RANK, SIDE + 1024 + t * P:SIDE + 1024 + (t + 1) * P], a_lr[:, t, :], ident)
                    mm.then_inc(sem("alr_turned"), 1)
                if at == 11:
                    pe.wait_ge(sem("alrT_ready"), 1)
                    pe.wait_ge(sem("gate_loaded"), 16)
                    for h in range(GLA_HEADS):
                        mm = mmul(ps[:, SIDE + S * h:SIDE + S * (h + 1)], gate_w2[:, h * HD:(h + 1) * HD], a_lrT, start=True, stop=True,
                                  skip_group_check=True)
                    mm.then_inc(sem("gate_mm"), 1)
                if at == 19:
                    pe.wait_ge(sem("kd_ready"), 1)
                    for h in range(GLA_HEADS):
                        for t in range(TT):
                            o = SIDE + P * (TT * h + t)
                            mm = nc.tensor.transpose(ps[:, o:o + P], head_tok(A3)[:, h, t * P:(t + 1) * P], ident)
                    mm.then_inc(sem("kd_turned"), 1)
                if at == 21:
                    pe.wait_ge(sem("kdT_ready"), 1)
                    pe.wait_ge(sem("modc_ready"), PH["in2"].pairs[0].unit + 1)
                    state_add(0)
                    state_add(1)
                if at == 23:
                    pe.wait_ge(sem("u_used"), 1)
                    state_add(2)
                if at >= 25 and at % 2 == 1 and (at - 25) // 2 <= len(LEVELS):
                    level_scores((at - 25) // 2)
                if at == 39:
                    pe.wait_ge(sem("lvl_sum"), len(LEVELS) + 1)
                    sc = reg(A5, 1024).rearrange("p (h t i) -> p h t i", h=GLA_HEADS, t=TT)
                    for t in range(TT):
                        for h in range(GLA_HEADS):
                            dst = side(2 * t, 1024)[:, GLA_DV * h:GLA_DV * (h + 1)]
                            mmul(dst, sc[:, h, t, :], vv(t, h), start=True, stop=False, skip_group_check=True)
                            chunks = [c for c in (2 * t, 2 * t + 1) if c > 0]
                            for c in chunks:
                                mm = mmul(dst, q_ex[:, h, c - 1, :], states[:, c - 1, h, :], start=False, stop=(c == chunks[-1]),
                                          skip_group_check=True)
                    mm.then_inc(sem("o_done"), 1)
                if at == 45:
                    pe.wait_ge(sem("o_gated"), 2)
                    for f in range(8):
                        for t in range(TT):
                            mm = nc.tensor.transpose(ps[:, SIDE + S * f + P * t:SIDE + S * f + P * (t + 1)],
                                                     reg(A2, 2048).rearrange("p (t n) -> p t n", t=TT)[:, t, f * P:(f + 1) * P], ident)
                    mm.then_inc(sem("o_turned"), 1)

            def gate_row(q):
                pe.wait_ge(sem("diag_ready"), q + 1)
                for n in range(4):
                    mm = mmul(side(n), ones, diag[:, 4 * n:4 * n + 4, :].rearrange("p k f -> p (k f)"), start=True, stop=True)
                mm.then_inc(sem("row_mm"), 1)

            pairs("in2", GATE_RANK, mixer2)
            pe.wait_ge(sem("yT_gla_ready"), 8)
            gate_row(0)
            pe.wait_ge(sem("row_ready"), 1)
            pairs("out2")
            norm(3)

            def last_row(at):
                if at == 37:
                    pe.wait_ge(sem("modc_ready"), 24)
                    gate_row(1)

            pairs("up2", between=last_row)
            pe.wait_ge(sem("row_ready"), 2)
            down("down2", 1)


VECTORS = ["attn_norm_g", "w_in", "pool_w", "pool_scale", "q_norm_g", "k_norm_g", "w_out", "ffn_norm_g", "w_up", "conv_w", "conv_b",
           "w_down", "c_2", "w_mod_2", "b_mod_2", "mix_pre_w_2", "mix_post_w_2", "w_in_2", "conv_w_2", "gate_w2_2", "gate_b_2",
           "gla_norm_w_2", "w_out_2", "ffn_pre_w_2", "ffn_post_w_2", "w_up_2", "ffn_conv_w_2", "w_down_2"]


def kernel(**inputs):
    import concourse.bacc as bacc
    from concourse.bass_utils import run_bass_kernel_spmd

    nc = bacc.Bacc("TRN2", target_bir_lowering=False, num_devices=1, dynamic_dma_scratch_size=1024)
    arrays = {}

    def dram(name, a):
        arrays[name] = a
        return nc.dram_tensor(name, a.shape, F32, kind="ExternalInput").ap()

    x = np.ascontiguousarray(inputs["x"])
    x_in = dram("in_x", x.reshape(S, D))
    w = {}
    for name in VECTORS:
        a = np.ascontiguousarray(inputs[name])
        if name.endswith("_2") and a.shape[0] == 1:
            a = a.reshape(a.shape[1:])
        w[name] = dram("in_" + name, a)
    consts = dram("in_constants", constants())
    out = nc.dram_tensor("out_x", (S, D), F32, kind="ExternalOutput").ap()
    two_blocks(nc, consts, x_in, out, w)
    r = run_bass_kernel_spmd(nc, [arrays], core_ids=[0])
    return r.results[0]["out_x"].reshape(x.shape)
```

```python
from contextlib import ExitStack

import numpy as np

import concourse.bass as bass
from concourse import mybir

F32 = mybir.dt.float32
F32R = mybir.dt.float32r
ALU = mybir.AluOpType
ACT = mybir.ActivationFunctionType
AX_X = mybir.AxisListType.X

P = 128
D = 2048
S = 256
TT = S // P
KT = D // P
F = 5632
FT = F // P
EPS = 1e-6
NEG = float(np.finfo(np.float32).min)
HEADS = 8
HD = 128
IDX_HEADS = 16
IDX_DIM = 64
TOPK = S // 4
TOP_ROUNDS = TOPK // 8
WINDOWS = (2, 4, 8, 16)
GLA_HEADS = 4
GLA_DV = 256
CHUNK = 64
NCHUNK = S // CHUNK
GATE_RANK = 16
GATE_TAU = 16
LEVELS = (32, 16, 8, 4, 2, 1)

BLOCK = 512
PAIRS_UP = F // BLOCK
KC = 4
CHUNK_EL = KC * BLOCK
HALF = CHUNK_EL // 2
RAW_SLOTS = 4
HL_SLOTS = 4
BLOCK_CHUNKS = KT // KC
UNIT_OPS = KT

IDX_REST = IDX_DIM + IDX_HEADS
IN1_STARTS = (4096, 2048, 1024, 0, 3072)
IN2_STARTS = (3072, 4096, 5120, 1024, 2048, 0)
IN1_REST = 5120
IN2_REST = 6144

C_ID, C_ONE, C_LVL, C_RST, C_TRI, C_INV = 0, 128, 256, 256 + 896, 256 + 896 + 256, 256 + 896 + 384
C_N = C_INV + 64

A_ATTN, A_FFN, A_PSC, A_MPRE, A_FPRE, A_MPOST, A_GB, A_QG, A_KG, A_GLA, A_CW = 0, 16, 32, 40, 56, 72, 88, 92, 93, 94, 96
A_ROWS = 120
B_MOD, B_C, B_FPOST = 0, 96, 112
CONV_ROWS = 2 * FT
N_FIRST, N_SECOND = 2, 21
DOWN_BODY = 8


def constants():
    c = np.zeros((P, C_N), np.float32)
    c[:, C_ID:C_ID + P] = np.eye(P)
    c[:, C_ONE:C_ONE + P] = 1.0
    j, i = np.arange(P)[:, None], np.arange(P)[None, :]
    for n, s in enumerate(LEVELS):
        c[:, C_LVL + n * P:C_LVL + (n + 1) * P] = (j // (2 * s) == i // (2 * s)) & (j % (2 * s) < s) & (i % (2 * s) >= s)
    c[:, C_LVL + 6 * P:C_LVL + 7 * P] = np.eye(P)
    c[:, C_RST:C_RST + S] = (np.arange(S) % CHUNK != 0)
    c[:, C_TRI:C_TRI + P] = np.where(i <= j, 0.0, NEG)
    for n, w in enumerate(WINDOWS):
        c[:, C_INV + 16 * n:C_INV + 16 * n + 16] = 1.0 / np.minimum(np.arange(16) + 1, w)
    return c


class Pair:

    def __init__(self, order, units, block, m0, mod):
        self.n0, self.m0, self.b0 = len(order), m0, block
        self.unit = units if mod else None


class Phase:
    def __init__(self):
        self.pairs, self.rest, self.m0, self.n0, self.unit = [], None, None, None, None


WITH_UNIT = "ggggmgmgmggm"
DOWN_WITH_UNIT = "gmgmgmgmgggg"

STREAM = (
    ("in1", (0, 1, 0, 1, 0), True),
    ("out1", (1, 1), False),
    ("up1", (1,) * 8 + (0,) * (PAIRS_UP - 8), False),
    ("down1", 5, False),
    ("in2", (1, 0, 0, 0, 0, 0), True),
    ("out2", (1, 1), False),
    ("up2", (1,) * 4 + (0,) * (PAIRS_UP - 4), False),
    ("down2", 0, False),
)


def plan():
    order, phases, blocks, units = [], {}, 0, 0
    count = {"g": 0, "m": 0}

    def add(kinds):
        for kind in kinds:
            order.append((kind, count[kind]))
            count[kind] += 1

    for name, mods, rest in STREAM:
        ph = phases[name] = Phase()
        ph.m0, ph.n0 = count["g"], len(order)
        if type(mods) is int:
            ph.unit = units if mods else None
            units += mods
            add("gggg" + (DOWN_WITH_UNIT if mods else "g" * DOWN_BODY) * ((FT - 4) // DOWN_BODY))
            assert mods in (0, (FT - 4) // DOWN_BODY)
            continue
        for i, mod in enumerate(mods):
            ph.pairs.append(Pair(order, units, blocks, count["g"], mod))
            units += mod
            blocks += 2
            add(WITH_UNIT if mod else "g" * 8)
            if rest and i == 0:
                ph.rest = count["g"]
                count["g"] += 1
    return order, phases


ORDER, PH = plan()
RAW_OF = {m: n for n, (kind, m) in enumerate(ORDER) if kind == "g"}
RAW_OF_MOD = {k: n for n, (kind, k) in enumerate(ORDER) if kind == "m"}


def raw_stride(pair):
    return 16 * (8 if pair.unit is None else 12) // RAW_SLOTS


def down_items(ph):
    n = ph.n0 + 4
    return [(n + j, *ORDER[n + j]) for j in range(DOWN_BODY if ph.unit is None else DOWN_BODY + 4)]


def pair_items(pair):
    return [(n, *ORDER[n]) for n in range(pair.n0, pair.n0 + (8 if pair.unit is None else 12))]


def two_blocks(nc, consts, x_in, out, w):
    with ExitStack() as ctx:
        def sb(name, shape, dt=F32):
            return ctx.enter_context(nc.sbuf_tensor(name, shape, dt))

        sems = {}

        def sem(name):
            if name not in sems:
                sems[name] = ctx.enter_context(nc.semaphore(name))
            return sems[name]

        raw = sb("raw", [P, RAW_SLOTS, CHUNK_EL])
        w_hi = sb("w_hi", [P, HL_SLOTS, HALF], F32R)
        w_lo = sb("w_lo", [P, HL_SLOTS, HALF], F32R)
        x = sb("x", [P, TT, D])
        a_hi = sb("a_hi", [P, KT, S], F32R)
        a_lo = sb("a_lo", [P, KT, S], F32R)
        con = sb("con", [P, C_N])
        col = sb("col", [P, 9, P])
        modc = sb("modc", [P, 96])
        mod_acc = sb("mod_acc", [P, BLOCK])
        small = sb("small", [P, 288])
        REGION = 24576
        region = sb("region", [P, REGION])
        ps = ctx.enter_context(nc.psum_tensor("ps", [P, 4096], F32))

        def reg(at, n):
            return region[:, at:at + n]

        def main(g):
            return ps[:, 1024 * g:1024 * (g + 1)]

        SIDE = 2048

        def side(b, n=512):
            return ps[:, SIDE + 512 * b:SIDE + 512 * b + n]

        def turn_bank(k):
            return side(k % 5) if k % 5 < 4 else main(1)[:, 512:1024]

        ident = con[:, C_ID:C_ID + P]
        ones = con[:, C_ONE:C_ONE + P]
        tri = con[:, C_TRI:C_TRI + P]

        def colA(r, n=1):
            return col[:, 0, r:r + n]

        def colB(r, n=1):
            return col[:, 1, r:r + n]

        def sm(at, n=1):
            return small[:, at:at + n]
        SS, MS, SD, RSTD = 0, 8, 16, 24
        C_ACT, SCALE_M, SCALE_F = 32, 48, 64
        QK_SS, QK_SD = 80, 112
        MX, RSUM, RINV = 144, 160, 168
        E_LAST = 176
        O_SS, O_SD = 192, 200
        P_SS, P_SD, P_RSTD = 264, 272, 276
        GP = 216
        WIDX = 232
        SPARE = 284
        SS_HALF = 280

        hn = reg(0, 4096).rearrange("p (t d) -> p t d", t=TT)
        xt = reg(4096, 4096).rearrange("p (k s) -> p k s", k=KT)
        stage = reg(8192, 9 * P).rearrange("p (n d) -> p n d", n=9)
        z = reg(0, 12288).rearrange("p (b n) -> p b n", b=12)

        def zw(b):
            return region[:, 1024 * b:1024 * b + 2048].rearrange("p (f s) -> p f s", f=8)

        pool_w = reg(12288, 2048).rearrange("p (g c d) -> p g c d", g=4, c=2)
        kT = reg(14336, 2048).rearrange("p (h s) -> p h s", h=HEADS)
        qT = reg(16384, 2048).rearrange("p (h s) -> p h s", h=HEADS)
        widxT = region[0:IDX_HEADS, 18432:18432 + S]
        kidxT = reg(18688, 256)
        rest1 = reg(18944, KT * IDX_REST)
        relu_buf = reg(18944, 1024).rearrange("p (b j s) -> p b j s", b=2, j=2)
        sc_buf = reg(18944, 2048).rearrange("p (b n) -> p b n", b=2)
        iscore = reg(21024, 512).rearrange("p (t s) -> p t s", t=TT)
        work = reg(21536, 512).rearrange("p (t s) -> p t s", t=TT)
        top8 = reg(22048, 128).rearrange("p (n e) -> p n e", e=8)
        notsel = reg(22176, 512).rearrange("p (t s) -> p t s", t=TT)
        win = [reg(22688 + 512 * n, 512).rearrange("p (f s) -> p f s", f=2) for n in range(2)]
        pT = [reg(512 * u, 512) if u < 4 else reg(21024 + 512 * (u - 4), 512) for u in range(6)]
        dT = zw(2)
        yT_attn = zw(4)
        yT_pool = zw(6)
        A1, A2, A3, A4, A5, A6 = (12288 + 1024 * n for n in range(6))
        A7 = 23552

        def head_tok(at):
            return reg(at, 1024).rearrange("p (h s) -> p h s", h=GLA_HEADS)
        q_ex = reg(18432, 1536).rearrange("p (h c s) -> p h c s", h=GLA_HEADS, c=3)
        states = reg(19968, 3072).rearrange("p (c h e) -> p c h e", c=3, h=GLA_HEADS)
        rest2 = reg(A7, KT * GATE_RANK)
        a_lrT = region[0:GATE_RANK, 20224:20224 + S]
        gate_w2 = region[0:GATE_RANK, 23040:23040 + 512]
        o_gla = reg(A2, 2048).rearrange("p (t h e) -> p t h e", t=TT, h=GLA_HEADS)
        yT_gla = zw(0)
        cc, cx, cb = zw(6), zw(8), zw(10)
        yT_conv = cb
        q_lvl_at = (A2, A7)
        g = reg(0, FT * S).rearrange("p (f s) -> p f s", f=FT)
        c_gate = reg(11264, 1024).rearrange("p (f s) -> p f s", f=4)
        c_val = reg(12288, 1024).rearrange("p (f s) -> p f s", f=4)
        DOWN_ACC = 13312
        y = reg(12288, 4096).rearrange("p (t d) -> p t d", t=TT)
        diag = reg(16384, 2048).rearrange("p (k f) -> p k f", k=KT)
        g_row = reg(22528, 2048)

        def attention_unit(u):
            return (0, 4 * u, 4, P) if u < 2 else (1, 2 * (u - 2), 2, S)

        ATTEND = ((0, 0, 0, 4), (1, 0, 1, 5), (0, 1, 0, 5), (1, 1, 2, 6))

        raw_full = [sem(f"raw_full{s}") for s in range(RAW_SLOTS)]
        hi_ready = sem("hi_ready")
        lo_ready = sem("lo_ready")
        w_used = sem("w_used")
        mod_step = sem("mod_step")
        mod_red = sem("mod_red")
        epi_done = sem("epi_done")
        act_hi = sem("act_hi")
        act_ready = sem("act_ready")

        RUNS = {
            "in1": [(0, 1, "W"), (1, 2, "T"), (2, 3, "T"), (3, 4, "W"), (4, 5, "T")],
            "out1": [(0, 1, "T"), (1, 2, "T")],
            "up1": [(0, 1, "W"), (1, 8, "W"), (8, 9, "W"), (9, PAIRS_UP, "W")],
            "in2": [(0, 1, "W"), (1, 2, "T"), (2, 3, "T"), (3, 4, "W"), (4, 5, "W"), (5, 6, "W")],
            "out2": [(0, 1, "T"), (1, 2, "T")],
            "up2": [(0, 1, "W"), (1, 4, "W"), (4, 5, "W"), (5, PAIRS_UP, "W")],
        }
        K_ORDER = {name: (0, 1, 2, 3) for name in RUNS}
        K_ORDER["out2"] = (2, 3, 0, 1)
        FILL = {"in1": 0, "out1": 1, "up1": 2, "in2": 3, "out2": 4, "up2": 5}

        def run_pairs(eng, name, body):
            for a, b, layout in RUNS[name]:
                if b - a == 1:
                    body(a, a, 0, layout)
                else:
                    with eng.Fori(a, b) as i:
                        body(a, i, i - a, layout)

        def block_end(ph, i0, blk):
            return 2 * (ph.pairs[i0].m0 + 4 * (blk + 1))

        def blocks_before(name):
            return PH[name].pairs[0].b0

        SQUARES = (3, 11, 14, 17)
        REST = {"in1": rest1, "in2": rest2}
        BEFORE_DOWN = {"down1": PH["up1"].pairs[-1], "down2": PH["up2"].pairs[-1]}

        def down_end(name):
            return 2 * (PH[name].m0 + FT)

        block = ctx.enter_context(nc.Block())

        @block.sync
        def _(sp):
            def slot_free(n, r=0, stride=16):
                if n < RAW_SLOTS:
                    return
                kind, at = ORDER[n - RAW_SLOTS]
                if kind == "g":
                    sp.wait_ge(lo_ready, 2 * (at + 1) + r * stride)
                else:
                    sp.wait_ge(mod_step, 4 * (at + 1) + r * stride)

            def settled(value):
                return value if type(value) is int else sp.snap(value)

            def load_columns(n, src):
                sp.dma_start(raw[:, n % RAW_SLOTS, :].rearrange("p (k n) -> p k n", k=KC),
                             src.rearrange("(k p) n -> p k n", p=P)).then_inc(raw_full[n % RAW_SLOTS], 16)

            def load_mod(n, c, unit, r):
                src = w["w_mod_2"][c * KC * P:(c + 1) * KC * P, bass.ds(settled(unit * BLOCK + r * BLOCK), BLOCK)]
                slot_free(n, r)
                load_columns(n, src)

            def pairs(name, wt, column, step=0, beside=None):
                ph = PH[name]

                def body(i0, i, r, layout):
                    pair = ph.pairs[i0]
                    for n, kind, at in pair_items(pair):
                        if kind == "g":
                            blk, c = divmod(at - pair.m0, 4)
                            k0 = K_ORDER[name][c] * KC * P
                            src = wt[k0:k0 + KC * P, bass.ds(settled(column(i0, blk) + step * r), BLOCK)]
                            slot_free(n, r)
                            load_columns(n, src)
                            if beside and n == RAW_SLOTS - 1:
                                beside()
                        else:
                            load_mod(n, at % 4, pair.unit, r)

                run_pairs(sp, name, body)

            def down(name, wt):
                ph = PH[name]

                def load(n, kt, r):
                    src = wt[bass.ds(settled(kt * P), P), :]
                    slot_free(n, r)
                    sp.dma_start(raw[:, n % RAW_SLOTS, :], src).then_inc(raw_full[n % RAW_SLOTS], 16)

                for j in range(4):
                    load(ph.n0 + j, j, 0)
                with sp.Fori(0, (FT - 4) // DOWN_BODY) as r:
                    for n, kind, at in down_items(ph):
                        if kind == "g":
                            load(n, r * DOWN_BODY + (at - ph.m0), r)
                        else:
                            load_mod(n, at % 4, ph.unit, r)

            def load_rest(name, wt, c0, cols):
                with nc.allow_non_contiguous_dma(reason="the last few columns of w_in"):
                    sp.dma_start(REST[name].rearrange("p (k n) -> p k n", k=KT),
                                 wt[:, c0:c0 + cols].rearrange("(k p) n -> p k n", p=P)).then_inc(sem(f"rest_{name}"), 16)

            def load_parameters():
                loads = [(con[:, C_LVL:C_N], consts[:, C_LVL:C_N])]
                for tile, name, r in ((1, "c_2", B_C), (1, "b_mod_2", B_MOD), (1, "ffn_post_w_2", B_FPOST), (0, "ffn_norm_g", A_FFN),
                                      (0, "pool_scale", A_PSC), (0, "mix_pre_w_2", A_MPRE), (0, "ffn_pre_w_2", A_FPRE),
                                      (0, "mix_post_w_2", A_MPOST), (0, "gate_b_2", A_GB), (0, "q_norm_g", A_QG), (0, "k_norm_g", A_KG),
                                      (0, "gla_norm_w_2", A_GLA)):
                    v = w[name].rearrange("(r p) -> r p", p=P)
                    loads.append((stage[r:r + v.shape[0], tile, :], v))
                loads.append((stage[A_CW:A_CW + 24, 0, :], w["conv_w_2"].rearrange("j (r p) -> (j r) p", p=P)))
                for j in range(3):
                    loads.append((stage[0:CONV_ROWS, (4, 5, 2)[j], :], w["conv_w"][j].rearrange("(r p) -> r p", p=P)))
                loads.append((stage[0:CONV_ROWS, 3, :], w["conv_b"].rearrange("(r p) -> r p", p=P)))
                for j in range(3):
                    loads.append((stage[0:CONV_ROWS, (7, 8, 6)[j], :], w["ffn_conv_w_2"][j].rearrange("(r p) -> r p", p=P)))
                assert len(loads) == N_SECOND
                for dst, src in loads:
                    sp.dma_start(dst, src).then_inc(sem("second_params"), 16)
                load_rest("in1", w["w_in"], IN1_REST, IDX_REST)
                sp.dma_start(pool_w, w["pool_w"].rearrange("g (c p) d -> p g c d", p=P)).then_inc(sem("pool_w_loaded"), 16)

            for t in range(TT):
                sp.dma_start(x[:, t, :], x_in[t * P:(t + 1) * P, :]).then_inc(sem(f"x_loaded{t}"), 16)
            pairs("in1", w["w_in"], lambda i, blk: IN1_STARTS[i] + BLOCK * blk, beside=load_parameters)
            pairs("out1", w["w_out"], lambda i, blk: 1024 * i + BLOCK * blk)
            pairs("up1", w["w_up"], lambda i, blk: BLOCK * i + F * blk, BLOCK)
            sp.wait_ge(sem("yT_pool_ready"), 8)
            sp.dma_start(gate_w2, w["gate_w2_2"]).then_inc(sem("gate_loaded"), 16)
            load_rest("in2", w["w_in_2"], IN2_REST, GATE_RANK)
            down("down1", w["w_down"])
            pairs("in2", w["w_in_2"], lambda i, blk: IN2_STARTS[i] + BLOCK * blk)
            pairs("out2", w["w_out_2"], lambda i, blk: 1024 * i + BLOCK * blk)
            pairs("up2", w["w_up_2"], lambda i, blk: BLOCK * i + F * blk, BLOCK)
            down("down2", w["w_down_2"])
            for t in range(TT):
                for half in range(2):
                    cols = slice(D // 2 * half, D // 2 * (half + 1))
                    sp.wait_ge(sem("x_new"), 5 + 2 * t + half)
                    sp.dma_start(out[t * P:(t + 1) * P, cols], x[:, t, cols]).then_inc(sem("stored"), 16)
            sp.wait_ge(sem("stored"), 16 * 2 * TT)

        @block.scalar
        def _(act):
            seq = [0]

            def link(ins):
                seq[0] += 1
                ins.then_inc(sem("act_step"), 1)
                act.wait_ge(sem("act_step"), seq[0])

            def round_half(m, half, r=0, raw_add=0):
                n, hh = RAW_OF[m], 2 * m + half
                if half == 0:
                    act.wait_ge(raw_full[n % RAW_SLOTS], 16 * (n // RAW_SLOTS + 1) + r * raw_add)
                if hh >= HL_SLOTS:
                    act.wait_ge(w_used, hh - HL_SLOTS + 1 + r * 16)
                nc.scalar.activation(w_hi[:, hh % HL_SLOTS, :], raw[:, n % RAW_SLOTS, half * HALF:(half + 1) * HALF],
                                     ACT.Copy).then_inc(hi_ready, 1)

            def rest_rounds(name, cols):
                act.wait_ge(sem(f"rest_{name}"), 16)
                n_el = KT * cols // 2
                for half in range(2):
                    hh = 2 * PH[name].rest + half
                    act.wait_ge(w_used, hh - HL_SLOTS + 1)
                    nc.scalar.activation(w_hi[:, hh % HL_SLOTS, 0:n_el], REST[name][:, half * n_el:(half + 1) * n_el],
                                         ACT.Copy).then_inc(hi_ready, 1)

            def lead(name, halves=range(4)):
                for h in halves:
                    round_half(PH[name].m0 + h // 2, h % 2)

            def pairs(name, epi, narrow=0, between=None, late=None):
                ph = PH[name]

                def body(i0, i, r, layout):
                    pair = ph.pairs[i0]
                    for c in range(8):
                        if i0 > 0 or c >= 2:
                            for half in range(2):
                                round_half(pair.m0 + c, half, r, raw_stride(pair))
                        if c == 1 and i0 > 0:
                            epi(ph, 1, i0 - 1, i - 1, r)
                        if c == 5:
                            epi(ph, 0, i0, i, r)
                        if between:
                            between(8 * i0 + c)
                    if late:
                        late(ph, i0, r)
                    if narrow and i0 == 0:
                        rest_rounds(name, narrow)

                run_pairs(act, name, body)

            def last_epi(name, epi):
                i = RUNS[name][-1][1] - 1
                epi(PH[name], 1, i, i, 0)

            def norm_sums(p):
                flat = xt.rearrange("p k s -> p (k s)")
                if p == 0:
                    act.wait_ge(sem("x_loaded0"), 16)
                else:
                    act.wait_ge(sem("x_new"), 2 * (p - 2) + 1)
                nc.scalar.activation(flat[:, 0:D], x[:, 0, :], ACT.Square, accum_out=sm(SS + 2 * p)).then_inc(sem("sq_done"), 1)
                if p == 0:
                    act.wait_ge(sem("x_loaded1"), 16)
                elif p == 2:
                    act.wait_ge(sem("x_new"), 2)
                else:
                    act.wait_ge(sem("x_new_pool"), 1)
                nc.scalar.activation(flat[:, D:D + D // 2], x[:, 1, D // 2:], ACT.Square,
                                     accum_out=sm(SS_HALF + p)).then_inc(sem("sq_done"), 1)

            def residual_sums(j):
                act.wait_ge(epi_done, blocks_before("out1") + j + 1)
                flat = xt.rearrange("p k s -> p (k s)")
                for t in range(1 if j == 3 else TT):
                    at = BLOCK * (2 * j + t)
                    nc.scalar.activation(flat[:, at:at + BLOCK], x[:, t, BLOCK * j:BLOCK * (j + 1)], ACT.Square,
                                         accum_out=sm(P_SS + 4 * t + j)).then_inc(sem("sq_done"), 1)

            def norm(p, name, halves, before=None):
                act.wait_ge(sem("ms_ready"), p + 1)
                nc.scalar.activation(sm(SD + 2 * p, 2), sm(MS + 2 * p, 2), ACT.Sqrt).then_inc(sem("sd_ready"), 1)
                act.wait_ge(sem("rstd_ready"), p + 1)
                for half in range(2):
                    cols = slice(D // 2 * half, D // 2 * (half + 1))
                    nc.scalar.activation(hn[:, 1, cols], x[:, 1, cols], ACT.Copy, scale=sm(RSTD + 2 * p + 1)).then_inc(sem("hn_act"), 1)
                if before:
                    before()
                for k in range(KT // 2):
                    act.wait_ge(sem("xt_ready"), KT * p + 2 * k + 2)
                    nc.scalar.activation(a_hi[:, 2 * k:2 * k + 2, :], xt[:, 2 * k:2 * k + 2, :], ACT.Copy).then_inc(act_hi, 1)
                    if k in halves:
                        lead(name, (halves[k],))

            def split_mixed(src, kts):
                for k in kts:
                    at = 2 * (k % 4)
                    nc.scalar.activation(a_hi[:, 2 * k:2 * k + 2, :], src[:, at:at + 2, :], ACT.Copy).then_inc(act_hi, 1)

            def epi_z(ph, blk, i0, i, r):
                act.wait_ge(w_used, block_end(ph, i0, blk) + 16 * r)
                nc.scalar.activation(z[:, bass.ds(2 * i + blk, 1), :].rearrange("p b n -> p (b n)"), main(blk),
                                     ACT.Copy).then_inc(epi_done, 1)

            def epi_none(ph, blk, i0, i, r):
                pass

            def epi_conv(layer, q):
                def epi(ph, blk, i0, i, r):
                    dst = (c_gate, c_val)[blk]
                    act.wait_ge(w_used, block_end(ph, i0, blk) + 16 * r)
                    if q + i0 > 0:
                        act.wait_ge(sem("g_done"), q * PAIRS_UP + i0 + r)
                    last = 2 if layer == 1 else 6
                    for f in range(4):
                        tap = col[:, last, bass.ds(4 * i + f + FT * blk, 1)]
                        bias = col[:, 3, bass.ds(4 * i + f + FT * blk, 1)] if layer == 1 else 0.0
                        nc.scalar.activation(dst[:, f, :], main(blk)[:, S * f:S * (f + 1)], ACT.Identity, bias=bias,
                                             scale=tap).then_inc(sem("conv_first"), 1)
                return epi

            def gate_silu(ph, i0, r):
                act.wait_ge(epi_done, ph.pairs[i0].b0 + 1 + 2 * r)
                nc.scalar.activation(c_gate, c_gate, ACT.Silu).then_inc(sem("silu_done"), 1)

            def down(name, q, epi_prev):
                ph = PH[name]

                def split_g(j, kt):
                    nc.scalar.activation(a_hi[:, j % 4, :], g[:, bass.ds(kt, 1), :].rearrange("p f s -> p (f s)"),
                                         ACT.Copy).then_inc(sem("g_hi"), 1)

                act.wait_ge(w_used, 2 * (BEFORE_DOWN[name].m0 + 5))
                act.wait_ge(sem("g_done"), PAIRS_UP * q + 1)
                for j in range(4):
                    split_g(j, j)
                lead(name, range(3))
                epi_prev()
                lead(name, range(3, 4))
                for j in range(2, 4):
                    for half in range(2):
                        round_half(ph.m0 + j, half)
                act.wait_ge(sem("g_done"), PAIRS_UP * (q + 1))
                with act.Fori(0, (FT - 4) // DOWN_BODY) as r:
                    for j in range(DOWN_BODY):
                        act.wait_ge(w_used, 2 * (ph.m0 + j + 1) + 16 * r)
                        split_g(j, r * DOWN_BODY + (4 + j))
                        for half in range(2):
                            round_half(ph.m0 + 4 + j, half, r, 32 if ph.unit is None else 48)

            loads = [(con[:, 0:C_LVL], consts[:, 0:C_LVL]),
                     (stage[A_ATTN:A_ATTN + KT, 0, :], w["attn_norm_g"].rearrange("(r p) -> r p", p=P))]
            assert len(loads) == N_FIRST
            for dst, src in loads:
                act.dma_start(dst, src).then_inc(sem("first_params"), 16)
            def load_table(n):
                nc.scalar.activation(sm(SPARE + n), ones[:, 0:1], ACT.Sqrt)

            def first_columns():
                act.wait_ge(sem("cols_turned"), 1)
                nc.scalar.activation(col[:, 0, 0:KT], main(0)[:, 0:KT], ACT.Copy).then_inc(sem("cols_ready"), 1)
                lead("in1", range(1))

            def all_columns():
                act.wait_ge(sem("cols_turned"), 2)
                nc.scalar.activation(col[:, 0, KT:A_ROWS], side(0)[:, KT:A_ROWS], ACT.Copy).then_inc(sem("cols_ready"), 1)
                nc.scalar.activation(col[:, 1, :], side(0)[:, P:2 * P], ACT.Copy).then_inc(sem("cols_ready"), 1)
                nc.scalar.activation(col[:, 2:9, 0:CONV_ROWS],
                                     ps[:, SIDE + 2 * P:SIDE + 9 * P].rearrange("p (n r) -> p n r", n=7)[:, :, 0:CONV_ROWS],
                                     ACT.Copy).then_inc(sem("cols_ready"), 1)
                act.wait_ge(sem("cols_ready"), 4)
                nc.scalar.activation(sm(C_ACT, KT), colB(B_C, KT), ACT.Silu).then_inc(sem("c_act"), 1)

            act.wait_ge(sem("first_params"), 16 * N_FIRST)
            load_table(0)
            norm_sums(0)
            norm(0, "in1", {1: 1, 3: 2, 5: 3}, first_columns)

            def rest1_out():
                act.wait_ge(w_used, 2 * (PH["in1"].rest + 1))
                for half in range(2):
                    nc.scalar.activation(kidxT[IDX_DIM * half:IDX_DIM * (half + 1), :], side(0)[0:IDX_DIM, 0:S],
                                         ACT.Copy).then_inc(sem("kidxT_ready"), 1)
                nc.scalar.activation(widxT, side(0)[IDX_DIM:IDX_REST, 0:S], ACT.Copy,
                                     scale=IDX_HEADS ** -0.5 * IDX_DIM ** -0.5).then_inc(sem("widxT_ready"), 1)

            def rectify(n):
                K = P * (n // 8 + 1)
                act.wait_ge(sem("is_done"), n + 1)
                if n >= 2:
                    act.wait_ge(sem("relu_used"), n - 1)
                nc.scalar.activation(relu_buf[:, n % 2, :, 0:K], side(n % 3).rearrange("p (j s) -> p j s", j=2)[:, :, 0:K],
                                     ACT.Relu).then_inc(sem("relu_ready"), 1)

            def qk_out(n):
                dst, wcol = ((kT, colA(A_KG)), (qT, colA(A_QG)))[n // 4]
                b, t = divmod(n % 4, 2)
                act.wait_ge(sem("qk_turned"), n + 1)
                nc.scalar.activation(dst[:, 4 * b:4 * b + 4, t * P:(t + 1) * P], side(n % 3).rearrange("p (h s) -> p h s", h=4),
                                     ACT.Copy, scale=wcol).then_inc(sem("qkT_ready"), 1)

            def soft_exp(u):
                t, h0, nh, K = attention_unit(u)
                s = sc_buf[:, u % 2, 0:nh * K]
                act.wait_ge(sem("sm_ready"), u + 1)
                nc.scalar.activation(s, s, ACT.Exp, scale=HD ** -0.5).then_inc(sem("p_exp"), 1)

            def probs_out(u):
                act.wait_ge(sem("p_turned"), u + 1)
                nc.scalar.activation(pT[u], side(u % 3), ACT.Copy).then_inc(sem("pT_ready"), 1)

            def attn_out(n):
                t, hg, b, _ = ATTEND[n]
                act.wait_ge(sem("pv_done"), n + 1)
                nc.scalar.activation(yT_attn[:, 4 * hg:4 * hg + 4, t * P:(t + 1) * P], side(b).rearrange("p (h s) -> p h s", h=4),
                                     ACT.Copy).then_inc(sem("yT_attn_ready"), 1)

            def pool_out(e):
                act.wait_ge(sem("pool_mixed"), e + 1)
                for f in (2 * e, 2 * e + 1):
                    nc.scalar.activation(yT_pool[:, f, :], side(3)[:, S * (f % 2):S * (f % 2 + 1)], ACT.Copy,
                                         scale=colA(A_PSC + f)).then_inc(sem("yT_pool_ready"), 1)

            def mixer1(at):
                if at == 5:
                    all_columns()
                if at == 10:
                    rest1_out()
                if at == 12:
                    act.wait_ge(sem("widx_turned"), 1)
                    nc.scalar.activation(sm(WIDX, TT * IDX_HEADS), side(2, TT * IDX_HEADS), ACT.Copy).then_inc(sem("widx_ready"), 1)
                if 13 <= at < 21:
                    rectify(2 * (at - 13))
                    rectify(2 * (at - 13) + 1)
                if at in (18, 25):
                    n = (at - 18) // 7
                    act.wait_ge(epi_done, 4 + 2 * n)
                    nc.scalar.activation((kT, qT)[n].rearrange("p h s -> p (h s)"), reg(2048 + 2048 * n, 2048),
                                         ACT.Square).then_inc(sem("qk_sq"), 1)
                if at in (20, 27):
                    n = (at - 20) // 7
                    act.wait_ge(sem("qk_ms"), n + 1)
                    nc.scalar.activation(sm(QK_SD + 16 * n, 16), sm(QK_SS + 16 * n, 16), ACT.Sqrt).then_inc(sem("qk_sd"), 1)
                for n in {24: (0, 1), 25: (2, 3), 30: (4, 5, 6), 32: (7,)}.get(at, ()):
                    qk_out(n)
                for u in {35: (0, 1), 38: (2,), 39: (3,)}.get(at, ()):
                    probs_out(u)
                for u in {34: (0, 1), 36: (2,), 38: (3,), 39: (4,)}.get(at, ()):
                    soft_exp(u)
                if at == 39:
                    pool_out(0)

            pairs("in1", epi_z, IDX_REST, mixer1)
            lead("out1", range(3))
            soft_exp(5)
            probs_out(4)
            attn_out(0)
            last_epi("in1", epi_z)
            pool_out(1)
            attn_out(1)
            pool_out(2)
            probs_out(5)
            attn_out(2)
            pool_out(3)
            act.wait_ge(w_used, 2 * PH["out1"].m0)
            act.wait_ge(sem("yT_pool_ready"), 8)
            split_mixed(yT_pool, range(0, 4))
            attn_out(3)
            lead("out1", range(3, 4))
            act.wait_ge(sem("yT_attn_ready"), 4)
            split_mixed(yT_attn, range(4, 8))

            def block_sums(at):
                if at in (7, 11, 15):
                    residual_sums((at - 7) // 4)
                if at == 15:
                    load_table(1)

            pairs("out1", epi_none, between=block_sums)
            lead("up1", range(2))
            residual_sums(3)
            norm(1, "up1", {1: 2, 3: 3})
            pairs("up1", epi_conv(1, 0), late=gate_silu)
            down("down1", 0, lambda: last_epi("up1", epi_conv(1, 0)))

            lead("in2", range(2))
            load_table(2)
            norm_sums(2)
            norm(2, "in2", {1: 2, 3: 3})
            xg, ta = head_tok(A1), head_tok(A2)
            r_gate = reg(4096, 2048)

            def mixer2(at):
                if at == 10:
                    act.wait_ge(w_used, 2 * (PH["in2"].rest + 1))
                    nc.scalar.activation(a_lrT, side(0)[0:GATE_RANK, 0:S], ACT.Copy).then_inc(sem("alrT_ready"), 1)
                if at == 14:
                    act.wait_ge(sem("gate_mm"), 1)
                    for h in range(GLA_HEADS):
                        nc.scalar.activation(xg[:, h, :], ps[:, SIDE + S * h:SIDE + S * (h + 1)], ACT.Identity,
                                             bias=colA(A_GB + h)).then_inc(sem("xg_ready"), 1)
                if at == 15:
                    act.wait_ge(sem("xg_ready"), 4)
                    link(nc.scalar.activation(ta, xg, ACT.Abs))
                    link(nc.scalar.activation(ta, ta, ACT.Exp, scale=-1.0))
                    nc.scalar.activation(ta, ta, ACT.Ln, bias=ones[:, 0:1]).then_inc(sem("ln_ready"), 1)
                if at == 18:
                    act.wait_ge(sem("b_ready"), 1)
                    nc.scalar.activation(head_tok(A1), head_tok(A4), ACT.Exp).then_inc(sem("eb_ready"), 1)
                    nc.scalar.activation(sm(E_LAST, 16), reg(A4, 1024).rearrange("p (c s) -> p c s", s=CHUNK)[:, :, CHUNK - 1],
                                         ACT.Exp).then_inc(sem("e_last"), 1)
                if at == 19:
                    act.wait_ge(sem("kd_diff"), 1)
                    nc.scalar.activation(reg(A3, 1024), reg(A3, 1024), ACT.Exp, scale=-1.0).then_inc(sem("kd_exp"), 1)
                if at == 22:
                    act.wait_ge(sem("kd_turned"), 1)
                    nc.scalar.activation(reg(A6, 1024), ps[:, SIDE:SIDE + 1024], ACT.Copy).then_inc(sem("kdT_ready"), 1)
                if at >= 24 and at % 2 == 0 and (at - 24) // 2 < len(LEVELS):
                    act.wait_ge(sem("lvl_diff"), (at - 24) // 2 + 1)
                    link(nc.scalar.activation(reg(A1, 1024), reg(A1, 1024), ACT.Abs))
                    nc.scalar.activation(reg(A1, 1024), reg(A1, 1024), ACT.Exp, scale=-1.0).then_inc(sem("lvl_exp"), 1)
                if at == 37:
                    act.wait_ge(epi_done, blocks_before("in2") + 6)
                    nc.scalar.activation(r_gate, r_gate, ACT.Silu).then_inc(sem("r_silu"), 1)
                if at in (39, 43):
                    b = (at - 39) // 4
                    act.wait_ge(sem("ccx_ready"), b + 1)
                    for f in range(4 * b, 4 * b + 4):
                        nc.scalar.activation(cx[:, f, :], cc[:, f, :], ACT.Copy, scale=colA(A_CW + 16 + f)).then_inc(sem("mix_tap"), 1)
                if at == 41:
                    act.wait_ge(sem("o_done"), 1)
                    nc.scalar.activation(o_gla.rearrange("p t h e -> p (t h e)"), ps[:, SIDE:SIDE + 2048],
                                         ACT.Copy).then_inc(sem("o_out"), 1)
                    act.wait_ge(sem("o_out"), 1)
                    nc.scalar.activation(reg(A4, 2048), o_gla.rearrange("p t h e -> p (t h e)"), ACT.Square).then_inc(sem("o_sq"), 1)
                if at == 44:
                    act.wait_ge(sem("o_ms"), 1)
                    nc.scalar.activation(sm(O_SD, 8), sm(O_SS, 8), ACT.Sqrt).then_inc(sem("o_sd"), 1)
                if at == 47:
                    act.wait_ge(sem("o_turned"), 1)
                    for f in range(8):
                        nc.scalar.activation(yT_gla[:, f, :], ps[:, SIDE + S * f:SIDE + S * (f + 1)], ACT.Copy,
                                             scale=colA(A_GLA + f % 2)).then_inc(sem("yT_gla_ready"), 1)

            pairs("in2", epi_z, GATE_RANK, mixer2)
            lead("out2", range(3))
            act.wait_ge(w_used, 2 * PH["out2"].m0)
            act.wait_ge(sem("yT_gla_ready"), 8)
            split_mixed(yT_gla, range(4, 8))
            last_epi("in2", epi_z)
            lead("out2", range(3, 4))
            for b in range(2):
                act.wait_ge(sem("yT_conv_ready"), b + 1)
                split_mixed(yT_conv, range(2 * b, 2 * b + 2))

            def gate_row(q):
                act.wait_ge(sem("row_mm"), q + 1)
                nc.scalar.activation(g_row, ps[:, SIDE:SIDE + 2048], ACT.Copy).then_inc(sem("row_ready"), 1)

            def post_sd():
                act.wait_ge(sem("post_ms"), 1)
                nc.scalar.activation(sm(P_SD, 2), sm(P_SS, 2), ACT.Sqrt).then_inc(sem("post_sd"), 1)

            def epi_sums(ph, blk, i0, i, r):
                act.wait_ge(w_used, block_end(ph, i0, blk))
                j = 2 * i0 + blk
                for t in range(TT):
                    nc.scalar.activation(xt.rearrange("p k s -> p (k s)")[:, BLOCK * (2 * j + t):BLOCK * (2 * j + t + 1)],
                                         main(blk)[:, BLOCK * t:BLOCK * (t + 1)], ACT.Square,
                                         accum_out=sm(P_SS + 4 * t + j)).then_inc(sem("post_sq"), 1)

            def first_row(at):
                if at == 5:
                    gate_row(0)

            pairs("out2", epi_sums, between=first_row)
            lead("up2", range(2))
            last_epi("out2", epi_sums)
            post_sd()
            act.wait_ge(sem("post_rstd"), 1)
            act.wait_ge(epi_done, blocks_before("up2"))
            nc.scalar.activation(y[:, 1, D // 2:], y[:, 1, D // 2:], ACT.Copy, scale=sm(P_RSTD + 1)).then_inc(sem("y_scaled"), 1)
            norm_sums(3)
            norm(3, "up2", {1: 2, 3: 3})

            def last_row(at):
                if at == 39:
                    gate_row(1)

            pairs("up2", epi_conv(2, 1), between=last_row, late=gate_silu)
            down("down2", 1, lambda: last_epi("up2", epi_conv(2, 1)))
            load_table(3)
            for t in range(TT):
                act.wait_ge(sem("first_tokens"), 2) if t == 0 else act.wait_ge(w_used, down_end("down2"))
                for half in range(2):
                    if half:
                        act.wait_ge(sem("yg_ready"), 2 * t + 1)
                    at = D * t + D // 2 * half
                    nc.scalar.activation(xt.rearrange("p k s -> p (k s)")[:, at:at + D // 2], ps[:, at:at + D // 2], ACT.Square,
                                         accum_out=sm(P_SS + 4 * t + half)).then_inc(sem("post_sq"), 1)
                act.wait_ge(sem("post_ms"), 2 + t)
                nc.scalar.activation(sm(P_SD + 2 + t), sm(P_SS + 4 * t + 3), ACT.Sqrt).then_inc(sem("post_sd"), 1)

        @block.vector
        def _(dve):
            v = nc.vector
            seq = [0]

            def link(ins):
                seq[0] += 1
                ins.then_inc(sem("dve_step"), 1)
                dve.wait_ge(sem("dve_step"), seq[0])

            def low_half(m, half, r=0):
                n, hh = RAW_OF[m], 2 * m + half
                dve.wait_ge(hi_ready, hh + 1 + r * 16)
                v.tensor_tensor(w_lo[:, hh % HL_SLOTS, :], raw[:, n % RAW_SLOTS, half * HALF:(half + 1) * HALF],
                                w_hi[:, hh % HL_SLOTS, :].bitcast(F32), ALU.subtract).then_inc(lo_ready, 1)

            def rest_lows(name, cols):
                n_el = KT * cols // 2
                for half in range(2):
                    hh = 2 * PH[name].rest + half
                    dve.wait_ge(hi_ready, hh + 1)
                    v.tensor_tensor(w_lo[:, hh % HL_SLOTS, 0:n_el], REST[name][:, half * n_el:(half + 1) * n_el],
                                    w_hi[:, hh % HL_SLOTS, 0:n_el].bitcast(F32), ALU.subtract).then_inc(lo_ready, 1)

            def lead(name, halves=range(4)):
                for h in halves:
                    low_half(PH[name].m0 + h // 2, h % 2)

            def mod_chunk(acc, k, r):
                n, c = RAW_OF_MOD[k], k % 4
                dve.wait_ge(raw_full[n % RAW_SLOTS], 16 * (n // RAW_SLOTS + 1) + r * 48)
                part = raw[:, n % RAW_SLOTS, :].rearrange("p (k n) -> p k n", k=KC)
                for kk in range(KC):
                    kt = KC * c + kk
                    step = UNIT_OPS * (k // 4) + kt
                    if kt == 0:
                        v.tensor_scalar(acc, part[:, 0, :], sm(C_ACT), None, ALU.mult).then_inc(mod_step, 1)
                    else:
                        dve.wait_ge(mod_step, step + r * UNIT_OPS)
                        v.scalar_tensor_tensor(out=acc, in0=part[:, kk, :], scalar=sm(C_ACT + kt), in1=acc,
                                               op0=ALU.mult, op1=ALU.add).then_inc(mod_step, 1)

            def mod_columns(u):
                dve.wait_ge(mod_red, u + 1)
                v.tensor_tensor(modc[:, bass.ds(u * 4, 4)], side(3)[:, 508:512], col[:, 1, bass.ds(u * 4 + B_MOD, 4)],
                                ALU.add).then_inc(sem("modc_ready"), 1)

            def pairs(name, epi, narrow=0, between=None):
                ph = PH[name]

                def body(i0, i, r, layout):
                    pair = ph.pairs[i0]
                    for n, kind, at in pair_items(pair):
                        if kind == "m":
                            mod_chunk(mod_acc[:], at, r)
                            continue
                        c = at - pair.m0
                        if i0 > 0 or c >= 2:
                            for half in range(2):
                                low_half(at, half, r)
                        if c == 2 and i0 > 0:
                            if ph.pairs[i0 - 1].unit is not None:
                                mod_columns(ph.pairs[i0 - 1].unit + r)
                            epi(ph, 1, i0 - 1, i - 1, r)
                        if c == 6:
                            epi(ph, 0, i0, i, r)
                        if between:
                            between(8 * i0 + c)
                    if narrow and i0 == 0:
                        rest_lows(name, narrow)

                run_pairs(dve, name, body)

            def last_epi(name, epi):
                i = RUNS[name][-1][1] - 1
                epi(PH[name], 1, i, i, 0)

            def last_unit(name):
                mod_columns(PH[name].pairs[-1].unit)

            def norm_sums(p):
                flat = xt.rearrange("p k s -> p (k s)")

                def squares(cols, at, total):
                    v.scalar_tensor_tensor(out=flat[:, at:at + cols.stop - cols.start], in0=x[:, 1, cols], scalar=1.0, in1=x[:, 1, cols],
                                           op0=ALU.mult, op1=ALU.mult, accum_out=total).then_inc(sem("sq_done"), 1)

                if p == 1:
                    dve.wait_ge(epi_done, blocks_before("up1"))
                    squares(slice(D - BLOCK, D), 7 * BLOCK, sm(P_SS + 7))
                    dve.wait_ge(sem("sq_done"), SQUARES[1])
                    link(v.tensor_reduce(sm(SS + 2, 2), sm(P_SS, 8).rearrange("p (t j) -> p t j", t=TT), AX_X, ALU.add))
                else:
                    if p == 0:
                        dve.wait_ge(sem("x_loaded1"), 16)
                    else:
                        dve.wait_ge(sem("x_new"), 2 * (p - 1))
                    squares(slice(0, D // 2), D + D // 2, sm(SS + 2 * p + 1))
                    dve.wait_ge(sem("sq_done"), SQUARES[p])
                    link(v.tensor_tensor(sm(SS + 2 * p + 1), sm(SS + 2 * p + 1), sm(SS_HALF + p), ALU.add))
                v.tensor_scalar(sm(MS + 2 * p, 2), sm(SS + 2 * p, 2), 1.0 / D, EPS, ALU.mult, ALU.add).then_inc(sem("ms_ready"), 1)

            def norm(p, name, halves, scale, shift=None, before=None):
                f = FILL[name]
                dve.wait_ge(sem("sd_ready"), p + 1)
                v.reciprocal(sm(RSTD + 2 * p, 2), sm(SD + 2 * p, 2)).then_inc(sem("rstd_ready"), 1)
                dve.wait_ge(sem("rstd_ready"), p + 1)
                for half in range(2):
                    cols = slice(D // 2 * half, D // 2 * (half + 1))
                    v.tensor_scalar(hn[:, 0, cols], x[:, 0, cols], sm(RSTD + 2 * p), None, ALU.mult).then_inc(sem("hn_dve"), 1)

                def lows(k):
                    dve.wait_ge(act_hi, 8 * f + k + 1)
                    v.tensor_tensor(a_lo[:, 2 * k:2 * k + 2, :], xt[:, 2 * k:2 * k + 2, :],
                                    a_hi[:, 2 * k:2 * k + 2, :].bitcast(F32), ALU.subtract).then_inc(act_ready, 1)

                if before:
                    before()
                for k in range(KT // 2):
                    dve.wait_ge(sem("turned"), 8 * p + k + 1)
                    for kk in range(2):
                        kt = 2 * k + kk
                        add = (None, ALU.bypass) if shift is None else (shift[:, kt:kt + 1], ALU.add)
                        v.tensor_scalar(xt[:, kt, :], turn_bank(k)[:, S * kk:S * (kk + 1)], scale[:, kt:kt + 1], add[0],
                                        ALU.mult, add[1]).then_inc(sem("xt_ready"), 1)
                    if k:
                        lows(k - 1)
                    if k in halves:
                        lead(name, (halves[k],))
                lows(KT // 2 - 1)

            def split_mixed(name, src, kts, done):
                for n, k in enumerate(kts):
                    at = 2 * (k % 4)
                    dve.wait_ge(act_hi, 8 * FILL[name] + done + n + 1)
                    v.tensor_tensor(a_lo[:, 2 * k:2 * k + 2, :], src[:, at:at + 2, :], a_hi[:, 2 * k:2 * k + 2, :].bitcast(F32),
                                    ALU.subtract).then_inc(act_ready, 1)

            def epi_none(ph, blk, i0, i, r):
                pass

            def epi_residual(ph, blk, i0, i, r):
                dve.wait_ge(w_used, block_end(ph, i0, blk))
                j = 2 * i0 + blk
                xs = x[:, :, BLOCK * j:BLOCK * (j + 1)]
                v.tensor_tensor(xs, main(blk).rearrange("p (t n) -> p t n", t=TT), xs, ALU.add).then_inc(epi_done, 1)

            def epi_conv(layer, q):
                rows = (4, 5) if layer == 1 else (7, 8)

                def epi(ph, blk, i0, i, r):
                    dst = (c_gate, c_val)[blk]
                    n = q * 2 * PAIRS_UP + 2 * i0 + blk
                    dve.wait_ge(sem("conv_first"), 4 * n + 4 + 8 * r)
                    for j, shift in ((1, 1), (0, 2)):
                        if j == 0:
                            dve.wait_ge(sem("conv_second"), 4 * n + 4 + 8 * r)
                        for f in range(4):
                            tap = col[:, rows[j], bass.ds(4 * i + f + FT * blk, 1)]
                            ins = v.scalar_tensor_tensor(
                                out=dst[:, f, shift:], in0=main(blk)[:, S * f:S * (f + 1) - shift], scalar=tap, in1=dst[:, f, shift:],
                                op0=ALU.mult, op1=ALU.add)
                            if j == 1:
                                ins.then_inc(sem("conv_second"), 1)
                            elif f == 3:
                                ins.then_inc(epi_done, 1)
                return epi

            def down(name, q, epi_prev):
                ph = PH[name]

                def split_g(j, kt, r):
                    dve.wait_ge(sem("g_hi"), FT * q + j + 1 + DOWN_BODY * r)
                    v.tensor_tensor(a_lo[:, j % 4, :], g[:, bass.ds(kt, 1), :].rearrange("p f s -> p (f s)"),
                                    a_hi[:, j % 4, :].bitcast(F32), ALU.subtract).then_inc(sem("g_split"), 1)

                for j in range(4):
                    split_g(j, j, 0)
                lead(name, range(3))
                epi_prev()
                lead(name, range(3, 4))
                for j in range(2, 4):
                    for half in range(2):
                        low_half(ph.m0 + j, half)
                with dve.Fori(0, (FT - 4) // DOWN_BODY) as r:
                    for n, kind, at in down_items(ph):
                        if kind == "m":
                            mod_chunk(region[:, bass.ds(r * BLOCK + DOWN_ACC, BLOCK)], at, r)
                            continue
                        split_g(at - ph.m0, r * DOWN_BODY + (at - ph.m0), r)
                        for half in range(2):
                            low_half(at, half, r)

            norm_sums(0)

            def first_columns():
                lead("in1", range(1))
                dve.wait_ge(sem("cols_ready"), 1)

            norm(0, "in1", {2: 1, 4: 2, 6: 3}, colA(A_ATTN, KT), None, first_columns)

            def index_sum(n):
                t, b = divmod(n, 8)
                K = P * (t + 1)
                dve.wait_ge(sem("relu_ready"), n + 1)
                for j in range(2):
                    h = 4 * (b // 2) + b % 2 + 2 * j
                    wcol = sm(WIDX + IDX_HEADS * t + h)
                    rel = relu_buf[:, n % 2, j, 0:K]
                    if b + j == 0:
                        link(v.tensor_scalar(iscore[:, t, 0:K], rel, wcol, None, ALU.mult))
                        continue
                    ins = v.scalar_tensor_tensor(out=iscore[:, t, 0:K], in0=rel, scalar=wcol, in1=iscore[:, t, 0:K],
                                                 op0=ALU.mult, op1=ALU.add)
                    if j == 0:
                        link(ins)
                    else:
                        ins.then_inc(sem("relu_used"), 1)
                        dve.wait_ge(sem("relu_used"), n + 1)

            def reach(t):
                K = P * (t + 1)
                last = iscore[:, t, t * P:(t + 1) * P]
                link(v.tensor_tensor(last, last, tri, ALU.add))
                link(v.tensor_copy(work[:, t, 0:K], iscore[:, t, 0:K]))

            def best(t, rounds):
                K = P * (t + 1)
                for k in rounds:
                    link(v.max(top8[:, 8 * t + k, :], work[:, t, 0:K]))
                    link(v.match_replace(work[:, t, 0:K], top8[:, 8 * t + k, :], work[:, t, 0:K], NEG))

            def left(t):
                K = P * (t + 1)
                link(v.tensor_tensor(notsel[:, t, 0:K], iscore[:, t, 0:K], work[:, t, 0:K], ALU.is_equal))

            def soft_shift(u):
                t, h0, nh, K = attention_unit(u)
                s = sc_buf[:, u % 2, 0:nh * K].rearrange("p (h s) -> p h s", h=nh)
                dve.wait_ge(sem("sc_done"), u + 1)
                if u >= 2:
                    dve.wait_ge(sem("p_turned"), u - 1)
                link(v.scalar_tensor_tensor(out=s, in0=notsel[:, t, 0:K].unsqueeze(1).to_broadcast([P, nh, K]), scalar=NEG,
                                            in1=side(u % 3).rearrange("p (h s) -> p h s", h=nh), op0=ALU.mult, op1=ALU.add))
                link(v.tensor_reduce(sm(MX, nh), s, AX_X, ALU.max))
                v.tensor_tensor(s, s, sm(MX, nh).unsqueeze(2).to_broadcast([P, nh, K]), ALU.subtract).then_inc(sem("sm_ready"), 1)

            def soft_norm(u):
                t, h0, nh, K = attention_unit(u)
                s = sc_buf[:, u % 2, 0:nh * K].rearrange("p (h s) -> p h s", h=nh)
                dve.wait_ge(sem("p_exp"), u + 1)
                link(v.tensor_reduce(sm(RSUM, nh), s, AX_X, ALU.add))
                link(v.reciprocal(sm(RINV, nh), sm(RSUM, nh)))
                v.tensor_tensor(s, s, sm(RINV, nh).unsqueeze(2).to_broadcast([P, nh, K]), ALU.mult).then_inc(sem("p_ready"), 1)

            def mixer1(at):
                if at == 7:
                    dve.wait_ge(sem("c_act"), 1)
                if 14 <= at < 22:
                    index_sum(2 * (at - 14))
                    index_sum(2 * (at - 14) + 1)
                if at == 22:
                    reach(0)
                    best(0, range(3))
                if at == 23:
                    best(0, range(3, TOP_ROUNDS))
                    left(0)
                if at == 24:
                    reach(1)
                    best(1, range(1))
                if at in (19, 26):
                    n = (at - 19) // 7
                    dve.wait_ge(sem("qk_sq"), n + 1)
                    src = (kT, qT)[n].rearrange("p h s -> p (h s)").rearrange("p (n d) -> p n d", d=HD)
                    ss = sm(QK_SS + 16 * n, 16)
                    link(v.tensor_reduce(ss, src, AX_X, ALU.add))
                    v.tensor_scalar(ss, ss, 1.0 / HD, EPS, ALU.mult, ALU.add).then_inc(sem("qk_ms"), 1)
                if at in (21, 27):
                    n = (at - 21) // 6
                    dve.wait_ge(sem("qk_sd"), n + 1)
                    v.reciprocal(sm(QK_SS + 16 * n, 16), sm(QK_SD + 16 * n, 16)).then_inc(sem("qk_rstd"), 1)
                if at in (25, 27, 28):
                    first = {25: 1, 27: 3, 28: 5}[at]
                    best(1, range(first, first + 2))
                if at == 29:
                    best(1, range(7, TOP_ROUNDS))
                    left(1)
                for u in {34: (0, 1), 36: (2,), 38: (3,), 39: (4,)}.get(at, ()):
                    soft_norm(u)
                for u in {33: (0, 1), 35: (2,), 37: (3,), 38: (4,)}.get(at, ()):
                    soft_shift(u)

            pairs("in1", epi_none, IDX_REST, mixer1)
            lead("out1", range(3))
            soft_shift(5)
            soft_norm(5)
            split_mixed("out1", yT_pool, range(0, 4), 0)
            lead("out1", range(3, 4))
            split_mixed("out1", yT_attn, range(4, 8), 4)

            pairs("out1", epi_residual)
            lead("up1", range(2))
            last_epi("out1", epi_residual)
            norm_sums(1)
            last_unit("out1")
            norm(1, "up1", {2: 2, 4: 3}, colA(A_FFN, KT))
            pairs("up1", epi_conv(1, 0))
            down("down1", 0, lambda: last_epi("up1", epi_conv(1, 0)))

            def scales(at, wcols, first):
                dve.wait_ge(sem("modc_ready"), first // 4 + 4)
                link(v.scalar_tensor_tensor(out=sm(at, KT), in0=modc[:, first:first + KT], scalar=1.0, in1=wcols,
                                            op0=ALU.add, op1=ALU.mult))

            lead("in2", range(2))
            scales(SCALE_M, colA(A_MPRE, KT), 16)
            for t in range(TT):
                dve.wait_ge(sem("first_tokens"), 1) if t == 0 else dve.wait_ge(w_used, down_end("down1"))
                v.tensor_tensor(x[:, t, :], ps[:, D * t:D * (t + 1)], x[:, t, :], ALU.add).then_inc(sem("x_new"), 1)
            norm_sums(2)
            norm(2, "in2", {2: 2, 4: 3}, sm(SCALE_M, KT), modc[:, 0:KT])
            first, units = 4 * PH["down1"].unit, (FT - 4) // DOWN_BODY
            dve.wait_ge(mod_red, PH["down1"].unit + units)
            v.tensor_tensor(modc[:, first:first + 4 * units], main(1)[:, 0:4 * units], colB(B_MOD + first, 4 * units),
                            ALU.add).then_inc(sem("modc_ready"), units)

            xg, ta, bb = head_tok(A1), head_tok(A2), head_tok(A4)
            q, k = head_tok(0), head_tok(1024)
            GS = HD ** -0.5
            bc = reg(A4, 1024).rearrange("p (c s) -> p c s", s=CHUNK)

            def log_decay():
                dve.wait_ge(sem("ln_ready"), 1)
                link(v.scalar_tensor_tensor(out=ta, in0=xg, scalar=0.0, in1=ta, op0=ALU.min, op1=ALU.subtract))
                link(v.tensor_scalar(ta, ta, 1.0 / GATE_TAU, None, ALU.mult))

            def decay_sums():
                for h in range(GLA_HEADS):
                    ins = v.tensor_tensor_scan(bb[:, h, :], con[:, C_RST:C_RST + S], ta[:, h, :], 0.0, ALU.mult, ALU.add)
                    if h < GLA_HEADS - 1:
                        link(ins)
                ins.then_inc(sem("b_ready"), 1)
                dve.wait_ge(sem("b_ready"), 1)
                v.tensor_tensor(reg(A3, 1024).rearrange("p (c s) -> p c s", s=CHUNK), bc,
                                bc[:, :, CHUNK - 1:CHUNK].to_broadcast([P, 16, CHUNK]), ALU.subtract).then_inc(sem("kd_diff"), 1)

            def from_start():
                dve.wait_ge(sem("eb_ready"), 1)
                dve.wait_ge(sem("q_ex_zero"), 1)
                for c in range(1, NCHUNK):
                    at = CHUNK * (c % 2)
                    ins = v.scalar_tensor_tensor(out=q_ex[:, :, c - 1, at:at + CHUNK], in0=q[:, :, CHUNK * c:CHUNK * (c + 1)], scalar=GS,
                                                 in1=head_tok(A1)[:, :, CHUNK * c:CHUNK * (c + 1)], op0=ALU.mult, op1=ALU.mult)
                ins.then_inc(sem("q_ex_ready"), 1)

            def to_end():
                dve.wait_ge(sem("kd_exp"), 1)
                v.tensor_tensor(reg(A3, 1024), reg(A3, 1024), reg(1024, 1024), ALU.mult).then_inc(sem("kd_ready"), 1)

            def first_states():
                dve.wait_ge(sem("e_last"), 1)
                dve.wait_ge(sem("u_done"), 1)
                link(v.tensor_copy(states[:, 0, :, :], side(0, 1024).rearrange("p (h e) -> p h e", h=GLA_HEADS)))
                dve.wait_ge(sem("u_done"), 2)
                for h in range(GLA_HEADS):
                    ins = v.scalar_tensor_tensor(out=states[:, 1, h, :], in0=states[:, 0, h, :], scalar=sm(E_LAST + NCHUNK * h + 1),
                                                 in1=side(2, 1024)[:, GLA_DV * h:GLA_DV * (h + 1)], op0=ALU.mult, op1=ALU.add)
                ins.then_inc(sem("u_used"), 1)

            def last_state():
                dve.wait_ge(sem("u_done"), 3)
                dve.wait_ge(sem("u_used"), 1)
                for h in range(GLA_HEADS):
                    ins = v.scalar_tensor_tensor(out=states[:, 2, h, :], in0=states[:, 1, h, :], scalar=sm(E_LAST + NCHUNK * h + 2),
                                                 in1=side(0, 1024)[:, GLA_DV * h:GLA_DV * (h + 1)], op0=ALU.mult, op1=ALU.add)
                ins.then_inc(sem("states_ready"), 1)

            def level_diff(n):
                s = LEVELS[n]
                b4 = reg(A4, 1024).rearrange("p (c s) -> p c s", s=2 * s)
                if n:
                    dve.wait_ge(sem("k_lvl"), n)
                    dve.wait_ge(sem("q_lvl"), n)
                else:
                    dve.wait_ge(sem("q_ex_ready"), 1)
                v.tensor_tensor(reg(A1, 1024).rearrange("p (c s) -> p c s", s=2 * s), b4,
                                b4[:, :, s - 1:s].to_broadcast([P, 512 // s, 2 * s]), ALU.subtract).then_inc(sem("lvl_diff"), 1)

            def second_half(a, half):
                return a.rearrange("p (c two s) -> p c two s", two=2, s=half)[:, :, 1, :]

            def level_q(n):
                if n >= 2:
                    dve.wait_ge(sem("lvl_mm"), n - 1)
                if n < len(LEVELS):
                    half = LEVELS[n]
                    qt = reg(q_lvl_at[n % 2], 512).rearrange("p (c s) -> p c s", s=half)
                    dve.wait_ge(sem("lvl_exp"), n + 1)
                    v.scalar_tensor_tensor(out=qt, in0=second_half(reg(0, 1024), half), scalar=GS, in1=second_half(reg(A1, 1024), half),
                                           op0=ALU.mult, op1=ALU.mult).then_inc(sem("q_lvl"), 1)
                else:
                    v.tensor_scalar(head_tok(q_lvl_at[n % 2]), q, GS, None, ALU.mult).then_inc(sem("q_lvl"), 1)

            def level_sum(n):
                dve.wait_ge(sem("lvl_mm"), n + 1)
                mask = con[:, C_LVL + P * n:C_LVL + P * (n + 1)]
                if n < len(LEVELS):
                    half = LEVELS[n]
                    blocks = P // (2 * half)

                    def shape(a):
                        return a.rearrange("p (n c s) -> p n c s", n=8, s=half)
                    mask = second_half(mask, half).unsqueeze(1).to_broadcast([P, 8, blocks, half])
                    got, tmp = shape(side(2 * (n % 2))), shape(reg(A6, 512))
                    acc = reg(A5, 1024).rearrange("p (n c two s) -> p n c two s", n=8, two=2, s=half)[:, :, :, 1, :]
                else:
                    mask = mask.unsqueeze(1).to_broadcast([P, 8, P])
                    got, tmp, acc = (a.rearrange("p (n i) -> p n i", n=8) for a in (side(2 * (n % 2), 1024), reg(A6, 1024), reg(A5, 1024)))
                dve.wait_ge(sem("lvl_sum"), n) if n else dve.wait_ge(sem("sc_zero"), 1)
                link(v.tensor_tensor(tmp, got, mask, ALU.mult))
                v.tensor_tensor(acc, acc, tmp, ALU.add).then_inc(sem("lvl_sum"), 1)

            def o_means():
                dve.wait_ge(sem("o_sq"), 1)
                link(v.tensor_reduce(sm(O_SS, 8), reg(A4, 2048).rearrange("p (n e) -> p n e", e=GLA_DV), AX_X, ALU.add))
                v.tensor_scalar(sm(O_SS, 8), sm(O_SS, 8), 1.0 / GLA_DV, EPS, ALU.mult, ALU.add).then_inc(sem("o_ms"), 1)

            def o_norm():
                dve.wait_ge(sem("o_sd"), 1)
                link(v.reciprocal(sm(O_SS, 8), sm(O_SD, 8)))
                o8 = reg(A2, 2048).rearrange("p (n e) -> p n e", e=GLA_DV)
                link(v.tensor_tensor(o8, o8, sm(O_SS, 8).unsqueeze(2).to_broadcast([P, 8, GLA_DV]), ALU.mult))

            def o_gate():
                dve.wait_ge(sem("r_silu"), 1)
                for b in range(2):
                    oo = reg(A2, 2048).rearrange("p (t n) -> p t n", t=TT)[:, :, 512 * b:512 * (b + 1)]
                    v.tensor_tensor(oo, oo, z[:, 4 + b, :].rearrange("p (t n) -> p t n", t=TT), ALU.mult).then_inc(sem("o_gated"), 1)

            def mix_taps(b, j, shift):
                if j == 1:
                    dve.wait_ge(sem("mix_tap"), 12 * b + 4)
                else:
                    dve.wait_ge(sem("mix_tap"), 12 * b + 8)
                for f in range(4 * b, 4 * b + 4):
                    v.scalar_tensor_tensor(out=cx[:, f, shift:], in0=cc[:, f, 0:S - shift], scalar=colA(A_CW + 8 * j + f),
                                           in1=cx[:, f, shift:], op0=ALU.mult, op1=ALU.add).then_inc(sem("mix_tap"), 1)

            def conv_out(b):
                dve.wait_ge(sem("mix_tap"), 12 * b + 12)
                dve.wait_ge(epi_done, blocks_before("in2") + 11 + b)
                v.tensor_tensor(cb[:, 4 * b:4 * b + 4, :], cb[:, 4 * b:4 * b + 4, :], cx[:, 4 * b:4 * b + 4, :],
                                ALU.mult).then_inc(sem("yT_conv_ready"), 1)

            def gate_diag(wcols, first):
                dve.wait_ge(sem("modc_ready"), first // 4 + 4)
                link(v.tensor_tensor(sm(GP, KT), modc[:, first:first + KT], wcols, ALU.mult))
                v.tensor_tensor(diag, ident.unsqueeze(1).to_broadcast([P, KT, P]), sm(GP, KT).unsqueeze(2).to_broadcast([P, KT, P]),
                                ALU.mult).then_inc(sem("diag_ready"), 1)

            def mixer2(at):
                if at == 16:
                    log_decay()
                if at == 17:
                    decay_sums()
                if at == 19:
                    from_start()
                if at == 20:
                    to_end()
                if at == 24:
                    first_states()
                if at == 26:
                    last_state()
                if at >= 24 and at % 2 == 0 and (at - 24) // 2 < len(LEVELS):
                    level_diff((at - 24) // 2)
                if at >= 25 and at % 2 == 1 and (at - 25) // 2 <= len(LEVELS):
                    level_q((at - 25) // 2)
                if at >= 28 and at % 2 == 0 and (at - 28) // 2 <= len(LEVELS):
                    level_sum((at - 28) // 2)
                if at in (40, 41):
                    mix_taps(0, 41 - at, at - 39)
                if at == 43:
                    o_means()
                if at in (44, 45):
                    mix_taps(1, 45 - at, at - 43)
                if at == 45:
                    o_norm()
                if at == 46:
                    o_gate()
                if at == 47:
                    conv_out(0)

            pairs("in2", epi_none, GATE_RANK, mixer2)
            lead("out2", range(3))
            split_mixed("out2", yT_gla, range(4, 8), 0)
            conv_out(1)
            lead("out2", range(3, 4))
            split_mixed("out2", yT_conv, range(0, 4), 4)

            def epi_gated(ph, blk, i0, i, r):
                j = 2 * i0 + blk
                dve.wait_ge(sem("post_sq"), 2 * j + 2)
                dve.wait_ge(sem("row_ready"), 1)
                v.tensor_tensor(y[:, :, BLOCK * j:BLOCK * (j + 1)], main(blk).rearrange("p (t n) -> p t n", t=TT),
                                g_row[:, BLOCK * j:BLOCK * (j + 1)].unsqueeze(1).to_broadcast([P, TT, BLOCK]),
                                ALU.mult).then_inc(epi_done, 1)

            def first_row(at):
                if at == 2:
                    gate_diag(colA(A_MPOST, KT), 32)

            pairs("out2", epi_gated, between=first_row)
            lead("up2", range(2))
            dve.wait_ge(sem("post_sq"), 8)
            link(v.tensor_reduce(sm(P_RSTD, 2), sm(P_SS, 8).rearrange("p (t j) -> p t j", t=TT), AX_X, ALU.add))
            v.tensor_scalar(sm(P_SS, 2), sm(P_RSTD, 2), 1.0 / D, EPS, ALU.mult, ALU.add).then_inc(sem("post_ms"), 1)
            last_epi("out2", epi_gated)
            dve.wait_ge(epi_done, blocks_before("up2"))
            dve.wait_ge(sem("post_sd"), 1)
            v.reciprocal(sm(P_RSTD, 2), sm(P_SD, 2)).then_inc(sem("post_rstd"), 1)
            dve.wait_ge(sem("post_rstd"), 1)
            for t, cols in ((0, slice(0, D)), (1, slice(0, D // 2))):
                v.scalar_tensor_tensor(out=x[:, t, cols], in0=y[:, t, cols], scalar=sm(P_RSTD + t), in1=x[:, t, cols],
                                       op0=ALU.mult, op1=ALU.add).then_inc(sem("x_new"), 1)
            norm_sums(3)
            last_unit("out2")
            scales(SCALE_F, colA(A_FPRE, KT), 64)
            norm(3, "up2", {2: 2, 4: 3}, sm(SCALE_F, KT), modc[:, 48:64])

            def last_row(at):
                if at == 36:
                    gate_diag(colB(B_FPOST, KT), 80)

            pairs("up2", epi_conv(2, 1), between=last_row)
            down("down2", 1, lambda: last_epi("up2", epi_conv(2, 1)))
            dve.wait_ge(sem("row_ready"), 2)
            for t in range(TT):
                dve.wait_ge(sem("first_tokens"), 2) if t == 0 else dve.wait_ge(w_used, down_end("down2"))
                for half in (1, 0):
                    if half == 0:
                        dve.wait_ge(sem("post_sq"), 8 + 2 * t + 1)
                    cols = slice(D // 2 * half, D // 2 * (half + 1))
                    at = D * t + D // 2 * half
                    v.tensor_tensor(y[:, t, cols], ps[:, at:at + D // 2], g_row[:, cols], ALU.mult).then_inc(sem("yg_ready"), 1)
                dve.wait_ge(sem("post_sq"), 8 + 2 * t + 2)
                link(v.tensor_tensor(sm(P_SS + 4 * t + 2), sm(P_SS + 4 * t), sm(P_SS + 4 * t + 1), ALU.add))
                v.tensor_scalar(sm(P_SS + 4 * t + 3), sm(P_SS + 4 * t + 2), 1.0 / D, EPS, ALU.mult, ALU.add).then_inc(sem("post_ms"), 1)
                dve.wait_ge(sem("post_sd"), 2 + t)
                link(v.reciprocal(sm(P_RSTD + 2 + t), sm(P_SD + 2 + t)))
                dve.wait_ge(sem("yg_ready"), 2 * t + 2)
                for half in range(2):
                    cols = slice(D // 2 * half, D // 2 * (half + 1))
                    v.scalar_tensor_tensor(out=x[:, t, cols], in0=y[:, t, cols], scalar=sm(P_RSTD + 2 + t), in1=x[:, t, cols],
                                           op0=ALU.mult, op1=ALU.add).then_inc(sem("x_new"), 1)

        @block.gpsimd
        def _(pool):
            gp = nc.gpsimd
            seq = [0]

            def link(ins):
                seq[0] += 1
                ins.then_inc(sem("pool_step"), 1)
                pool.wait_ge(sem("pool_step"), seq[0])

            for n in range(2):
                pool.wait_ge(sem("qk_rstd"), n + 1)
                zz = reg(2048 + 2048 * n, 2048).rearrange("p (n d) -> p n d", d=HD)
                gp.tensor_tensor(zz, zz, sm(QK_SS + 16 * n, 16).unsqueeze(2).to_broadcast([P, 16, HD]),
                                 ALU.mult).then_inc(sem("qk_normed"), 1)
            pool.wait_ge(sem("qkT_ready"), 4)
            for n, win_size in enumerate(WINDOWS):
                pool.wait_ge(epi_done, 7 + n // 2)
                u = yT_pool[:, 2 * n:2 * n + 2, :]
                cur, sh, b = u, 1, 0
                while sh < win_size:
                    nxt = win[b]
                    link(gp.tensor_tensor(nxt[:, :, sh:], cur[:, :, sh:], cur[:, :, 0:S - sh], ALU.add))
                    link(gp.tensor_copy(nxt[:, :, 0:sh], cur[:, :, 0:sh]))
                    cur, b, sh = nxt, 1 - b, 2 * sh
                mean = win[b]
                link(gp.tensor_scalar(mean[:, :, 16:], cur[:, :, 16:], 1.0 / win_size, None, ALU.mult))
                link(gp.tensor_tensor(mean[:, :, 0:16], cur[:, :, 0:16],
                                      con[:, C_INV + 16 * n:C_INV + 16 * n + 16].unsqueeze(1).to_broadcast([P, 2, 16]), ALU.mult))
                gp.tensor_tensor(dT[:, 2 * n:2 * n + 2, :], mean, u, ALU.subtract).then_inc(sem("d_ready"), 1)
                pool.wait_ge(sem("d_ready"), n + 1)

            def gated(name, q):
                b0 = PH[name].pairs[0].b0
                with pool.Fori(0, PAIRS_UP) as i:
                    pool.wait_ge(sem("silu_done"), q * PAIRS_UP + 1 + i)
                    pool.wait_ge(epi_done, b0 + 2 + 2 * i)
                    gp.tensor_tensor(g[:, bass.ds(4 * i, 4), :], c_gate, c_val, ALU.mult).then_inc(sem("g_done"), 1)

            gated("up1", 0)

            pool.wait_ge(epi_done, blocks_before("in2") + 1)
            gp.memset(q_ex, 0.0).then_inc(sem("q_ex_zero"), 1)
            gp.memset(reg(A5, 1024), 0.0).then_inc(sem("sc_zero"), 1)
            for n in range(len(LEVELS)):
                pool.wait_ge(sem("lvl_exp"), n + 1)
                if n:
                    pool.wait_ge(sem("lvl_mm"), n)
                else:
                    pool.wait_ge(sem("kd_turned"), 1)
                gp.tensor_tensor(reg(A3, 1024), reg(1024, 1024), reg(A1, 1024), ALU.mult).then_inc(sem("k_lvl"), 1)
            for b in range(2):
                pool.wait_ge(epi_done, blocks_before("in2") + 9 + b)
                gp.tensor_tensor(cc[:, 4 * b:4 * b + 4, :], cc[:, 4 * b:4 * b + 4, :], cx[:, 4 * b:4 * b + 4, :],
                                 ALU.mult).then_inc(sem("ccx_ready"), 1)
            pool.wait_ge(sem("y_scaled"), 1)
            half = slice(D // 2, D)
            gp.tensor_tensor(x[:, 1, half], y[:, 1, half], x[:, 1, half], ALU.add).then_inc(sem("x_new_pool"), 1)
            gated("up2", 1)

        @block.tensor
        def _(pe):
            mmul = nc.tensor.matmul

            def three(dst, lhs_hi, lhs_lo, rhs_hi, rhs_lo, start, stop):
                mmul(dst, lhs_hi, rhs_hi, start=start, stop=False, skip_group_check=True)
                mmul(dst, lhs_hi, rhs_lo, start=False, stop=False, skip_group_check=True)
                return mmul(dst, lhs_lo, rhs_hi, start=False, stop=stop, skip_group_check=True)

            def rest(name, cols):
                for half in range(2):
                    hh = 2 * PH[name].rest + half
                    pe.wait_ge(lo_ready, hh + 1)
                    for kk in range(KT // 2):
                        kt = KT // 2 * half + kk
                        wc = slice(kk * cols, (kk + 1) * cols)
                        mm = three(side(0)[0:cols, 0:S], w_hi[:, hh % HL_SLOTS, wc], w_lo[:, hh % HL_SLOTS, wc], a_hi[:, kt, :],
                                   a_lo[:, kt, :], kt == 0, kt == KT - 1)
                    mm.then_inc(w_used, 1)

            def half_T(dst, hh, kts, first, last):
                for kk, kt in enumerate(kts):
                    for t in range(TT):
                        tok = slice(t * P, (t + 1) * P)
                        wc = slice(kk * BLOCK, (kk + 1) * BLOCK)
                        mm = three(dst[:, t * BLOCK:(t + 1) * BLOCK], a_hi[:, kt, tok], a_lo[:, kt, tok],
                                   w_hi[:, hh % HL_SLOTS, wc], w_lo[:, hh % HL_SLOTS, wc],
                                   first and kk == 0, last and kk == len(kts) - 1)
                return mm

            def half_W(dst, hh, kts, first, last):
                for kk, kt in enumerate(kts):
                    for ft in range(4):
                        wc = slice(kk * BLOCK + ft * P, kk * BLOCK + (ft + 1) * P)
                        mm = three(dst[:, ft * S:(ft + 1) * S], w_hi[:, hh % HL_SLOTS, wc], w_lo[:, hh % HL_SLOTS, wc],
                                   a_hi[:, kt, :], a_lo[:, kt, :], first and kk == 0 and ft % 2 == 0, last and kk == len(kts) - 1)
                return mm

            def pairs(name, narrow=0, between=None):
                ph = PH[name]
                f = FILL[name]

                def body(i0, i, r, layout):
                    pair = ph.pairs[i0]
                    for blk in range(2):
                        b = pair.b0 + blk
                        if b >= 2:
                            pe.wait_ge(epi_done, b - 1 + 2 * r)
                        for c in range(BLOCK_CHUNKS):
                            for half in range(2):
                                hh = 2 * (pair.m0 + 4 * blk + c) + half
                                pe.wait_ge(lo_ready, hh + 1 + 16 * r)
                                if i0 == 0 and blk == 0:
                                    pe.wait_ge(act_ready, 8 * f + 2 * c + half + 1)
                                kts = [KC * K_ORDER[name][c] + 2 * half + kk for kk in range(2)]
                                (half_T if layout == "T" else half_W)(
                                    main(blk), hh, kts, c + half == 0, c == BLOCK_CHUNKS - 1 and half == 1).then_inc(w_used, 1)
                            if between:
                                between(8 * i0 + 4 * blk + c)
                    if pair.unit is not None:
                        pe.wait_ge(mod_step, UNIT_OPS * (pair.unit + 1) + UNIT_OPS * r)
                        for j in range(4):
                            mm = mmul(side(3)[:, 508 + j:509 + j], mod_acc[:, j * P:(j + 1) * P], ones[:, 0:1], start=True, stop=True)
                        mm.then_inc(mod_red, 1)
                    if narrow and i0 == 0:
                        rest(name, narrow)

                run_pairs(pe, name, body)

            def down(name, q, tail):
                ph = PH[name]

                def half_down(j, half, r, tiles=range(TT)):
                    hh = 2 * (ph.m0 + j) + half
                    pe.wait_ge(lo_ready, hh + 1 + 16 * r)
                    for t in tiles:
                        for n in range(2):
                            at = t * D + half * HALF + n * BLOCK
                            tok = slice(t * P, (t + 1) * P)
                            wc = slice(n * BLOCK, (n + 1) * BLOCK)
                            mm = three(ps[:, at:at + BLOCK], a_hi[:, j % 4, tok], a_lo[:, j % 4, tok], w_hi[:, hh % HL_SLOTS, wc],
                                       w_lo[:, hh % HL_SLOTS, wc], j == 0, False)
                    return mm

                def both(j, r):
                    pe.wait_ge(sem("g_split"), FT * q + j + 1 + DOWN_BODY * r)
                    for half in range(2):
                        half_down(j, half, r).then_inc(w_used, 1)

                b0 = BEFORE_DOWN[name].b0
                pe.wait_ge(epi_done, b0 + 1)
                pe.wait_ge(sem("g_split"), FT * q + 1)
                half_down(0, 0, 0).then_inc(w_used, 1)
                pe.wait_ge(sem("g_split"), FT * q + 2)
                half_down(1, 0, 0)
                pe.wait_ge(epi_done, b0 + 2)
                half_down(0, 1, 0).then_inc(w_used, 1)
                half_down(1, 1, 0).then_inc(w_used, 2)
                for j in range(2, 4):
                    both(j, 0)
                with pe.Fori(0, (FT - 4) // DOWN_BODY - 1) as r:
                    for j in range(4, 4 + DOWN_BODY):
                        both(j, r)
                for j in range(FT - DOWN_BODY, FT - tail):
                    both(j, 0)
                last = range(FT - tail, FT)
                for j in last:
                    pe.wait_ge(sem("g_split"), FT * q + j + 1)
                    for half in range(2):
                        mm = half_down(j, half, 0, (0,))
                mm.then_inc(sem("first_tokens"), 1)
                for j in last:
                    for half in range(2):
                        half_down(j, half, 0, (1,)).then_inc(w_used, 1)

            def norm(p, ks):
                for k in ks:
                    if k % 4 == 0:
                        pe.wait_ge(sem("hn_dve"), 2 * p + k // 4 + 1)
                        pe.wait_ge(sem("hn_act"), 2 * p + k // 4 + 1)
                    if k >= 5:
                        pe.wait_ge(sem("xt_ready"), KT * p + 2 * (k - 5) + 2)
                    for kk in range(2):
                        for t in range(TT):
                            at = S * kk + P * t
                            mm = nc.tensor.transpose(turn_bank(k)[:, at:at + P], hn[:, t, (2 * k + kk) * P:(2 * k + kk + 1) * P], ident)
                    mm.then_inc(sem("turned"), 1)

            rows = [A_ROWS, P] + [CONV_ROWS] * 7
            pe.wait_ge(sem("first_params"), 16 * N_FIRST)
            nc.tensor.transpose(main(0)[:, 0:KT], stage[0:KT, 0, :], ident[0:KT, 0:KT]).then_inc(sem("cols_turned"), 1)
            norm(0, range(0, 5))

            def turn_columns():
                pe.wait_ge(sem("second_params"), 16 * N_SECOND)
                pe.wait_ge(sem("xt_ready"), KT)
                for n in range(9):
                    at = SIDE + P * n
                    mm = nc.tensor.transpose(ps[:, at:at + rows[n]], stage[0:rows[n], n, :], ident[0:rows[n], 0:rows[n]])
                mm.then_inc(sem("cols_turned"), 1)

            def index_scores(n):
                t, b = divmod(n, 8)
                K = P * (t + 1)
                if n >= 3:
                    pe.wait_ge(sem("relu_ready"), n - 2)
                for j in range(2):
                    h = 4 * (b // 2) + b % 2 + 2 * j
                    half = slice(IDX_DIM * (h % 2), IDX_DIM * (h % 2 + 1))
                    mm = mmul(side(n % 3)[:, S * j:S * j + K], zw(0)[half, h // 2, t * P:(t + 1) * P], kidxT[half, 0:K],
                              start=True, stop=True, skip_group_check=True)
                mm.then_inc(sem("is_done"), 1)

            def qk_turn(n):
                b, t = divmod(n % 4, 2)
                pe.wait_ge(sem("qk_normed"), n // 4 + 1)
                pe.wait_ge(sem("relu_ready"), 16)
                if n >= 3:
                    pe.wait_ge(sem("qkT_ready"), n - 2)
                for h in range(4):
                    at = t * 512 + h * HD
                    mm = nc.tensor.transpose(side(n % 3)[:, h * P:(h + 1) * P], z[:, 2 + 2 * (n // 4) + b, at:at + HD], ident)
                mm.then_inc(sem("qk_turned"), 1)

            def scores(u):
                t, h0, nh, K = attention_unit(u)
                pe.wait_ge(sem("qkT_ready"), 8)
                if u >= 3:
                    pe.wait_ge(sem("pT_ready"), u - 2)
                for j in range(nh):
                    mm = mmul(side(u % 3)[:, K * j:K * (j + 1)], qT[:, h0 + j, t * P:(t + 1) * P], kT[:, h0 + j, 0:K],
                              start=True, stop=True, skip_group_check=True)
                mm.then_inc(sem("sc_done"), 1)

            def probs_turn(u):
                t, h0, nh, K = attention_unit(u)
                pe.wait_ge(sem("p_ready"), u + 1)
                for j in range(nh):
                    for st in range(t + 1):
                        o = K * j + P * st
                        mm = nc.tensor.transpose(side(u % 3)[:, o:o + P], sc_buf[:, u % 2, o:o + P], ident)
                mm.then_inc(sem("p_turned"), 1)

            def attend(n):
                t, hg, b, units = ATTEND[n]
                pe.wait_ge(sem("pT_ready"), units)
                pe.wait_ge(epi_done, 9 + hg)
                if n == 2:
                    pe.wait_ge(sem("yT_attn_ready"), 1)
                for j in range(4):
                    u, jj = (hg, j) if t == 0 else (2 + 2 * hg + j // 2, j % 2)
                    for st in range(t + 1):
                        at = st * 512 + j * HD
                        o = P * ((t + 1) * jj + st)
                        mm = mmul(side(b)[:, P * j:P * (j + 1)], z[:, 8 + hg, at:at + HD], pT[u][:, o:o + P],
                                  start=(st == 0), stop=(st == t), skip_group_check=True)
                mm.then_inc(sem("pv_done"), 1)

            def pool_mix(e):
                pe.wait_ge(sem("d_ready"), e + 1)
                pe.wait_ge(sem("pool_w_loaded"), 16)
                if e:
                    pe.wait_ge(sem("yT_pool_ready"), 2 * e)
                else:
                    pe.wait_ge(sem("modc_ready"), 2)
                for f in range(2):
                    for c in range(2):
                        mm = mmul(side(3)[:, S * f:S * (f + 1)], pool_w[:, e, c, P * f:P * (f + 1)], dT[:, 2 * e + c, :],
                                  start=(c == 0), stop=(c == 1), skip_group_check=True)
                mm.then_inc(sem("pool_mixed"), 1)

            def mixer1(at):
                if at == 0:
                    norm(0, range(5, 8))
                if at == 3:
                    turn_columns()
                if at == 7:
                    pe.wait_ge(sem("cols_ready"), 4)
                if at == 10:
                    pe.wait_ge(sem("widxT_ready"), 1)
                    for t in range(TT):
                        mm = nc.tensor.transpose(side(2)[:, t * IDX_HEADS:(t + 1) * IDX_HEADS], widxT[:, t * P:(t + 1) * P],
                                                 ident[0:IDX_HEADS, 0:IDX_HEADS])
                    mm.then_inc(sem("widx_turned"), 1)
                if at == 11:
                    pe.wait_ge(sem("kidxT_ready"), 2)
                if at == 12:
                    pe.wait_ge(sem("widx_ready"), 1)
                if 11 <= at < 19:
                    index_scores(2 * (at - 11))
                    index_scores(2 * (at - 11) + 1)
                for n in {21: (0, 1, 2), 23: (3,), 28: (4, 5, 6), 30: (7,)}.get(at, ()):
                    qk_turn(n)
                for u in {33: (0, 1), 36: (2,), 37: (3,), 39: (4,)}.get(at, ()):
                    probs_turn(u)
                for u in {31: (0, 1, 2), 34: (3, 4), 37: (5,)}.get(at, ()):
                    scores(u)
                if at == 38:
                    pool_mix(0)

            pairs("in1", IDX_REST, mixer1)
            attend(0)
            pool_mix(1)
            attend(1)
            pool_mix(2)
            probs_turn(5)
            attend(2)
            pool_mix(3)
            attend(3)

            pairs("out1")
            norm(1, range(0, 5))

            def later_tiles(at):
                if at == 0:
                    norm(1, range(5, 8))

            pairs("up1", between=later_tiles)
            down("down1", 0, 1)

            units = (FT - 4) // DOWN_BODY
            pe.wait_ge(sem("x_new"), TT)
            pe.wait_ge(mod_step, UNIT_OPS * (PH["down1"].unit + units))
            for j in range(4 * units):
                mm = mmul(main(1)[:, j:j + 1], region[:, DOWN_ACC + P * j:DOWN_ACC + P * (j + 1)],
                          ones[:, 0:1], start=True, stop=True, skip_group_check=True)
            mm.then_inc(mod_red, units)
            norm(2, range(0, 5))
            kdT = reg(A6, 1024).rearrange("p (h t d) -> p h t d", h=GLA_HEADS, t=TT)

            def vv(t, h):
                return z[:, 2 + h // 2, 512 * t + GLA_DV * (h % 2):512 * t + GLA_DV * (h % 2 + 1)]

            def state_add(c):
                rows_c = slice(CHUNK * (c % 2), CHUNK * (c % 2 + 1))
                for h in range(GLA_HEADS):
                    mm = mmul(side((0, 2, 0)[c], 1024)[:, GLA_DV * h:GLA_DV * (h + 1)], kdT[rows_c, h, c // 2, :], vv(c // 2, h)[rows_c, :],
                              start=True, stop=True, skip_group_check=True)
                mm.then_inc(sem("u_done"), 1)

            def level_scores(n):
                pe.wait_ge(sem("q_lvl"), n + 1)
                if n < len(LEVELS):
                    pe.wait_ge(sem("k_lvl"), n + 1)
                if n >= 2:
                    pe.wait_ge(sem("lvl_sum"), n - 1)
                else:
                    pe.wait_ge(sem("states_ready"), 1)
                kk = head_tok(A3) if n < len(LEVELS) else head_tok(1024)
                for h in range(GLA_HEADS):
                    for t in range(TT):
                        tok = slice(t * P, (t + 1) * P)
                        width = P // 2 if n < len(LEVELS) else P
                        at = width * (TT * h + t)
                        mm = mmul(side(2 * (n % 2), 1024)[:, at:at + width], kk[:, h, tok], reg(q_lvl_at[n % 2] + at, width), start=True,
                                  stop=True, skip_group_check=True)
                mm.then_inc(sem("lvl_mm"), 1)

            def mixer2(at):
                if at == 0:
                    norm(2, range(5, 8))
                if at == 3:
                    pe.wait_ge(sem("modc_ready"), PH["in2"].pairs[0].unit)
                if at == 11:
                    pe.wait_ge(sem("alrT_ready"), 1)
                    pe.wait_ge(sem("gate_loaded"), 16)
                    for h in range(GLA_HEADS):
                        mm = mmul(ps[:, SIDE + S * h:SIDE + S * (h + 1)], gate_w2[:, h * HD:(h + 1) * HD], a_lrT, start=True, stop=True,
                                  skip_group_check=True)
                    mm.then_inc(sem("gate_mm"), 1)
                if at == 19:
                    pe.wait_ge(sem("kd_ready"), 1)
                    for h in range(GLA_HEADS):
                        for t in range(TT):
                            o = SIDE + P * (TT * h + t)
                            mm = nc.tensor.transpose(ps[:, o:o + P], head_tok(A3)[:, h, t * P:(t + 1) * P], ident)
                    mm.then_inc(sem("kd_turned"), 1)
                if at == 21:
                    pe.wait_ge(sem("kdT_ready"), 1)
                    pe.wait_ge(sem("modc_ready"), PH["in2"].pairs[0].unit + 1)
                    state_add(0)
                    state_add(1)
                if at == 23:
                    pe.wait_ge(sem("u_used"), 1)
                    state_add(2)
                if at >= 25 and at % 2 == 1 and (at - 25) // 2 <= len(LEVELS):
                    level_scores((at - 25) // 2)
                if at == 39:
                    pe.wait_ge(sem("lvl_sum"), len(LEVELS) + 1)
                    sc = reg(A5, 1024).rearrange("p (h t i) -> p h t i", h=GLA_HEADS, t=TT)
                    for t in range(TT):
                        for h in range(GLA_HEADS):
                            dst = side(2 * t, 1024)[:, GLA_DV * h:GLA_DV * (h + 1)]
                            mmul(dst, sc[:, h, t, :], vv(t, h), start=True, stop=False, skip_group_check=True)
                            chunks = [c for c in (2 * t, 2 * t + 1) if c > 0]
                            for c in chunks:
                                mm = mmul(dst, q_ex[:, h, c - 1, :], states[:, c - 1, h, :], start=False, stop=(c == chunks[-1]),
                                          skip_group_check=True)
                    mm.then_inc(sem("o_done"), 1)
                if at == 45:
                    pe.wait_ge(sem("o_gated"), 2)
                    for f in range(8):
                        for t in range(TT):
                            mm = nc.tensor.transpose(ps[:, SIDE + S * f + P * t:SIDE + S * f + P * (t + 1)],
                                                     reg(A2, 2048).rearrange("p (t n) -> p t n", t=TT)[:, t, f * P:(f + 1) * P], ident)
                    mm.then_inc(sem("o_turned"), 1)

            def gate_row(q):
                pe.wait_ge(sem("diag_ready"), q + 1)
                for n in range(4):
                    mm = mmul(side(n), ones, diag[:, 4 * n:4 * n + 4, :].rearrange("p k f -> p (k f)"), start=True, stop=True)
                mm.then_inc(sem("row_mm"), 1)

            pairs("in2", GATE_RANK, mixer2)

            def first_row(at):
                if at == 3:
                    pe.wait_ge(sem("yT_gla_ready"), 8)
                    gate_row(0)
                if at == 7:
                    pe.wait_ge(sem("row_ready"), 1)

            pairs("out2", between=first_row)
            norm(3, range(0, 5))

            def last_row(at):
                if at == 0:
                    norm(3, range(5, 8))
                if at == 37:
                    pe.wait_ge(sem("modc_ready"), 24)
                    gate_row(1)

            pairs("up2", between=last_row)
            pe.wait_ge(sem("row_ready"), 2)
            down("down2", 1, 2)


VECTORS = ["attn_norm_g", "w_in", "pool_w", "pool_scale", "q_norm_g", "k_norm_g", "w_out", "ffn_norm_g", "w_up", "conv_w", "conv_b",
           "w_down", "c_2", "w_mod_2", "b_mod_2", "mix_pre_w_2", "mix_post_w_2", "w_in_2", "conv_w_2", "gate_w2_2", "gate_b_2",
           "gla_norm_w_2", "w_out_2", "ffn_pre_w_2", "ffn_post_w_2", "w_up_2", "ffn_conv_w_2", "w_down_2"]


def kernel(**inputs):
    import concourse.bacc as bacc
    from concourse.bass_utils import run_bass_kernel_spmd

    nc = bacc.Bacc("TRN2", target_bir_lowering=False, num_devices=1, dynamic_dma_scratch_size=1024)
    arrays = {}

    def dram(name, a):
        arrays[name] = a
        return nc.dram_tensor(name, a.shape, F32, kind="ExternalInput").ap()

    x = np.ascontiguousarray(inputs["x"])
    x_in = dram("in_x", x.reshape(S, D))
    w = {}
    for name in VECTORS:
        a = np.ascontiguousarray(inputs[name])
        if name.endswith("_2") and a.shape[0] == 1:
            a = a.reshape(a.shape[1:])
        w[name] = dram("in_" + name, a)
    consts = dram("in_constants", constants())
    out = nc.dram_tensor("out_x", (S, D), F32, kind="ExternalOutput").ap()
    two_blocks(nc, consts, x_in, out, w)
    r = run_bass_kernel_spmd(nc, [arrays], core_ids=[0])
    return r.results[0]["out_x"].reshape(x.shape)
```
